# Optimizing a Trainium2 kernel written in Bass

```python
import math
import jax, jax.numpy as jnp
from jax import lax
import numpy as np

D_MODEL = 1024
BATCH = 1
SEQ = 512
DEPTH = 1

PLE_DIM = 256
EPS = 1e-6
GLA_HEADS = 4
GLA_DK = D_MODEL // 2 // GLA_HEADS
GLA_DV = D_MODEL // GLA_HEADS
GLA_RANK = 16
GLA_TAU = 16.0
GLA_CHUNK = 64
GLA_QK_W = GLA_HEADS * GLA_DK
GLA_V_W = GLA_HEADS * GLA_DV
ATT_GROUPS = ((128, 1), (512, 4), (2048, 16))
ATT_HEADS_PER_GROUP = 4
ATT_HEAD_DIM = 128
N_ATT_GROUPS = len(ATT_GROUPS)
N_ATT_HEADS = N_ATT_GROUPS * ATT_HEADS_PER_GROUP
ATT_W = ATT_HEADS_PER_GROUP * ATT_HEAD_DIM
ATT_BLOCK = 128
REL_BUCKETS = 32
REL_MAX_DIST = 2048
D_FF = 4 * D_MODEL
NEG_INF = -1e30

SPLIT_SIZES = (GLA_QK_W, GLA_QK_W, GLA_V_W, GLA_V_W, GLA_RANK,
               N_ATT_GROUPS * 3 * ATT_W, 2 * D_MODEL)
IN_COLS = sum(SPLIT_SIZES)


def rmsnorm(x, g):
    xf = x.astype(jnp.float32)
    y = xf * lax.rsqrt(jnp.mean(xf * xf, axis=-1, keepdims=True) + EPS)
    return (y * g.astype(jnp.float32)).astype(x.dtype)

def _split_cols(h, sizes):
    offsets = np.cumsum(np.array(sizes))[:-1].tolist()
    return jnp.split(h, offsets, axis=-1)

def _t5_causal_bucket(n):
    max_exact = REL_BUCKETS // 2
    nf = np.maximum(n, 1).astype(np.float32)
    large = max_exact + (np.log(nf / max_exact) / np.log(REL_MAX_DIST / max_exact)
                         * (REL_BUCKETS - max_exact)).astype(np.int32)
    large = np.minimum(large, REL_BUCKETS - 1)
    return np.where(n < max_exact, n, large).astype(np.int32)

def _group_bias(rel_bias, g, dil):
    qi = np.arange(ATT_BLOCK)[:, None]
    kj = np.arange(2 * ATT_BLOCK)[None, :]
    dist = np.maximum(qi + ATT_BLOCK - kj, 0) * dil
    bucket = _t5_causal_bucket(dist)
    tab = rel_bias[:, g * ATT_HEADS_PER_GROUP:(g + 1) * ATT_HEADS_PER_GROUP]
    return jnp.transpose(tab[bucket], (2, 0, 1)).astype(jnp.float32)

def gla_mixer(q, k, v, log_a):
    B, S, H, dk = q.shape
    dv = v.shape[-1]
    C = GLA_CHUNK
    N = S // C

    def chunk(t):
        return t.astype(jnp.float32).reshape(B, N, C, H, t.shape[-1]).transpose(0, 3, 1, 2, 4)

    q, k, v, g = chunk(q), chunk(k), chunk(v), chunk(log_a)
    b = jnp.cumsum(g, axis=3)
    b_last = b[:, :, :, -1:, :]
    q_dec = q * (dk ** -0.5) * jnp.exp(b)
    k_in = k * jnp.exp(-b)
    k_out = k * jnp.exp(b_last - b)
    causal = np.tril(np.ones((C, C), dtype=bool))
    attn = jnp.where(causal, jnp.einsum('bhncd,bhnsd->bhncs', q_dec, k_in), 0.0)
    o_intra = jnp.einsum('bhncs,bhnsv->bhncv', attn, v)
    upd = jnp.einsum('bhncd,bhncv->nbhdv', k_out, v)
    decay = jnp.exp(b_last[:, :, :, 0, :]).transpose(2, 0, 1, 3)

    def step(state, inp):
        dec, u = inp
        return dec[..., None] * state + u, state

    _, states = lax.scan(step, jnp.zeros((B, H, dk, dv), jnp.float32), (decay, upd))
    o_inter = jnp.einsum('bhncd,nbhdv->bhncv', q_dec, states)
    return (o_intra + o_inter).transpose(0, 2, 3, 1, 4).reshape(B, S, H, dv)

def dilated_attention(q, k, v, bias, dil, win_steps):
    B, S, H, hd = q.shape
    BLK = ATT_BLOCK
    L = S // dil
    nb = -(-L // BLK)
    Lp = nb * BLK
    Z = B * dil

    def sub(t):
        return t.reshape(B, L, dil, H, hd).transpose(0, 2, 3, 1, 4).reshape(Z, H, L, hd)

    qs = jnp.pad(sub(q), ((0, 0), (0, 0), (0, Lp - L), (0, 0))).reshape(Z, H, nb, BLK, hd)

    def kv_blocks(t):
        t = jnp.pad(sub(t), ((0, 0), (0, 0), (BLK, Lp - L), (0, 0))).reshape(Z, H, nb + 1, BLK, hd)
        return jnp.concatenate([t[:, :, :-1], t[:, :, 1:]], axis=3)

    kb, vb = kv_blocks(k), kv_blocks(v)
    qi = np.arange(BLK)[:, None]
    kj = np.arange(2 * BLK)[None, :]
    delta = qi + BLK - kj
    band = (delta >= 0) & (delta <= win_steps)
    valid = band[None] & ((np.arange(nb)[:, None, None] > 0) | (kj >= BLK)[None])
    logits = jnp.einsum('zhnqd,zhnkd->zhnqk', qs, kb).astype(jnp.float32) * (hd ** -0.5)
    logits = jnp.where(valid, logits + bias[:, None], NEG_INF)
    m = jnp.max(logits, axis=-1, keepdims=True)
    pexp = jnp.exp(logits - m)
    s = jnp.sum(pexp, axis=-1, keepdims=True)
    o = jnp.einsum('zhnqk,zhnkd->zhnqd', pexp, vb.astype(jnp.float32)) / s
    lse = (m + jnp.log(s))[..., 0]
    o = o.reshape(B, dil, H, Lp, hd)[:, :, :, :L].transpose(0, 3, 1, 2, 4).reshape(B, S, H, hd)
    lse = lse.reshape(B, dil, H, Lp)[..., :L].transpose(0, 3, 1, 2).reshape(B, S, H)
    return o, lse

def first_inputs(seed: int = 0) -> dict:
    key = jax.random.key(seed)
    ks = jax.random.split(key, 20)

    def nrm(k, shape, scale):
        return jax.random.normal(k, shape, jnp.float32) * scale

    return {
        "x": nrm(ks[0], (BATCH, SEQ, D_MODEL), 1.0),
        "p": nrm(ks[1], (DEPTH, BATCH, SEQ, PLE_DIM), 1.0),
        "ln1": 1.0 + nrm(ks[2], (DEPTH, D_MODEL), 0.02),
        "w_in": nrm(ks[3], (DEPTH, D_MODEL, IN_COLS), D_MODEL ** -0.5),
        "w_a2": nrm(ks[4], (DEPTH, GLA_RANK, GLA_QK_W), GLA_RANK ** -0.5),
        "b_a": nrm(ks[5], (DEPTH, GLA_QK_W), 0.1),
        "gla_gn": 1.0 + nrm(ks[6], (DEPTH, GLA_V_W), 0.02),
        "w_o_gla": nrm(ks[7], (DEPTH, GLA_V_W, D_MODEL), GLA_V_W ** -0.5),
        "w_o_attn": nrm(ks[8], (DEPTH, ATT_W, D_MODEL), ATT_W ** -0.5),
        "w_out": nrm(ks[9], (DEPTH, D_MODEL, D_MODEL), D_MODEL ** -0.5),
        "ln2": 1.0 + nrm(ks[10], (DEPTH, D_MODEL), 0.02),
        "w_mlp1": nrm(ks[11], (DEPTH, D_MODEL, D_FF), D_MODEL ** -0.5),
        "w_mlp2": nrm(ks[12], (DEPTH, D_FF, D_MODEL), D_FF ** -0.5),
        "ln3": 1.0 + nrm(ks[13], (DEPTH, D_MODEL), 0.02),
        "w_pp": nrm(ks[14], (DEPTH, PLE_DIM, D_MODEL), PLE_DIM ** -0.5),
        "w_pg": nrm(ks[15], (DEPTH, D_MODEL, D_MODEL), D_MODEL ** -0.5),
        "rel_bias": nrm(ks[16], (REL_BUCKETS, N_ATT_HEADS), 0.5),
        "ln_f": 1.0 + nrm(ks[17], (D_MODEL,), 0.02),
    }

def first_block(x, p, ln1, w_in, w_a2, b_a, gla_gn, w_o_gla, w_o_attn, w_out,
              ln2, w_mlp1, w_mlp2, ln3, w_pp, w_pg, rel_bias, ln_f):
    B, S, _ = x.shape
    for i in range(DEPTH):
        h = rmsnorm(x, ln1[i])
        hq, hk, hv, hr, ha, hatt, hgate = _split_cols(h @ w_in[i], SPLIT_SIZES)

        log_a = jax.nn.log_sigmoid((ha @ w_a2[i] + b_a[i]).astype(jnp.float32)) / GLA_TAU
        o = gla_mixer(hq.reshape(B, S, GLA_HEADS, GLA_DK),
                      hk.reshape(B, S, GLA_HEADS, GLA_DK),
                      hv.reshape(B, S, GLA_HEADS, GLA_DV),
                      log_a.reshape(B, S, GLA_HEADS, GLA_DK))
        o = o * lax.rsqrt(jnp.mean(o * o, axis=-1, keepdims=True) + EPS)
        o = o.reshape(B, S, GLA_V_W) * gla_gn[i].astype(jnp.float32) * jax.nn.silu(hr.astype(jnp.float32))
        y_gla = o.astype(x.dtype) @ w_o_gla[i]

        hatt = hatt.reshape(B, S, N_ATT_GROUPS, 3, ATT_HEADS_PER_GROUP, ATT_HEAD_DIM)
        outs, lses = [], []
        for g, (win, dil) in enumerate(ATT_GROUPS):
            o_g, lse_g = dilated_attention(hatt[:, :, g, 0], hatt[:, :, g, 1], hatt[:, :, g, 2],
                                           _group_bias(rel_bias, g, dil), dil, win // dil)
            outs.append(o_g)
            lses.append(lse_g)
        wts = jax.nn.softmax(jnp.stack(lses, axis=0), axis=0)
        o_att = jnp.sum(wts[..., None] * jnp.stack(outs, axis=0), axis=0).reshape(B, S, ATT_W)
        y_att = o_att.astype(x.dtype) @ w_o_attn[i]

        g_gla, g_att = jnp.split(hgate, 2, axis=-1)
        mix = (jax.nn.sigmoid(g_gla) * y_gla + jax.nn.sigmoid(g_att) * y_att) @ w_out[i]
        x = x + mix

        h2 = rmsnorm(x, ln2[i])
        x = x + jnp.square(jax.nn.relu(h2 @ w_mlp1[i])) @ w_mlp2[i]

        h3 = rmsnorm(x, ln3[i])
        x = x + jax.nn.sigmoid(h3 @ w_pg[i]) * (p[i] @ w_pp[i])
    return rmsnorm(x, ln_f)


DEPTH_2 = 2

CHUNK = 64

A_HEADS = 4
A_WIDTH = D_MODEL
A_HEAD_DIM = A_WIDTH // A_HEADS
CONV_WIDTH = 4

B_HEADS = 8
B_WIDTH = D_MODEL
B_HEAD_DIM = B_WIDTH // B_HEADS
SB_BLOCK = 128

POOL_WINDOWS = (2, 4, 8, 16)
C_GROUPS = len(POOL_WINDOWS)
C_WIDTH = 2 * D_MODEL
C_GROUP_DIM = C_WIDTH // C_GROUPS

N_EVEN = (DEPTH_2 + 1) // 2
N_ODD = DEPTH_2 // 2
EVEN_SPLITS = [A_WIDTH] * 5 + [A_HEADS] * 2 + [B_WIDTH] * 4
EVEN_IN = sum(EVEN_SPLITS)
EVEN_OUT = A_WIDTH + B_WIDTH
ODD_IN = 2 * C_WIDTH


def rmsnorm_2(x, g):
    xf = x.astype(jnp.float32)
    y = xf * lax.rsqrt(jnp.mean(xf * xf, axis=-1, keepdims=True) + EPS)
    return y * g.astype(jnp.float32)

def causal_dwconv(x, w):
    K = w.shape[0]
    S = x.shape[1]
    xp = jnp.pad(x, ((0, 0), (K - 1, 0), (0, 0)))
    return sum(xp[:, k:k + S] * w[k].astype(jnp.float32) for k in range(K))

def split_cols(u, sizes):
    idx = list(np.cumsum(sizes)[:-1])
    return jnp.split(u, idx, axis=-1)

def mlstm(q, k, v, ig, lf):
    Bn, S, H, dh = q.shape
    nc = S // CHUNK
    k = k * (dh ** -0.5)

    def chunks4(t):
        return t.reshape(Bn, nc, CHUNK, H, dh).transpose(1, 0, 3, 2, 4)

    def chunks3(t):
        return t.reshape(Bn, nc, CHUNK, H).transpose(1, 0, 3, 2)

    xs = (chunks4(q), chunks4(k), chunks4(v), chunks3(ig), chunks3(lf))
    tri = jnp.tril(jnp.ones((CHUNK, CHUNK), dtype=bool))

    def step(carry, inp):
        C, n, m = carry
        qc, kc, vc, ic, fc = inp
        b = jnp.cumsum(fc, axis=-1)
        Dm = jnp.where(tri, b[..., :, None] - b[..., None, :] + ic[..., None, :], -1e30)
        m_inter = b + m[..., None]
        m_t = jnp.maximum(m_inter, jnp.max(Dm, axis=-1))
        W = jnp.exp(Dm - m_t[..., None])
        Sc = jnp.einsum('bhtd,bhsd->bhts', qc, kc) * W
        s_inter = jnp.exp(m_inter - m_t)
        num = (jnp.einsum('bhts,bhsd->bhtd', Sc, vc)
               + s_inter[..., None] * jnp.einsum('bhvk,bhtk->bhtv', C, qc))
        den = jnp.sum(Sc, axis=-1) + s_inter * jnp.einsum('bhk,bhtk->bht', n, qc)
        h = num / jnp.maximum(jnp.abs(den), jnp.exp(-m_t))[..., None]
        g = b[..., -1]
        a = g[..., None] - b + ic
        m_new = jnp.maximum(g + m, jnp.max(a, axis=-1))
        decay = jnp.exp(g + m - m_new)
        wa = jnp.exp(a - m_new[..., None])
        C_new = decay[..., None, None] * C + jnp.einsum('bhs,bhsv,bhsk->bhvk', wa, vc, kc)
        n_new = decay[..., None] * n + jnp.einsum('bhs,bhsk->bhk', wa, kc)
        return (C_new, n_new, m_new), h

    init = (jnp.zeros((Bn, H, dh, dh), jnp.float32),
            jnp.zeros((Bn, H, dh), jnp.float32),
            jnp.zeros((Bn, H), jnp.float32))
    _, hs = lax.scan(step, init, xs)
    return hs.transpose(1, 0, 3, 2, 4).reshape(Bn, S, H * dh)

def stick_breaking(q, k, v):
    S, dh = q.shape[2], q.shape[3]
    scale = dh ** -0.5
    outs = []
    for blk in range(S // SB_BLOCK):
        q0 = blk * SB_BLOCK
        q1 = q0 + SB_BLOCK
        z = jnp.einsum('bhqd,bhkd->bhqk', q[:, :, q0:q1], k[:, :, :q1]) * scale
        mask = jnp.arange(q1)[None, :] < (q0 + jnp.arange(SB_BLOCK))[:, None]
        log_1mb = jnp.where(mask, jax.nn.log_sigmoid(-z), 0.0)
        after = lax.cumsum(log_1mb, axis=3, reverse=True) - log_1mb
        A = jnp.where(mask, jnp.exp(jax.nn.log_sigmoid(z) + after), 0.0)
        outs.append(jnp.einsum('bhqk,bhkd->bhqd', A, v[:, :, :q1]))
    return jnp.concatenate(outs, axis=2)

def multiscale_pool(p):
    S = p.shape[1]
    cs = jnp.cumsum(p, axis=1)
    cs0 = jnp.pad(cs, ((0, 0), (1, 0), (0, 0), (0, 0)))
    t = jnp.arange(S)
    outs = []
    for g, w in enumerate(POOL_WINDOWS):
        upper = cs0[:, 1:, g]
        lower = jnp.pad(cs0[:, :S + 1 - w, g], ((0, 0), (w - 1, 0), (0, 0)))
        cnt = jnp.minimum(t + 1, w).astype(jnp.float32)
        outs.append((upper - lower) / cnt[None, :, None] - p[:, :, g])
    return jnp.stack(outs, axis=2)

def head_norm(h, g, n_heads):
    Bn, S, W = h.shape
    hh = h.reshape(Bn, S, n_heads, W // n_heads)
    hh = hh * lax.rsqrt(jnp.mean(hh * hh, axis=-1, keepdims=True) + EPS)
    return hh.reshape(Bn, S, W) * g.astype(jnp.float32)

def even_layer(x, pre_g, post_g, w_in, conv_w, b_i, b_f, hn_g, w_out):
    Bn, S, _ = x.shape
    h = rmsnorm_2(x, pre_g)
    u = h @ w_in.astype(jnp.float32)
    qa, ka, va, oa, za, ia, fa, qb, kb, vb, zb = split_cols(u, EVEN_SPLITS)
    qk = jax.nn.silu(causal_dwconv(jnp.concatenate([qa, ka], axis=-1), conv_w))
    qa, ka = qk[..., :A_WIDTH], qk[..., A_WIDTH:]
    ig = ia + b_i.astype(jnp.float32)
    lf = jax.nn.log_sigmoid(fa + b_f.astype(jnp.float32))
    hs = (Bn, S, A_HEADS, A_HEAD_DIM)
    ha = mlstm(qa.reshape(hs), ka.reshape(hs), va.reshape(hs), ig, lf)
    ha = jax.nn.sigmoid(oa) * ha
    ya = head_norm(ha, hn_g, A_HEADS) * jax.nn.silu(za)
    def heads(t):
        return t.reshape(Bn, S, B_HEADS, B_HEAD_DIM).transpose(0, 2, 1, 3)
    hb = stick_breaking(heads(qb), heads(kb), heads(vb))
    hb = hb.transpose(0, 2, 1, 3).reshape(Bn, S, B_WIDTH)
    yb = hb * jax.nn.silu(zb)
    y = jnp.concatenate([ya, yb], axis=-1) @ w_out.astype(jnp.float32)
    return x + rmsnorm_2(y, post_g).astype(x.dtype)

def odd_layer(x, pre_g, post_g, w_in, pool_w, pool_scale, w_out):
    Bn, S, _ = x.shape
    h = rmsnorm_2(x, pre_g)
    u = h @ w_in.astype(jnp.float32)
    p, z = u[..., :C_WIDTH], u[..., C_WIDTH:]
    pooled = multiscale_pool(p.reshape(Bn, S, C_GROUPS, C_GROUP_DIM))
    mixed = jnp.einsum('bsgc,gce->bsge', pooled, pool_w.astype(jnp.float32))
    mixed = mixed.reshape(Bn, S, C_WIDTH) * pool_scale.astype(jnp.float32)
    y = (mixed * jax.nn.silu(z)) @ w_out.astype(jnp.float32)
    return x + rmsnorm_2(y, post_g).astype(x.dtype)

def second_inputs(seed: int = 0) -> dict:
    key = jax.random.key(seed)
    ks = jax.random.split(key, 14)
    f32 = jnp.float32
    x = jax.random.normal(ks[0], (BATCH, SEQ, D_MODEL), f32)
    pre_norm_g = 1.0 + 0.02 * jax.random.normal(ks[1], (DEPTH_2, D_MODEL), f32)
    post_norm_g = 1.0 + 0.02 * jax.random.normal(ks[2], (DEPTH_2, D_MODEL), f32)
    w_in_ab = jax.random.normal(ks[3], (N_EVEN, D_MODEL, EVEN_IN), f32) * D_MODEL ** -0.5
    conv_qk = jax.random.normal(ks[4], (N_EVEN, CONV_WIDTH, 2 * A_WIDTH), f32) * CONV_WIDTH ** -0.5
    bias_i = 0.1 * jax.random.normal(ks[5], (N_EVEN, A_HEADS), f32)
    bias_f = 3.0 + 3.0 * jax.random.uniform(ks[6], (N_EVEN, A_HEADS), f32)
    head_norm_g = 1.0 + 0.02 * jax.random.normal(ks[7], (N_EVEN, A_WIDTH), f32)
    w_out_ab = jax.random.normal(ks[8], (N_EVEN, EVEN_OUT, D_MODEL), f32) * EVEN_OUT ** -0.5
    w_in_c = jax.random.normal(ks[9], (N_ODD, D_MODEL, ODD_IN), f32) * D_MODEL ** -0.5
    pool_w = jax.random.normal(ks[10], (N_ODD, C_GROUPS, C_GROUP_DIM, C_GROUP_DIM), f32) * C_GROUP_DIM ** -0.5
    pool_scale = 1.0 + 0.1 * jax.random.normal(ks[11], (N_ODD, C_WIDTH), f32)
    w_out_c = jax.random.normal(ks[12], (N_ODD, C_WIDTH, D_MODEL), f32) * C_WIDTH ** -0.5
    return {"x": x, "pre_norm_g": pre_norm_g, "post_norm_g": post_norm_g,
            "w_in_ab": w_in_ab, "conv_qk": conv_qk, "bias_i": bias_i, "bias_f": bias_f,
            "head_norm_g": head_norm_g, "w_out_ab": w_out_ab,
            "w_in_c": w_in_c, "pool_w": pool_w, "pool_scale": pool_scale, "w_out_c": w_out_c}

def second_block(x, pre_norm_g, post_norm_g, w_in_ab, conv_qk, bias_i, bias_f, head_norm_g,
              w_out_ab, w_in_c, pool_w, pool_scale, w_out_c):
    for layer in range(DEPTH_2):
        if layer % 2 == 0:
            e = layer // 2
            x = even_layer(x, pre_norm_g[layer], post_norm_g[layer], w_in_ab[e], conv_qk[e],
                           bias_i[e], bias_f[e], head_norm_g[e], w_out_ab[e])
        else:
            o = layer // 2
            x = odd_layer(x, pre_norm_g[layer], post_norm_g[layer], w_in_c[o], pool_w[o],
                          pool_scale[o], w_out_c[o])
    return x


def setup_inputs(seed=0):
    out = dict(first_inputs(seed))
    for name, value in second_inputs(seed + 1).items():
        if name != "x":
            out[name + "_2"] = value
    return out


def reference(
    x, p, ln1, w_in, w_a2, b_a, gla_gn, w_o_gla, w_o_attn, w_out, ln2, w_mlp1, w_mlp2, ln3,
    w_pp, w_pg, rel_bias, ln_f, pre_norm_g_2, post_norm_g_2, w_in_ab_2, conv_qk_2, bias_i_2,
    bias_f_2, head_norm_g_2, w_out_ab_2, w_in_c_2, pool_w_2, pool_scale_2, w_out_c_2,
):
    x = first_block(
        x, p, ln1, w_in, w_a2, b_a, gla_gn, w_o_gla, w_o_attn, w_out, ln2, w_mlp1, w_mlp2, ln3,
        w_pp, w_pg, rel_bias, ln_f,
    )
    return second_block(
        x, pre_norm_g_2, post_norm_g_2, w_in_ab_2, conv_qk_2, bias_i_2, bias_f_2, head_norm_g_2,
        w_out_ab_2, w_in_c_2, pool_w_2, pool_scale_2, w_out_c_2,
    )


_drawn_inputs = setup_inputs


def setup_inputs(seed=0):
    import zlib

    import numpy as np

    out = dict(_drawn_inputs(seed))
    spreads = {}
    factors = {'ln1': 2.82,
     'b_a': 2.754,
     'gla_gn': 5.937,
     'ln3': 200.0,
     'post_norm_g_2': 2.889,
     'bias_i_2': 64.0,
     'head_norm_g_2': 4.201,
     'ln2': 7.067,
     'p': 3.075,
     'w_pp': 3.098,
     'w_pg': 4.45}
    for name, (base, spread) in spreads.items():
        noise = np.random.default_rng([zlib.crc32(name.encode()), seed]).standard_normal(out[name].shape)
        drawn = base * np.exp(spread * noise) if base else spread * noise
        out[name] = __import__('jax').numpy.asarray(drawn.astype(out[name].dtype))
    for name, factor in factors.items():
        out[name] = (out[name] * factor).astype(out[name].dtype)
    return out
```

```python
from contextlib import ExitStack

import numpy as np

import concourse.bass as bass
from concourse import mybir

F32 = mybir.dt.float32
F32R = mybir.dt.float32r
U32 = mybir.dt.uint32
ACT = mybir.ActivationFunctionType
ALU = mybir.AluOpType
AX = mybir.AxisListType.X

P = 128
SEQ = 512
MT = SEQ // P
D = 1024
KD = D // P
NCOL = 512
RING = 8
EPS = 1e-6
NEG = -1e30

GLA_HEADS, GLA_DK, GLA_DV, GLA_RANK, GLA_TAU, CHUNK = 4, 128, 256, 16, 16.0, 64
NCH = SEQ // CHUNK
ATT_HEADS, HD = 4, 128
ATT_GROUPS = ((128, 1), (512, 4), (2048, 16))
REL_BUCKETS, REL_MAX_DIST = 32, 2048
D_FF, PLE = 4 * D, 256
LSTM_HEADS, LSTM_HD, CONV = 4, 256, 4
SB_HEADS = 8
POOL_WINDOWS = (2, 4, 8, 16)
POOL_PAD = 16
C_WIDTH = 2 * D

DIAG = (3 * P - 1, 2 * P - 1, 2 * P - 1)
DIAG_AT = (0, DIAG[0], DIAG[0] + DIAG[1])
KEYS = (2 * P, P, P)


def bucket_one_hot():
    out = np.zeros((REL_BUCKETS + 1, sum(DIAG)), np.float32)
    half = REL_BUCKETS // 2
    for g, (window, dil) in enumerate(ATT_GROUPS):
        for e in range(DIAG[g]):
            steps = (2 * P - 1 - e) if g == 0 else (P - 1 - e)
            ok = 0 <= steps <= P if g < 2 else steps >= 0 and steps % 4 == 0
            row = REL_BUCKETS
            if ok:
                dist = steps * (1 if g == 0 else 4)
                far = half + int(np.int32(
                    np.log(np.float32(max(dist, 1)) / half) / np.log(REL_MAX_DIST / half) * (REL_BUCKETS - half)))
                row = dist if dist < half else min(far, REL_BUCKETS - 1)
            out[row, DIAG_AT[g] + e] = 1.0
    return out


def pool_edges():
    t = np.arange(POOL_PAD) + 1
    return np.stack([w / np.minimum(t, w) for w in POOL_WINDOWS]).astype(np.float32)


class Slab:

    def __init__(self, name, sources, banks):
        self.name, self.sources, self.banks = name, sources, banks
        self.n = len(sources)

    def phys(self, c):
        return 1 if self.name == "lstm_f" else c % 4


def plan_slabs(W):
    slabs = []

    def slab(name, w, col, row=0, rows=D, banks=MT):
        slabs.append(Slab(name, [w[row + k * P:row + (k + 1) * P, col:col + NCOL] for k in range(rows // P)], banks))

    def narrow(w, col):
        return [w[b * 512:(b + 1) * 512, col:col + P].rearrange("(k p) c -> p k c", p=P) for b in range(2)]

    w_in, w_ab, w_c = W["w_in"], W["w_in_ab_2"], W["w_in_c_2"]
    qk, dv = GLA_HEADS * GLA_DK, GLA_HEADS * GLA_DV
    at_a = 2 * qk + 2 * dv
    at_att = at_a + GLA_RANK
    at_gate = at_att + len(ATT_GROUPS) * 3 * ATT_HEADS * HD
    slabs.append(Slab("gla_a", narrow(w_in, at_a), 1))
    slab("gla_q", w_in, 0)
    slab("gla_k", w_in, qk)
    for i in range(2):
        slab("gla_v", w_in, 2 * qk + i * NCOL)
    for i in range(2):
        slab("gla_r", w_in, 2 * qk + dv + i * NCOL)
    for g in range(len(ATT_GROUPS)):
        for which in range(2):
            slab(f"att_{'qk'[which]}{g}", w_in, at_att + (3 * g + which) * NCOL)
    for g in range(len(ATT_GROUPS)):
        slab(f"att_v{g}", w_in, at_att + (3 * g + 2) * NCOL)
    for i in range(4):
        slab("mix_gate", w_in, at_gate + i * NCOL)
    for i in range(2):
        slab("gla_out", W["w_o_gla"], i * NCOL)
    for i in range(2):
        slab("att_out", W["w_o_attn"], i * NCOL, rows=ATT_HEADS * HD)
    for i in range(2):
        slab("mix_out", W["w_out"], i * NCOL)

    def up(g):
        slab("mlp_up", W["w_mlp1"], g * NCOL)

    def down(g):
        for i in range(2):
            slab("mlp_down", W["w_mlp2"], i * NCOL, row=g * NCOL, rows=NCOL)

    up(0)
    for g in range(1, D_FF // NCOL):
        up(g)
        down(g - 1)
    down(D_FF // NCOL - 1)
    for i in range(2):
        slab("ple_p", W["w_pp"], i * NCOL, rows=PLE)
    for i in range(2):
        slab("ple_gate", W["w_pg"], i * NCOL)

    at_if = 5 * D
    at_b = at_if + 2 * LSTM_HEADS
    slabs.append(Slab("lstm_i", narrow(w_ab, at_if), 1))
    slabs.append(Slab("lstm_f", narrow(w_ab, at_if + LSTM_HEADS), 1))
    for at, name in enumerate(("lstm_q", "lstm_k", "lstm_v")):
        for i in range(2):
            slab(name, w_ab, at * D + i * NCOL)
    slabs.append(Slab("lstm_core", [], MT * LSTM_HEADS))
    for at, name in enumerate(("lstm_o", "lstm_z")):
        for i in range(2):
            slab(name, w_ab, (3 + at) * D + i * NCOL)
    for half in range(2):
        for at, name in enumerate(("sb_q", "sb_k", "sb_v")):
            slab(name, w_ab, at_b + at * D + half * NCOL)
    for i in range(2):
        slab("sb_z", w_ab, at_b + 3 * D + i * NCOL)
    for half in range(2):
        for i in range(2):
            slab(f"even_out{half}", W["w_out_ab_2"], i * NCOL, row=half * D)

    for i in range(4):
        slab("odd_z", w_c, C_WIDTH + i * NCOL)

    def pool_in(g):
        slab("pool_in", w_c, g * NCOL)

    def pool_mix(g):
        slab("pool_mix", W["pool_w_2"], 0, row=g * NCOL, rows=NCOL)

    pool_in(0)
    for g in range(1, len(POOL_WINDOWS)):
        pool_in(g)
        pool_mix(g - 1)
    pool_mix(len(POOL_WINDOWS) - 1)
    for half in range(2):
        for i in range(2):
            slab(f"odd_out{half}", W["w_out_c_2"], i * NCOL, row=half * D)

    first = bank0 = used0 = 0
    filled = [0] * 4
    for at, s in enumerate(slabs):
        s.at, s.first, s.bank0, s.used0, s.end = at, first, bank0, used0, bank0 + s.banks
        s.need = []
        for c in range(s.banks):
            b = 1 if s.name == "lstm_f" else c % 4
            s.need.append(filled[b])
            filled[b] = bank0 + c + 1
        first += s.n
        bank0 += s.banks
        used0 += max(s.n - 1, 0)
    return slabs


def two_blocks(nc, W, out):
    slabs = plan_slabs(W)
    by_name = {}
    for s in slabs:
        by_name.setdefault(s.name, []).append(s)
    blocks = [(s, j) for s in slabs for j in range(s.n)]
    n_blocks = len(blocks)

    ctx = ExitStack()
    with ctx:
        def sb(name, shape, dt=F32):
            return ctx.enter_context(nc.sbuf_tensor(name, shape, dt))

        def sem(name):
            return ctx.enter_context(nc.semaphore(name))

        w_raw = sb("w_raw", [P, RING, NCOL])
        w_hi = sb("w_hi", [P, RING, NCOL], F32R)
        w_lo = sb("w_lo", [P, RING, NCOL], F32R)
        act_hi = sb("act_hi", [P, KD, SEQ], F32R)
        act_lo = sb("act_lo", [P, KD, SEQ], F32R)
        aux0_hi = sb("aux0_hi", [P, 4, SEQ], F32R)
        aux0_lo = sb("aux0_lo", [P, 4, SEQ], F32R)
        x = sb("x", [P, MT, D])
        ARENA = 22560
        arena_at = nc.sbuf_base
        arena = sb("arena", [P, ARENA])
        AUX1_AT = 18432

        ident = sb("ident", [P, P])
        chunk_ok = sb("chunk_ok", [P, P])
        chunk_neg = sb("chunk_neg", [P, P])
        before_ok = sb("before_ok", [P, P])
        before_neg = sb("before_neg", [P, P])
        sel = sb("sel", [LSTM_HEADS, LSTM_HEADS, P])
        cols = sb("cols", [P, 140])
        eps_col, one_col = sb("eps_col", [P, 1]), sb("one_col", [P, 1])
        stat = sb("stat", [P, 16])
        rstd = sb("rstd", [P, 16])
        att_negmax = sb("att_negmax", [P, 48])
        att_sum = sb("att_sum", [P, 48])
        att_tmp = sb("att_tmp", [P, 48])
        att_coef = sb("att_coef", [P, 48])
        decay = sb("decay", [P, 32])
        lstm_cols = sb("lstm_cols", [P, 48])
        lstm_den = sb("lstm_den", [P, 16])
        lstm_m = sb("lstm_m", [LSTM_HEADS, NCH + 1])
        lstm_dec = sb("lstm_dec", [LSTM_HEADS, NCH])
        lstm_b = sb("lstm_b", [LSTM_HEADS, 2])
        edges = sb("edges", [P, len(POOL_WINDOWS), POOL_PAD])

        proj = ctx.enter_context(nc.psum_tensor("proj", [P, 4, 512], F32))
        work = ctx.enter_context(nc.psum_tensor("work", [P, 4, 512], F32))

        def view(at, *shape):
            n = int(np.prod(shape))
            assert at + n <= ARENA, (at, shape)
            v = arena[:, at:at + n]
            names = "abc"[:len(shape)]
            if len(shape) == 1:
                return v
            return v.rearrange(f"p ({' '.join(names)}) -> p {' '.join(names)}", **{c: k for c, k in zip(names, shape)})

        aux1_hi = nc.alloc_sbuf_tensor_at("aux1_hi", [P, 4, SEQ], F32R, offset=arena_at + 4 * AUX1_AT)
        aux1_lo = nc.alloc_sbuf_tensor_at("aux1_lo", [P, 4, SEQ], F32R, offset=arena_at + 4 * (AUX1_AT + 4 * SEQ))

        rows1, rows2 = view(0, P), view(P, P)
        rel_rows, rel_wide = view(2 * P, 12), view(512, 12, P)
        one_hot, diag_stage = view(2048, sum(DIAG)), view(4096, 4 * sum(DIAG))
        xs = view(12288, MT, D)
        squares = view(12288, MT * D)
        gla_o = view(0, MT, D)
        q_dec, k_in, k_out = view(4096, 4, SEQ), view(6144, 4, SEQ), view(8192, 4, SEQ)
        gla_b, k_tok = view(10240, 4, SEQ), view(10240, 4, SEQ)
        gla_v = view(12288, MT, D)
        gate_l1, gate_min = view(12288, 4, SEQ), view(14336, 4, SEQ)
        gla_state = view(16384, 2, GLA_HEADS, GLA_DV)
        reset, w_a2, gla_a = view(18432, SEQ), view(18944, SEQ), view(19456, SEQ)
        gla_att = view(18432, 4, SEQ)
        bias = [view(20480, 4, KEYS[0]), view(21504, 4, KEYS[1]), view(22016, 4, KEYS[2])]
        gla_silu = view(4096, 2, SEQ)
        att_p = [view(4096, 4, 4 * KEYS[0]), view(8192, 4, 4 * KEYS[1]), view(10240, 4, 4 * KEYS[2])]
        att_q, att_k = view(12288, 4, SEQ), view(14336, 4, SEQ)
        att_v = [view(12288, MT, SEQ), view(14336, MT, SEQ), view(16384, MT, SEQ)]
        att_pt = [view(18432, 7 * P), view(19328, 4 * P), view(19840, 4 * P)]
        lse_rows, lse_max = view(18432, 3, SEQ), view(19968, SEQ)
        att_o = view(20480, 4, SEQ)
        mix = view(4096, 16, SEQ)
        relu, relu_sq = view(0, 2, SEQ), view(1024, 2, SEQ)
        ple_pp, ple_in, ple_sig = view(0, MT, D), view(4096, MT, PLE), view(5120, 2, SEQ)
        ln_f_row = view(8192, D)
        lstm_q, lstm_k = view(0, KD, SEQ), view(4096, KD, SEQ)
        lstm_v, k_wa = view(8192, MT, LSTM_HEADS * (LSTM_HD + 1)), view(12304, MT, D)
        lstm_c = view(16400, 2 * LSTM_HEADS, LSTM_HD + 1)
        lstm_s, lstm_w = view(18456, 4, SEQ), view(20504, 2, SEQ)
        row = {k: view(16400 + i * SEQ, SEQ)[0:LSTM_HEADS, :] for i, k in enumerate(
            ("i", "f", "min", "l1", "b", "a", "e", "wa", "emt"))}
        row["neg_e"], row["inter"] = view(21528, SEQ)[0:LSTM_HEADS, :], view(22040, SEQ)[0:LSTM_HEADS, :]
        lstm_reset = view(21008, SEQ)
        lstm_h, gate_tmp = view(4096, MT, D), view(17408, 2, SEQ)
        sb_q, sb_k, sb_v, sb_o = view(8192, 4, SEQ), view(10240, 4, SEQ), view(12288, MT, SEQ), view(0, MT, D)
        sb_l, sb_c, sb_at = view(14336, 2, SEQ), view(15360, 2, SEQ), view(16384, 2, SEQ)
        y = view(8192, MT, D)
        post_row = [view(16384, D), view(17408, D)]
        odd_z = view(0, 16, SEQ)
        PADDED = POOL_PAD + SEQ
        pool_raw, pool_sum, pooled = view(8192, 2, PADDED), view(9248, 2, PADDED), view(10304, 2, SEQ)

        diag_dram = [nc.dram_tensor(f"bias_diag{g}", (4, P * DIAG[g]), F32, kind="Internal") for g in range(3)]

        LN1, LN2, LN3, PRE, GN, HN, BA, PS, CONV_AT = 0, 8, 16, 24, 40, 48, 56, 60, 76

        params_loaded, x_loaded = sem("params_loaded"), sem("x_loaded")
        consts_ready = sem("consts_ready")
        raw_loaded = [sem(f"raw_loaded{j}") for j in range(RING)]
        hi_ready, lo_ready = sem("hi_ready"), sem("lo_ready")
        block_used = sem("block_used")
        proj_full, proj_free = sem("proj_full"), sem("proj_free")
        act_hi_ready, act_ready = sem("act_hi_ready"), sem("act_ready")
        aux_hi_ready, aux_ready = sem("aux_hi_ready"), sem("aux_ready")
        turned = sem("turned")
        vec_step, act_step, pool_step = sem("vec_step"), sem("act_step"), sem("pool_step")
        cols_full, cols_ready = sem("cols_full"), sem("cols_ready")
        rel_ready, diag_full, diag_copied = sem("rel_ready"), sem("diag_full"), sem("diag_copied")
        diag_spilled = [sem(f"diag_spilled{g}") for g in range(3)]
        bias_loaded = sem("bias_loaded")
        root_ready, scaled = sem("root_ready"), sem("scaled")
        x_final = sem("x_final")
        gate_full, gate_l1_ready, gate_done = sem("gate_full"), sem("gate_l1_ready"), sem("gate_done")
        gla_exp, gla_rest = sem("gla_exp"), sem("gla_rest")
        ktok_full, ktok_ready = sem("ktok_full"), sem("ktok_ready")
        gla_att_full, gla_att_ready = sem("gla_att_full"), sem("gla_att_ready")
        gla_upd_full, gla_state_ready = sem("gla_upd_full"), sem("gla_state_ready")
        gla_o_full, gla_o_copied, gla_gated = sem("gla_o_full"), sem("gla_o_copied"), sem("gla_gated")
        logits_full, biased, max_ready, exp_ready = sem("logits_full"), sem("biased"), sem("max_ready"), sem("exp_ready")
        log_ready, lse_ready, lse_full = sem("log_ready"), sem("lse_ready"), sem("lse_full")
        lse_shifted, lse_exp, share_ready, share_full = sem("lse_shifted"), sem("lse_exp"), sem("share_ready"), sem("share_full")
        p_scaled, pt_full, pv_done, att_o_copied = sem("p_scaled"), sem("pt_full"), sem("pv_done"), sem("att_o_copied")
        pt_copied = [sem(f"pt_copied{g}") for g in range(3)]
        mix_ready = sem("mix_ready")
        squared = sem("squared")
        ple_loaded, ple_done = sem("ple_loaded"), sem("ple_done")
        lstm_f_ready, lstm_l1 = sem("lstm_f_ready"), sem("lstm_l1")
        lstm_rows, lstm_exps = sem("lstm_rows"), sem("lstm_exps")
        lstm_cols_full, lstm_cols_ready = sem("lstm_cols_full"), sem("lstm_cols_ready")
        conv_silu = sem("conv_silu")
        qk_full, neg_e_full, inter_full, lstm_kt_full = sem("qk_full"), sem("neg_e_full"), sem("inter_full"), sem("lstm_kt_full")
        w_masked, w_ready, s_ready, q_inter = sem("w_masked"), sem("w_ready"), sem("s_ready"), sem("q_inter")
        lstm_kt_ready, lstm_upd_full, lstm_c_ready = sem("lstm_kt_ready"), sem("lstm_upd_full"), sem("lstm_c_ready")
        lstm_gated, ya_ready = sem("lstm_gated"), sem("ya_ready")
        sb_z_full, sb_abs, sb_l1, sb_t, sb_a = sem("sb_z_full"), sem("sb_abs"), sem("sb_l1"), sem("sb_t"), sem("sb_a")
        sb_at_full, sb_at_ready, sb_o_full, sb_o_copied = sem("sb_at_full"), sem("sb_at_ready"), sem("sb_o_full"), sem("sb_o_copied")
        yb_ready, post_loaded = sem("yb_ready"), sem("post_loaded")
        pool_done = sem("pool_done")
        stored = sem("stored")

        def counted(fills):
            at, out_ = 0, {}
            for name, n in fills:
                out_[name] = at
                at += n
            return out_

        ACT_AT = counted([("ln1", 8), ("gla", 8), ("mix", 8), ("ln2", 8), ("ln3", 8), ("pre0", 8), ("yb", 8),
                          ("pre1", 8), ("mixa", 8)])
        AUX_AT = counted([("att", 4), ("mlp", 4 * (D_FF // NCOL)), ("p", 2), ("ya", 8), ("pool", 16), ("mixb", 8)])
        TURN_AT = counted([("ln1", 8), ("gla", 8), ("ln2", 8), ("p", 2), ("ln3", 8), ("pre0", 8), ("ya", 8), ("yb", 8),
                           ("pre1", 8)])
        NORM = {name: n for n, name in enumerate(("ln1", "ln2", "ln3", "pre0", "pre1"))}
        ROOT_AT = {name: n + 1 for n, name in enumerate(
            ("ln1", "gla", "ln2", "ln3", "ln_f", "pre0", "lstm", "post0", "pre1", "post1"))}

        def end(name, which=-1):
            return by_name[name][which].end

        def aux(tile):
            hi, lo = (aux0_hi, aux0_lo) if tile < 4 else (aux1_hi, aux1_lo)
            return hi[:, tile % 4, :], lo[:, tile % 4, :]

        def tile_of(pair):
            return {"act": lambda k: (act_hi[:, k, :], act_lo[:, k, :]), "aux0": aux, "aux1": lambda k: aux(k + 4),
                    "aux": aux}[pair]

        def wait_used(eng, block):
            s, j = blocks[block]
            if j == s.n - 1:
                eng.wait_ge(proj_full, s.end)
            else:
                eng.wait_ge(block_used, s.used0 + j + 1)

        first_up = by_name["mlp_up"][2]
        LOOP_TURNS = 3
        LOOP_SLABS = slabs[first_up.at:first_up.at + 6]
        LOOP_BLOCKS = sum(s.n for s in LOOP_SLABS)
        LOOP_BANKS = sum(s.banks for s in LOOP_SLABS)
        LOOP_USED = sum(s.n - 1 for s in LOOP_SLABS)

        block = ctx.enter_context(nc.Block())

        @block.sync
        def _(sp):
            for m in range(MT):
                sp.dma_start(x[:, m, :], W["x"][0, m * P:(m + 1) * P, :]).then_inc(x_loaded, 16)

            def load(b, src):
                if b >= RING:
                    sp.wait_ge(lo_ready, b - RING + 1)
                sp.dma_start(w_raw[:, b % RING, :] if len(src.shape) == 2 else
                             w_raw[:, b % RING, :].rearrange("p (k c) -> p k c", c=P), src)\
                  .then_inc(raw_loaded[b % RING], 16)

            at = 0
            while at < len(slabs):
                s = slabs[at]
                if s is first_up:
                    g0 = 2
                    with sp.Fori(0, LOOP_TURNS) as i:
                        b = s.first
                        for t in range(2):
                            for k in range(KD):
                                sp.wait_ge(lo_ready, i * LOOP_BLOCKS + (b - RING + 1))
                                sp.dma_start(w_raw[:, b % RING, :], W["w_mlp1"][
                                    k * P:(k + 1) * P, bass.ds(i * (2 * NCOL) + (g0 + t) * NCOL, NCOL)])\
                                  .then_inc(raw_loaded[b % RING], 16)
                                b += 1
                            for c in range(2):
                                for k in range(4):
                                    sp.wait_ge(lo_ready, i * LOOP_BLOCKS + (b - RING + 1))
                                    sp.dma_start(w_raw[:, b % RING, :], W["w_mlp2"][
                                        bass.ds(i * (2 * NCOL) + (g0 + t - 1) * NCOL + k * P, P),
                                        c * NCOL:(c + 1) * NCOL]).then_inc(raw_loaded[b % RING], 16)
                                    b += 1
                    at += LOOP_TURNS * len(LOOP_SLABS)
                    continue
                for j, src in enumerate(s.sources):
                    load(s.first + j, src)
                at += 1
            for m in range(MT):
                sp.wait_ge(x_final, 2 * MT + m + 1)
                sp.dma_start(out[0, m * P:(m + 1) * P, :], x[:, m, :]).then_inc(stored, 16)
            sp.wait_ge(stored, 16 * MT)

        @block.gpsimd
        def _(pool):
            steps = [0]

            def step(ins):
                steps[0] += 1
                ins.then_inc(pool_step, 1)
                pool.wait_ge(pool_step, steps[0])

            step(pool.memset(ident[:], 0.0))
            step(pool.affine_select(out=ident[:], in_=ident[:], compare_op=ALU.not_equal, fill=1.0, base=0,
                                    pattern=[[-1, P]], channel_multiplier=1))
            for ok, fill, keep, far in ((chunk_ok, 1.0, 0.0, 0.0), (chunk_neg, 0.0, NEG, NEG)):
                step(pool.memset(ok[:], fill))
                step(pool.affine_select(out=ok[:], in_=ok[:], compare_op=ALU.is_ge, fill=keep, base=0,
                                        pattern=[[1, P]], channel_multiplier=-1))
                step(pool.memset(ok[0:CHUNK, CHUNK:P], far))
            for ok, fill, keep in ((before_ok, 1.0, 0.0), (before_neg, 0.0, NEG)):
                step(pool.memset(ok[:], fill))
                step(pool.affine_select(out=ok[:], in_=ok[:], compare_op=ALU.is_gt, fill=keep, base=0,
                                        pattern=[[-1, P]], channel_multiplier=1))
            step(pool.memset(sel[:], 0.0))
            step(pool.affine_select(out=sel[:], in_=sel[:], compare_op=ALU.not_equal, fill=1.0, base=0,
                                    pattern=[[-1, LSTM_HEADS], [0, P]], channel_multiplier=1))
            step(pool.memset(one_col[:], 1.0))
            pool.memset(eps_col[:], EPS).then_inc(consts_ready, 1)

            def rest(slot):
                return pool.tensor_tensor(w_lo[:, slot, :], w_raw[:, slot, :], w_hi[:, slot, :].bitcast(F32), ALU.subtract)

            with pool.Fori(0, n_blocks // RING) as turn:
                for slot in range(RING):
                    pool.wait_ge(hi_ready, turn * RING + (slot + 1))
                    rest(slot).then_inc(lo_ready, 1)
            for b in range(n_blocks - n_blocks % RING, n_blocks):
                pool.wait_ge(hi_ready, b + 1)
                rest(b % RING).then_inc(lo_ready, 1)

        @block.scalar
        def _(act):
            steps = [0]

            def step(ins):
                steps[0] += 1
                ins.then_inc(act_step, 1)
                act.wait_ge(act_step, steps[0])

            def w_hi_of(b):
                act.wait_ge(raw_loaded[b % RING], 16 * (b // RING + 1))
                if b >= RING:
                    wait_used(act, b - RING)
                act.copy(w_hi[:, b % RING, :], w_raw[:, b % RING, :]).then_inc(hi_ready, 1)

            prepared = [0]

            def ahead(s):
                until = s
                while until.at + 1 < len(slabs) and (until is s or until.n == 0):
                    until = slabs[until.at + 1]
                while prepared[0] < until.first + until.n:
                    w_hi_of(prepared[0])
                    prepared[0] += 1

            def bank(s, c):
                act.wait_ge(proj_full, s.bank0 + c + 1)
                return proj[:, s.phys(c), :]

            def fill_hi(pair, base, n, turn=None, gain=None, src=None, ready=None, after=0):
                if after:
                    act.wait_ge(proj_full, after)
                sem_, tile = (act_hi_ready, tile_of(pair)) if pair == "act" else (aux_hi_ready, tile_of(pair))
                for k in range(n):
                    hi, _ = tile(k)
                    if turn is not None:
                        act.wait_ge(turned, turn + k + 1)
                        if gain is None:
                            act.copy(hi, work[:, k % 4, :]).then_inc(sem_, 1)
                        else:
                            act.activation(hi, work[:, k % 4, :], ACT.Copy, scale=cols[:, gain + k:gain + k + 1])\
                               .then_inc(sem_, 1)
                    else:
                        act.wait_ge(ready[0], ready[1](k))
                        act.copy(hi, src[:, k, :]).then_inc(sem_, 1)

            def roots(name, src, n_rows, width):
                for r in range(n_rows):
                    s_ = src(r)
                    ins = act.activation(squares[:, r * width:(r + 1) * width], s_, ACT.Square, accum_out=stat[:, r:r + 1])
                    if r == n_rows - 1:
                        step(ins)
                act.activation(stat[:, 0:n_rows], stat[:, 0:n_rows], ACT.Sqrt, bias=eps_col[:, 0:1],
                               scale=1.0 / width).then_inc(root_ready, 1)

            loads = [(rows1[LN1:LN1 + 8, :], W["ln1"].rearrange("a (k p) -> (a k) p", p=P)),
                     (rows1[LN2:LN2 + 8, :], W["ln2"].rearrange("a (k p) -> (a k) p", p=P)),
                     (rows1[LN3:LN3 + 8, :], W["ln3"].rearrange("a (k p) -> (a k) p", p=P)),
                     (rows1[PRE:PRE + 16, :], W["pre_norm_g_2"].rearrange("a (k p) -> (a k) p", p=P)),
                     (rows1[GN:GN + 8, :], W["gla_gn"].rearrange("a (k p) -> (a k) p", p=P)),
                     (rows1[HN:HN + 8, :], W["head_norm_g_2"].rearrange("a (k p) -> (a k) p", p=P)),
                     (rows1[BA:BA + 4, :], W["b_a"].rearrange("a (k p) -> (a k) p", p=P)),
                     (rows1[PS:PS + 16, :], W["pool_scale_2"].rearrange("a (k p) -> (a k) p", p=P)),
                     (rows2[0:64, :], W["conv_qk_2"].rearrange("t (k p) -> (t k) p", p=P)),
                     (rel_rows[0:REL_BUCKETS, :], W["rel_bias"]),
                     (one_hot[0:REL_BUCKETS + 1, :], W["bucket_one_hot"]),
                     (w_a2[0:GLA_RANK, :], W["w_a2"]),
                     (lstm_b[:, 0:1], W["bias_i_2"].rearrange("a h -> h a")),
                     (lstm_b[:, 1:2], W["bias_f_2"].rearrange("a h -> h a")),
                     (edges[:], bass.AP(W["pool_edges"].tensor, 0, [[0, P], [POOL_PAD, 4], [1, POOL_PAD]]))]
            for dst, src in loads:
                act.dma_start(dst, src).then_inc(params_loaded, 16)
            act.wait_ge(consts_ready, 1)
            act.wait_ge(x_loaded, 16 * MT)
            roots("ln1", lambda r: x[:, r, :], MT, D)
            a_slab = by_name["gla_a"][0]
            while prepared[0] < a_slab.first + a_slab.n:
                w_hi_of(prepared[0])
                prepared[0] += 1
            act.wait_ge(cols_ready, 1)
            fill_hi("act", ACT_AT["ln1"], KD, turn=TURN_AT["ln1"], gain=LN1)
            ahead(a_slab)
            for g in range(3):
                act.wait_ge(diag_copied, 4 * (g + 1))
                act.dma_start(diag_dram[g].ap().rearrange("h (p e) -> p h e", p=P),
                              diag_stage[:, 4 * DIAG_AT[g]:4 * (DIAG_AT[g] + DIAG[g])].rearrange(
                                  "p (h e) -> p h e", h=4)).then_inc(diag_spilled[g], 16)
            for g in range(3):
                act.wait_ge(diag_spilled[g], 16)
                act.dma_start(bias[g], bass.AP(diag_dram[g], P - 1, [[DIAG[g] - 1, P], [P * DIAG[g], 4], [1, KEYS[g]]]))\
                   .then_inc(bias_loaded, 16)

            act.wait_ge(gate_full, GLA_HEADS)
            for h in range(GLA_HEADS):
                ins = act.activation(gate_l1[:, h, :], work[:, h, :], ACT.Abs, bias=cols[:, BA + h:BA + h + 1])
            step(ins)
            step(act.activation(gate_l1, gate_l1, ACT.Exp, scale=-1.0))
            act.activation(gate_l1, gate_l1, ACT.Ln, bias=1.0).then_inc(gate_l1_ready, 1)
            act.wait_ge(gate_done, 1)
            act.activation(q_dec, gla_b, ACT.Exp, scale=1.0 / GLA_TAU).then_inc(gla_exp, 1)
            act.activation(k_in, gla_b, ACT.Exp, scale=-1.0 / GLA_TAU).then_inc(gla_exp, 1)
            act.activation(decay[:, :].rearrange("p (h c) -> p h c", h=4),
                           gla_b.rearrange("p h (c t) -> p h c t", t=CHUNK)[:, :, :, CHUNK - 1],
                           ACT.Exp, scale=1.0 / GLA_TAU).then_inc(gla_exp, 1)
            act.wait_ge(gla_rest, 1)
            act.activation(k_out, gate_l1, ACT.Exp, scale=1.0 / GLA_TAU).then_inc(gla_exp, 1)
            ahead(by_name["gla_q"][0])
            ahead(by_name["gla_k"][0])
            for i, s in enumerate(by_name["gla_v"]):
                ahead(s)
                for m in range(MT):
                    act.copy(gla_v[:, m, i * NCOL:(i + 1) * NCOL], bank(s, m)).then_inc(proj_free, 1)
            for h in range(GLA_HEADS):
                act.wait_ge(ktok_full, h + 1)
                act.copy(k_tok[:, h, :], work[:, h, :]).then_inc(ktok_ready, 1)
            for m in range(MT):
                for b in range(2):
                    act.wait_ge(gla_o_full, 2 * m + b + 1)
                    act.copy(gla_o[:, m, b * 512:(b + 1) * 512], work[:, b, :]).then_inc(gla_o_copied, 1)
            act.wait_ge(gla_o_copied, 2 * MT)
            roots("gla", lambda r: gla_o[:, r // GLA_HEADS, (r % GLA_HEADS) * GLA_DV:(r % GLA_HEADS + 1) * GLA_DV],
                  MT * GLA_HEADS, GLA_DV)
            n = 0
            for s in by_name["gla_r"]:
                ahead(s)
                for m in range(MT):
                    if n >= 2:
                        act.wait_ge(gla_gated, n - 1)
                    act.activation(gla_silu[:, n % 2, :], bank(s, m), ACT.Silu).then_inc(proj_free, 1)
                    n += 1

            for g in range(3):
                sq, sk = by_name[f"att_q{g}"][0], by_name[f"att_k{g}"][0]
                ahead(sq)
                ahead(sk)
                for h in range(ATT_HEADS):
                    bank(sk, h)
                    if g and h == 0:
                        act.wait_ge(logits_full, 4 * g)
                    src = proj[:, h, :] if g == 0 else proj[:, h, :].rearrange("p (l z) -> p z l", z=4)
                    dst = att_k[:, h, :] if g == 0 else att_k[:, h, :].rearrange("p (z l) -> p z l", z=4)
                    act.copy(dst, src).then_inc(proj_free, 1)
                for h in range(ATT_HEADS):
                    act.wait_ge(max_ready, 4 * g + h + 1)
                    for z in range(4):
                        c = (g * 4 + z) * 4 + h
                        p_ = att_p[g][:, h, z * KEYS[g]:(z + 1) * KEYS[g]]
                        ins = act.activation(p_, p_, ACT.Exp, bias=att_negmax[:, c:c + 1],
                                             accum_out=att_sum[:, c:c + 1])
                    ins.then_inc(exp_ready, 1)
            act.wait_ge(exp_ready, 12)
            act.activation(att_tmp[:], att_sum[:], ACT.Ln).then_inc(log_ready, 1)

            def values(g):
                s = by_name[f"att_v{g}"][0]
                ahead(s)
                for m in range(MT):
                    act.copy(att_v[g][:, m, :], bank(s, m)).then_inc(proj_free, 1)

            values(0)
            act.wait_ge(lse_shifted, 1)
            act.activation(lse_rows[0:4], lse_rows[0:4], ACT.Exp).then_inc(lse_exp, 1)
            values(1)
            values(2)
            for h in range(ATT_HEADS):
                act.wait_ge(pt_full, 3 * h + 1)
                if h:
                    act.wait_ge(pv_done, 3 * h - 2)
                act.copy(att_pt[0][:, 0:512], work[:, 0, :]).then_inc(pt_copied[0], 1)
                act.copy(att_pt[0][:, 512:7 * P], work[:, 1, 0:3 * P]).then_inc(pt_copied[0], 1)
            for i, s in enumerate(by_name["mix_gate"]):
                ahead(s)
                for c in range(4):
                    act.activation(mix[:, 4 * i + c, :], bank(s, c), ACT.Sigmoid).then_inc(proj_free, 1)
            fill_hi("aux0", AUX_AT["att"], 4, src=att_o, ready=(att_o_copied, lambda k: k + 1))
            fill_hi("act", ACT_AT["gla"], KD, turn=TURN_AT["gla"], gain=GN, after=end("mix_gate"))
            for s in by_name["gla_out"] + by_name["att_out"]:
                ahead(s)
            fill_hi("act", ACT_AT["mix"], KD, src=mix, ready=(mix_ready, lambda k: k + 1), after=end("gla_out"))
            for s in by_name["mix_out"]:
                ahead(s)

            act.wait_ge(proj_free, end("mix_out"))
            act.dma_start(ple_in, W["p"][0, 0].rearrange("(m p) c -> p m c", p=P)).then_inc(ple_loaded, 16)
            act.dma_start(ln_f_row, bass.AP(W["ln_f"].tensor, 0, [[0, P], [1, D]])).then_inc(ple_loaded, 16)
            roots("ln2", lambda r: x[:, r, :], MT, D)
            fill_hi("act", ACT_AT["ln2"], KD, turn=TURN_AT["ln2"], gain=LN2, after=end("mix_out"))

            def mlp_turned(full, n, par, n0):
                for c in range(4):
                    act.wait_ge(proj_full, full + (c + 1))
                    if n0 + c >= 2:
                        act.wait_ge(squared, n + (c - 1))
                        act.wait_ge(aux_hi_ready, AUX_AT["mlp"] + n + (c - 1))
                    act.activation(relu[:, c % 2, :], proj[:, c, :], ACT.Relu).then_inc(proj_free, 1)
                    act.wait_ge(proj_free, full + (c + 1))
                    act.activation(aux(4 * par + c)[0], relu[:, c % 2, :], ACT.Square).then_inc(aux_hi_ready, 1)

            ups, downs = by_name["mlp_up"], by_name["mlp_down"]
            for g in range(2):
                ahead(ups[g])
                mlp_turned(ups[g].bank0, 4 * g, g, 4 * g)
            s0 = LOOP_SLABS[0]
            while prepared[0] < s0.first:
                w_hi_of(prepared[0])
                prepared[0] += 1
            with act.Fori(0, LOOP_TURNS) as i:
                b = s0.first

                def loop_hi(n):
                    nonlocal b
                    for _ in range(n):
                        act.wait_ge(raw_loaded[b % RING], i * (16 * LOOP_BLOCKS // RING) + 16 * (b // RING + 1))
                        r = b - RING
                        if r < s0.first:
                            rs, rj = blocks[r + LOOP_BLOCKS]
                            full, used = rs.end - LOOP_BANKS, rs.used0 - LOOP_USED
                        else:
                            rs, rj = blocks[r]
                            full, used = rs.end, rs.used0
                        if rj == rs.n - 1:
                            act.wait_ge(proj_full, i * LOOP_BANKS + full)
                        else:
                            act.wait_ge(block_used, i * LOOP_USED + (used + rj + 1))
                        act.copy(w_hi[:, b % RING, :], w_raw[:, b % RING, :]).then_inc(hi_ready, 1)
                        b += 1

                for t in range(2):
                    up = LOOP_SLABS[3 * t]
                    loop_hi(KD)
                    loop_hi(4)
                    mlp_turned(i * LOOP_BANKS + up.bank0, i * 8 + 4 * (2 + t), t, 8)
                    loop_hi(4)
            prepared[0] += LOOP_TURNS * LOOP_BLOCKS

            down_end = end("mlp_down")
            ahead(downs[-1])
            fill_hi("aux0", AUX_AT["p"], 2, turn=TURN_AT["p"], after=end("mlp_up"))
            for i, s in enumerate(by_name["ple_p"]):
                ahead(s)
                for m in range(MT):
                    act.copy(ple_pp[:, m, i * NCOL:(i + 1) * NCOL], bank(s, m)).then_inc(proj_free, 1)
            act.wait_ge(proj_free, down_end)
            roots("ln3", lambda r: x[:, r, :], MT, D)
            fill_hi("act", ACT_AT["ln3"], KD, turn=TURN_AT["ln3"], gain=LN3, after=end("mlp_up"))
            n = 0
            for s in by_name["ple_gate"]:
                ahead(s)
                for m in range(MT):
                    if n >= 2:
                        act.wait_ge(ple_done, n - 1)
                    act.activation(ple_sig[:, n % 2, :], bank(s, m), ACT.Sigmoid).then_inc(proj_free, 1)
                    n += 1
            act.wait_ge(ple_done, 2 * MT)
            roots("ln_f", lambda r: x[:, r, :], MT, D)
            act.wait_ge(x_final, MT)
            roots("pre0", lambda r: x[:, r, :], MT, D)
            fill_hi("act", ACT_AT["pre0"], KD, turn=TURN_AT["pre0"], gain=PRE, after=end("ple_gate"))

            ahead(by_name["lstm_i"][0])
            ahead(by_name["lstm_f"][0])
            act.wait_ge(lstm_f_ready, 1)
            step(act.activation(row["l1"], row["f"], ACT.Abs))
            step(act.activation(row["l1"], row["l1"], ACT.Exp, scale=-1.0))
            act.activation(row["l1"], row["l1"], ACT.Ln, bias=1.0).then_inc(lstm_l1, 1)
            act.wait_ge(lstm_rows, 1)
            act.activation(row["inter"], row["inter"], ACT.Exp).then_inc(lstm_exps, 1)
            act.activation(row["wa"], row["wa"], ACT.Exp).then_inc(lstm_exps, 1)
            act.activation(row["emt"], row["emt"], ACT.Exp, scale=-1.0).then_inc(lstm_exps, 1)
            act.activation(lstm_dec[:], lstm_dec[:], ACT.Exp).then_inc(lstm_exps, 1)
            for dst, name in ((lstm_q, "lstm_q"), (lstm_k, "lstm_k")):
                for i, s in enumerate(by_name[name]):
                    ahead(s)
                    for c in range(4):
                        act.wait_ge(proj_free, s.bank0 + c + 1)
                        act.activation(dst[:, 4 * i + c, :], dst[:, 4 * i + c, :], ACT.Silu).then_inc(conv_silu, 1)
            v4 = lstm_v.rearrange("p m (h c) -> p m h c", h=LSTM_HEADS)
            for i, s in enumerate(by_name["lstm_v"]):
                ahead(s)
                for m in range(MT):
                    act.copy(v4[:, m, 2 * i:2 * i + 2, 0:LSTM_HD],
                             bank(s, m).rearrange("p (h c) -> p h c", h=2)).then_inc(proj_free, 1)
            for h in range(LSTM_HEADS):
                act.wait_ge(w_masked, h + 1)
                for m in range(MT):
                    w_ = lstm_w[:, h % 2, m * P:(m + 1) * P]
                    ins = act.activation(w_, w_, ACT.Exp, bias=lstm_cols[:, m * 4 + h:m * 4 + h + 1])
                ins.then_inc(w_ready, 1)
            n = 0
            for s in by_name["lstm_o"]:
                ahead(s)
                for m in range(MT):
                    if n >= 2:
                        act.wait_ge(lstm_gated, n - 1)
                    act.activation(gate_tmp[:, n % 2, :], bank(s, m), ACT.Sigmoid).then_inc(proj_free, 1)
                    n += 1
            act.wait_ge(lstm_gated, 2 * MT)
            roots("lstm", lambda r: lstm_h[:, r // LSTM_HEADS, (r % LSTM_HEADS) * LSTM_HD:(r % LSTM_HEADS + 1) * LSTM_HD],
                  MT * LSTM_HEADS, LSTM_HD)
            n = 0
            for s in by_name["lstm_z"]:
                ahead(s)
                for m in range(MT):
                    if n >= 2:
                        act.wait_ge(ya_ready, n - 1)
                    act.activation(gate_tmp[:, n % 2, :], bank(s, m), ACT.Silu).then_inc(proj_free, 1)
                    n += 1
            fill_hi("aux", AUX_AT["ya"], KD, turn=TURN_AT["ya"], gain=HN)

            for half in range(2):
                ahead(by_name["sb_q"][half])
                ahead(by_name["sb_k"][half])
                s = by_name["sb_v"][half]
                ahead(s)
                for m in range(MT):
                    act.copy(sb_v[:, m, :], bank(s, m)).then_inc(proj_free, 1)
                u0 = 16 * half

                def log_terms(u):
                    nk = (u % 4 + 1) * P
                    l_ = sb_l[:, u % 2, 0:nk]
                    act.wait_ge(sb_z_full, u + 1)
                    if u >= 2:
                        act.wait_ge(sb_t, u - 1)
                    act.activation(l_, work[:, u % 2, 0:nk], ACT.Abs).then_inc(sb_abs, 1)
                    act.wait_ge(sb_abs, u + 1)
                    step(act.activation(l_, l_, ACT.Exp, scale=-1.0))
                    act.activation(l_, l_, ACT.Ln, bias=1.0).then_inc(sb_l1, 1)

                def weights(u):
                    nk = (u % 4 + 1) * P
                    act.wait_ge(sb_t, u + 1)
                    act.activation(sb_c[:, u % 2, 0:nk], sb_c[:, u % 2, 0:nk], ACT.Exp).then_inc(sb_a, 1)
                    act.wait_ge(sb_at_full, u + 1)
                    if u >= 2:
                        act.wait_ge(sb_o_full, u - 1)
                    act.copy(sb_at[:, u % 2, 0:nk], work[:, 2, 0:nk]).then_inc(sb_at_ready, 1)

                for u in range(u0, u0 + 16):
                    log_terms(u)
                    if u > u0:
                        weights(u - 1)
                weights(u0 + 15)
            n = 0
            for s in by_name["sb_z"]:
                ahead(s)
                for m in range(MT):
                    if n >= 2:
                        act.wait_ge(yb_ready, n - 1)
                    act.activation(gate_tmp[:, n % 2, :], bank(s, m), ACT.Silu).then_inc(proj_free, 1)
                    n += 1
            act.wait_ge(yb_ready, 2 * MT)
            for r in range(2):
                act.dma_start(post_row[r], bass.AP(W["post_norm_g_2"].tensor, r * D, [[0, P], [1, D]]))\
                   .then_inc(post_loaded, 16)
            for s in by_name["even_out0"]:
                ahead(s)
            fill_hi("act", ACT_AT["yb"], KD, turn=TURN_AT["yb"], after=end("sb_z"))
            for s in by_name["even_out1"]:
                ahead(s)
            act.wait_ge(proj_free, end("even_out1"))
            roots("post0", lambda r: y[:, r, :], MT, D)
            act.wait_ge(x_final, 2 * MT)
            roots("pre1", lambda r: x[:, r, :], MT, D)
            fill_hi("act", ACT_AT["pre1"], KD, turn=TURN_AT["pre1"], gain=PRE + 8, after=end("even_out1"))

            for i, s in enumerate(by_name["odd_z"]):
                ahead(s)
                for c in range(4):
                    act.activation(odd_z[:, 4 * i + c, :], bank(s, c), ACT.Silu).then_inc(proj_free, 1)
            def pool_hi_of(n):
                act.wait_ge(pool_done, n + 1)
                act.copy(aux(n % 8)[0], pooled[:, n % 2, :]).then_inc(aux_hi_ready, 1)

            n = 0
            for g, s in enumerate(by_name["pool_in"]):
                ahead(s)
                for c in range(4):
                    if n >= 2:
                        act.wait_ge(pool_done, n - 1)
                    act.copy(pool_raw[:, n % 2, POOL_PAD:PADDED], bank(s, c)).then_inc(proj_free, 1)
                    if n:
                        pool_hi_of(n - 1)
                    n += 1
                if g == 3:
                    pool_hi_of(n - 1)
                if g:
                    ahead(by_name["pool_mix"][g - 1])
            ahead(by_name["pool_mix"][3])
            fill_hi("act", ACT_AT["mixa"], KD, src=odd_z, after=end("pool_in"),
                    ready=(proj_free, lambda k: by_name["pool_mix"][k // 4].bank0 + k % 4 + 1))
            for s in by_name["odd_out0"]:
                ahead(s)
            fill_hi("aux", AUX_AT["mixb"], KD, src=odd_z[:, KD:2 * KD, :], after=end("pool_mix"),
                    ready=(proj_free, lambda k: by_name["pool_mix"][2 + k // 4].bank0 + k % 4 + 1))
            for s in by_name["odd_out1"]:
                ahead(s)
            act.wait_ge(proj_free, end("odd_out1"))
            roots("post1", lambda r: y[:, r, :], MT, D)

        @block.vector
        def _(vec):
            steps = [0]

            def step(ins):
                steps[0] += 1
                ins.then_inc(vec_step, 1)
                vec.wait_ge(vec_step, steps[0])

            def bank(s, c):
                vec.wait_ge(proj_full, s.bank0 + c + 1)
                return proj[:, s.phys(c), :]

            def fill_lo(pair, base, n, turn=False, gain=None, src=None):
                hi_sem, sem_ = (act_hi_ready, act_ready) if pair == "act" else (aux_hi_ready, aux_ready)
                for k in range(n):
                    hi, lo = tile_of(pair)(k)
                    vec.wait_ge(hi_sem, base + k + 1)
                    v = work[:, k % 4, :] if turn else src[:, k, :]
                    if gain is None:
                        vec.tensor_tensor(lo, v, hi.bitcast(F32), ALU.subtract).then_inc(sem_, 1)
                    else:
                        vec.scalar_tensor_tensor(lo, v, cols[:, gain + k:gain + k + 1], hi.bitcast(F32),
                                                 ALU.mult, ALU.subtract).then_inc(sem_, 1)

            def scales(name, n):
                vec.wait_ge(root_ready, ROOT_AT[name])
                step(vec.reciprocal(rstd[:, 0:n], stat[:, 0:n]))

            def scaled_tokens(name):
                scales(name, MT)
                for m in range(MT):
                    vec.tensor_scalar(xs[:, m, :], x[:, m, :], rstd[:, m:m + 1], None, ALU.mult).then_inc(scaled, 1)

            def add_to_x(s, i):
                for m in range(MT):
                    xm = x[:, m, i * NCOL:(i + 1) * NCOL]
                    vec.tensor_tensor(xm, xm, bank(s, m), ALU.add).then_inc(proj_free, 1)

            vec.wait_ge(params_loaded, 16 * 15)
            step(vec.memset(rel_rows[REL_BUCKETS:REL_BUCKETS + 1, :], NEG))
            vec.tensor_copy(rel_wide[0:REL_BUCKETS + 1], rel_rows[0:REL_BUCKETS + 1, :].unsqueeze(2).to_broadcast(
                [REL_BUCKETS + 1, 12, P])).then_inc(rel_ready, 1)
            vec.wait_ge(cols_full, 1)
            vec.tensor_copy(cols[:, 0:CONV_AT], work[:, 0, 0:CONV_AT])
            vec.tensor_copy(cols[:, CONV_AT:CONV_AT + 64], work[:, 0, P:P + 64]).then_inc(cols_ready, 1)
            vec.wait_ge(cols_ready, 1)
            for n in range(12):
                g, h = n // 4, n % 4
                vec.wait_ge(diag_full, n + 1)
                vec.tensor_copy(diag_stage[:, 4 * DIAG_AT[g] + h * DIAG[g]:4 * DIAG_AT[g] + (h + 1) * DIAG[g]],
                                work[:, 1 + n % 3, 0:DIAG[g]]).then_inc(diag_copied, 1)
            scaled_tokens("ln1")
            fill_lo("act", ACT_AT["ln1"], KD, turn=True, gain=LN1)

            step(vec.memset(reset, 1.0))
            step(vec.memset(reset.rearrange("p (c t) -> p c t", t=CHUNK)[:, :, 0:1], 0.0))
            vec.tensor_copy(gla_a[0:GLA_RANK, :], bank(by_name["gla_a"][0], 0)[0:GLA_RANK, :]).then_inc(proj_free, 1)
            vec.wait_ge(gate_l1_ready, 1)
            for h in range(GLA_HEADS):
                ins = vec.tensor_scalar(gate_min[:, h, :], work[:, h, :], cols[:, BA + h:BA + h + 1], 0.0, ALU.add, ALU.min)
            step(ins)
            step(vec.tensor_tensor(gate_min, gate_min, gate_l1, ALU.subtract))
            for h in range(GLA_HEADS):
                ins = vec.tensor_tensor_scan(gla_b[:, h, :], reset, gate_min[:, h, :], 0.0, ALU.mult, ALU.add)
            ins.then_inc(gate_done, 1)
            vec.wait_ge(gate_done, 1)
            b_chunks = gla_b.rearrange("p h (c t) -> p (h c) t", t=CHUNK)
            vec.tensor_tensor(gate_l1.rearrange("p h (c t) -> p (h c) t", t=CHUNK),
                              b_chunks[:, :, CHUNK - 1:CHUNK].to_broadcast([P, GLA_HEADS * NCH, CHUNK]),
                              b_chunks, ALU.subtract).then_inc(gla_rest, 1)
            vec.wait_ge(gate_full, GLA_HEADS)
            step(vec.memset(gla_att, 0.0))
            s = by_name["gla_q"][0]
            vec.wait_ge(gla_exp, 1)
            for h in range(GLA_HEADS):
                vec.scalar_tensor_tensor(q_dec[:, h, :], bank(s, h), GLA_DK ** -0.5, q_dec[:, h, :],
                                         ALU.mult, ALU.mult).then_inc(proj_free, 1)
            s = by_name["gla_k"][0]
            vec.wait_ge(gla_exp, 4)
            for h in range(GLA_HEADS):
                k_ = bank(s, h)
                vec.tensor_tensor(k_in[:, h, :], k_in[:, h, :], k_, ALU.mult)
                vec.tensor_tensor(k_out[:, h, :], k_out[:, h, :], k_, ALU.mult).then_inc(proj_free, 1)
            for h in range(GLA_HEADS):
                vec.wait_ge(gla_att_full, h + 1)
                vec.copy_predicated(gla_att[:, h, :].rearrange("p (m t) -> p m t", m=MT),
                                    chunk_ok[:].bitcast(U32).unsqueeze(1).to_broadcast([P, MT, P]),
                                    work[:, h, :].rearrange("p (m t) -> p m t", m=MT)).then_inc(gla_att_ready, 1)
            for n in range(NCH - 1):
                for h in range(GLA_HEADS):
                    if h % 2 == 0:
                        vec.wait_ge(gla_upd_full, 2 * n + h // 2 + 1)
                    upd = work[:, 2 + h // 2, (h % 2) * GLA_DV:(h % 2 + 1) * GLA_DV]
                    new = gla_state[:, (n + 1) % 2, h, :]
                    if n == 0:
                        vec.tensor_copy(new, upd).then_inc(gla_state_ready, 1)
                    else:
                        vec.wait_ge(gla_state_ready, 4 * (n - 1) + h + 1)
                        vec.scalar_tensor_tensor(new, gla_state[:, n % 2, h, :], decay[:, h * NCH + n:h * NCH + n + 1],
                                                 upd, ALU.mult, ALU.add).then_inc(gla_state_ready, 1)
            scales("gla", MT * GLA_HEADS)
            n = 0
            for i, s in enumerate(by_name["gla_r"]):
                for m in range(MT):
                    vec.wait_ge(proj_free, s.bank0 + m + 1)
                    for hh in range(2):
                        h = 2 * i + hh
                        o_ = gla_o[:, m, h * GLA_DV:(h + 1) * GLA_DV]
                        ins = vec.scalar_tensor_tensor(o_, o_, rstd[:, m * 4 + h:m * 4 + h + 1],
                                                       gla_silu[:, n % 2, hh * GLA_DV:(hh + 1) * GLA_DV], ALU.mult, ALU.mult)
                    ins.then_inc(gla_gated, 1)
                    n += 1

            vec.wait_ge(bias_loaded, 16 * 3)
            vec.wait_ge(gla_gated, 2 * MT)
            p0 = att_p[0].rearrange("p h (z k) -> p h z k", z=4)
            vec.memset(p0[:, :, 0, 0:P], NEG)
            for g in range(3):
                s = by_name[f"att_q{g}"][0]
                for h in range(ATT_HEADS):
                    src = bank(s, h)
                    if g and h == 0:
                        vec.wait_ge(logits_full, 4 * g)
                    dst = att_q[:, h, :]
                    if g:
                        src, dst = src.rearrange("p (l z) -> p z l", z=4), dst.rearrange("p (z l) -> p z l", z=4)
                    vec.tensor_copy(dst, src).then_inc(proj_free, 1)
                for h in range(ATT_HEADS):
                    vec.wait_ge(logits_full, 4 * g + h + 1)
                    b_ = bias[g][:, h, :]
                    p_ = att_p[g][:, h, :].rearrange("p (z k) -> p z k", z=4)

                    def biased_logits(dst, src, b):
                        return vec.scalar_tensor_tensor(dst, src, HD ** -0.5, b, ALU.mult, ALU.add)

                    if g == 0:
                        b0 = 2 * (h % 2)
                        biased_logits(p_[:, 0, P:2 * P], work[:, b0, 0:P], b_[:, P:2 * P])
                        biased_logits(p_[:, 1, :], work[:, b0, 2 * P:4 * P], b_)
                        ins = biased_logits(p_[:, 2:4, :], work[:, b0 + 1, :].rearrange("p (z k) -> p z k", z=2),
                                            b_.unsqueeze(1).to_broadcast([P, 2, 2 * P]))
                    else:
                        ins = biased_logits(p_, work[:, h, :].rearrange("p (z k) -> p z k", z=4),
                                            b_.unsqueeze(1).to_broadcast([P, 4, P]))
                    ins.then_inc(biased, 1)
                    vec.wait_ge(biased, 4 * g + h + 1)
                    nm = att_negmax[:, 16 * g:16 * g + 16].rearrange("p (z h) -> p z h", z=4)[:, :, h]
                    step(vec.tensor_reduce(nm, p_, AX, ALU.max))
                    vec.tensor_scalar(nm, nm, -1.0, None, ALU.mult).then_inc(max_ready, 1)
            vec.wait_ge(log_ready, 1)
            vec.tensor_tensor(att_tmp[:], att_tmp[:], att_negmax[:], ALU.subtract).then_inc(lse_ready, 1)
            for g in range(3):
                vec.wait_ge(lse_full, g + 1)
                src, dst = work[0:4, g, :], lse_rows[0:4, g, :]
                if g:
                    src, dst = src.rearrange("p (z l) -> p z l", z=4), dst.rearrange("p (l z) -> p z l", z=4)
                step(vec.tensor_copy(dst, src))
            top_ = lse_max[0:4, :]
            step(vec.tensor_tensor(top_, lse_rows[0:4, 0, :], lse_rows[0:4, 1, :], ALU.max))
            step(vec.tensor_tensor(top_, top_, lse_rows[0:4, 2, :], ALU.max))
            vec.tensor_tensor(lse_rows[0:4], lse_rows[0:4], top_.unsqueeze(1).to_broadcast([4, 3, SEQ]), ALU.subtract)\
               .then_inc(lse_shifted, 1)
            vec.wait_ge(lse_exp, 1)
            step(vec.tensor_tensor(top_, lse_rows[0:4, 0, :], lse_rows[0:4, 1, :], ALU.add))
            step(vec.tensor_tensor(top_, top_, lse_rows[0:4, 2, :], ALU.add))
            step(vec.reciprocal(top_, top_))
            vec.tensor_tensor(lse_rows[0:4], lse_rows[0:4], top_.unsqueeze(1).to_broadcast([4, 3, SEQ]), ALU.mult)\
               .then_inc(share_ready, 1)
            step(vec.reciprocal(att_coef[:], att_sum[:]))
            vec.wait_ge(share_full, 1)
            step(vec.tensor_tensor(att_coef[:], att_coef[:], work[:, 3, 0:48], ALU.mult))
            for h in range(ATT_HEADS):
                for g in range(3):
                    for z in range(4):
                        p_ = att_p[g][:, h, z * KEYS[g]:(z + 1) * KEYS[g]]
                        c = (g * 4 + z) * 4 + h
                        ins = vec.tensor_scalar(p_, p_, att_coef[:, c:c + 1], None, ALU.mult)
                    ins.then_inc(p_scaled, 1)
            for h in range(ATT_HEADS):
                for g in (1, 2):
                    vec.wait_ge(pt_full, 3 * h + g + 1)
                    if h:
                        vec.wait_ge(pv_done, 3 * (h - 1) + g + 1)
                    vec.tensor_copy(att_pt[g], work[:, 2 if g == 1 else 0, :]).then_inc(pt_copied[g], 1)
                vec.wait_ge(pv_done, 3 * h + 3)
                vec.tensor_copy(att_o[:, h, :], work[:, 3, :]).then_inc(att_o_copied, 1)
            fill_lo("aux0", AUX_AT["att"], 4, src=att_o)
            fill_lo("act", ACT_AT["gla"], KD, turn=True, gain=GN)
            for i, s in enumerate(by_name["gla_out"]):
                for c in range(4):
                    t = mix[:, 4 * i + c, :]
                    vec.tensor_tensor(t, t, bank(s, c), ALU.mult).then_inc(proj_free, 1)
            for i, s in enumerate(by_name["att_out"]):
                for c in range(4):
                    t, u = mix[:, 4 * i + c, :], mix[:, 8 + 4 * i + c, :]
                    vec.tensor_tensor(u, u, bank(s, c), ALU.mult).then_inc(proj_free, 1)
                    vec.wait_ge(proj_free, s.bank0 + c + 1)
                    vec.tensor_tensor(t, t, u, ALU.add).then_inc(mix_ready, 1)
            fill_lo("act", ACT_AT["mix"], KD, src=mix)
            for i, s in enumerate(by_name["mix_out"]):
                add_to_x(s, i)

            scaled_tokens("ln2")
            fill_lo("act", ACT_AT["ln2"], KD, turn=True, gain=LN2)
            ups, downs = by_name["mlp_up"], by_name["mlp_down"]

            def mlp_rest(full, n, par, n0):
                for c in range(4):
                    vec.wait_ge(proj_free, full + (c + 1))
                    if n0 + c >= 2:
                        vec.wait_ge(aux_ready, AUX_AT["mlp"] + n + (c - 1))
                    vec.tensor_tensor(relu_sq[:, c % 2, :], relu[:, c % 2, :], relu[:, c % 2, :], ALU.mult).then_inc(squared, 1)
                    vec.wait_ge(squared, n + (c + 1))
                    vec.wait_ge(aux_hi_ready, AUX_AT["mlp"] + n + (c + 1))
                    hi, lo = aux(4 * par + c)
                    vec.tensor_tensor(lo, relu_sq[:, c % 2, :], hi.bitcast(F32), ALU.subtract).then_inc(aux_ready, 1)

            def mlp_add(full, i):
                for m in range(MT):
                    xm = x[:, m, i * NCOL:(i + 1) * NCOL]
                    vec.wait_ge(proj_full, full + (m + 1))
                    vec.tensor_tensor(xm, xm, proj[:, m, :], ALU.add).then_inc(proj_free, 1)

            mlp_rest(ups[0].bank0, 0, 0, 0)
            mlp_rest(ups[1].bank0, 4, 1, 4)
            for i in range(2):
                mlp_add(downs[i].bank0, i)
            with vec.Fori(0, LOOP_TURNS) as turn:
                for t in range(2):
                    up, d0, d1 = LOOP_SLABS[3 * t:3 * t + 3]
                    mlp_rest(turn * LOOP_BANKS + up.bank0, turn * 8 + 4 * (2 + t), t, 8)
                    mlp_add(turn * LOOP_BANKS + d0.bank0, 0)
                    mlp_add(turn * LOOP_BANKS + d1.bank0, 1)
            for i in range(2):
                mlp_add(downs[-2 + i].bank0, i)

            fill_lo("aux0", AUX_AT["p"], 2, turn=True)
            scaled_tokens("ln3")
            fill_lo("act", ACT_AT["ln3"], KD, turn=True, gain=LN3)
            n = 0
            for i, s in enumerate(by_name["ple_gate"]):
                for m in range(MT):
                    vec.wait_ge(proj_free, s.bank0 + m + 1)
                    g_ = ple_sig[:, n % 2, :]
                    xm = x[:, m, i * NCOL:(i + 1) * NCOL]
                    step(vec.tensor_tensor(g_, g_, ple_pp[:, m, i * NCOL:(i + 1) * NCOL], ALU.mult))
                    vec.tensor_tensor(xm, xm, g_, ALU.add).then_inc(ple_done, 1)
                    n += 1
            scales("ln_f", MT)
            for m in range(MT):
                vec.scalar_tensor_tensor(x[:, m, :], x[:, m, :], rstd[:, m:m + 1], ln_f_row, ALU.mult, ALU.mult)\
                   .then_inc(x_final, 1)
            vec.wait_ge(x_final, MT)
            scaled_tokens("pre0")
            fill_lo("act", ACT_AT["pre0"], KD, turn=True, gain=PRE)

            H = LSTM_HEADS
            vec.tensor_scalar(row["i"], bank(by_name["lstm_i"][0], 0)[0:H, :], lstm_b[:, 0:1], None, ALU.add).then_inc(proj_free, 1)
            vec.tensor_scalar(row["f"], bank(by_name["lstm_f"][0], 0)[0:H, :], lstm_b[:, 1:2], None, ALU.add)\
               .then_inc(lstm_f_ready, 1)
            vec.wait_ge(lstm_f_ready, 1)
            vec.tensor_scalar(row["min"], row["f"], 0.0, None, ALU.min).then_inc(proj_free, 1)
            step(vec.memset(lstm_reset, 1.0))
            step(vec.memset(lstm_reset.rearrange("p (c t) -> p c t", t=CHUNK)[:, :, 0:1], 0.0))
            step(vec.memset(lstm_m[:, 0:1], 0.0))
            vec.wait_ge(lstm_l1, 1)
            step(vec.tensor_tensor(row["min"], row["min"], row["l1"], ALU.subtract))
            step(vec.tensor_tensor_scan(row["b"], lstm_reset[0:H, :], row["min"], 0.0, ALU.mult, ALU.add))
            step(vec.tensor_tensor(row["a"], row["i"], row["b"], ALU.subtract))
            for c in range(NCH):
                t0, t1 = c * CHUNK, (c + 1) * CHUNK
                step(vec.tensor_tensor_scan(row["e"][:, t0:t1], row["a"][:, t0:t1], row["a"][:, t0:t1],
                                            lstm_m[:, c:c + 1], ALU.max, ALU.max))
                step(vec.tensor_tensor(lstm_m[:, c + 1:c + 2], row["b"][:, t1 - 1:t1], row["e"][:, t1 - 1:t1], ALU.add))

            def chunks(r):
                return row[r].rearrange("p (c t) -> p c t", t=CHUNK)

            e_last = chunks("e")[:, :, CHUNK - 1:CHUNK]
            vec.tensor_scalar(row["neg_e"], row["e"], -1.0, None, ALU.mult)
            vec.tensor_tensor(chunks("inter"), lstm_m[:, 0:NCH].unsqueeze(2).to_broadcast([H, NCH, CHUNK]), chunks("e"), ALU.subtract)
            vec.tensor_tensor(chunks("wa"), chunks("a"), e_last.to_broadcast([H, NCH, CHUNK]), ALU.subtract)
            vec.tensor_tensor(row["emt"], row["b"], row["e"], ALU.add)
            vec.tensor_tensor(lstm_dec[:], lstm_m[:, 0:NCH], e_last[:, :, 0], ALU.subtract).then_inc(lstm_rows, 1)
            for at, (dst, name) in enumerate(((lstm_q, "lstm_q"), (lstm_k, "lstm_k"))):
                for i, s in enumerate(by_name[name]):
                    for c in range(4):
                        u, o_ = bank(s, c), dst[:, 4 * i + c, :]
                        tap = [cols[:, CONV_AT + k * 16 + 8 * at + 4 * i + c:CONV_AT + k * 16 + 8 * at + 4 * i + c + 1]
                               for k in range(CONV)]
                        step(vec.tensor_scalar(o_, u, tap[CONV - 1], None, ALU.mult))
                        for back in range(1, CONV):
                            ins = vec.scalar_tensor_tensor(o_[:, back:], u[:, 0:SEQ - back], tap[CONV - 1 - back], o_[:, back:],
                                                           ALU.mult, ALU.add)
                            if back < CONV - 1:
                                step(ins)
                        ins.then_inc(proj_free, 1)
            vec.wait_ge(lstm_cols_full, 1)
            vec.tensor_copy(lstm_cols[:], work[:, 0, 0:48]).then_inc(lstm_cols_ready, 1)
            vec.wait_ge(lstm_cols_full, 2)
            vec.tensor_copy(decay[:], work[:, 1, 0:32]).then_inc(lstm_cols_ready, 1)
            vec.wait_ge(lstm_cols_ready, 2)
            va = lstm_v.rearrange("p m (h c) -> p m h c", h=H)
            step(vec.memset(va[:, :, :, LSTM_HD:LSTM_HD + 1], 1.0))
            for h in range(H):
                vec.wait_ge(neg_e_full, h + 1)
                vec.tensor_tensor(lstm_w[:, h % 2, :].rearrange("p (m t) -> p m t", m=MT),
                                  work[:, 1, :].rearrange("p (m t) -> p m t", m=MT),
                                  chunk_neg[:].unsqueeze(1).to_broadcast([P, MT, P]), ALU.add).then_inc(w_masked, 1)
                vec.wait_ge(qk_full, h + 1)
                vec.wait_ge(inter_full, h + 1)
                for kk in range(2):
                    q_ = lstm_q[:, 2 * h + kk, :]
                    ins = vec.tensor_tensor(q_, q_, work[:, 2, :], ALU.mult)
                ins.then_inc(q_inter, 1)
                for pair in range(2):
                    vec.wait_ge(lstm_kt_full, 2 * h + pair + 1)
                    for mm in range(2):
                        m = 2 * pair + mm
                        ins = vec.tensor_scalar(k_wa[:, m, h * LSTM_HD:(h + 1) * LSTM_HD],
                                                work[:, 3, mm * LSTM_HD:(mm + 1) * LSTM_HD],
                                                lstm_cols[:, 16 + m * 4 + h:16 + m * 4 + h + 1], LSTM_HD ** -0.5,
                                                ALU.mult, ALU.mult)
                    ins.then_inc(lstm_kt_ready, 1)
                vec.wait_ge(w_ready, h + 1)
                vec.scalar_tensor_tensor(lstm_s[:, h, :], work[:, 0, :], LSTM_HD ** -0.5, lstm_w[:, h % 2, :],
                                         ALU.mult, ALU.mult).then_inc(s_ready, 1)
            core = by_name["lstm_core"][0]
            for m in range(MT):
                for n in (2 * m, 2 * m + 1):
                    if n == NCH - 1:
                        continue
                    for hk in range(2 * H):
                        vec.wait_ge(lstm_upd_full, 8 * n + hk + 1)
                        c_ = lstm_c[:, hk, :]
                        upd = work[:, hk % 4, 0:LSTM_HD + 1]
                        if n == 0:
                            vec.tensor_copy(c_, upd).then_inc(lstm_c_ready, 1)
                        else:
                            vec.wait_ge(lstm_c_ready, 8 * (n - 1) + hk + 1)
                            d = (hk // 2) * NCH + n
                            vec.scalar_tensor_tensor(c_, c_, decay[:, d:d + 1], upd, ALU.mult, ALU.add).then_inc(lstm_c_ready, 1)
                for h in range(H):
                    vec.wait_ge(proj_full, core.bank0 + 4 * m + h + 1)
                    den = lstm_den[:, m * 4 + h:m * 4 + h + 1]
                    raw = proj[:, h, LSTM_HD:LSTM_HD + 1]
                    step(vec.scalar_tensor_tensor(den, raw, -1.0, lstm_cols[:, 32 + m * 4 + h:32 + m * 4 + h + 1],
                                                  ALU.mult, ALU.max))
                    step(vec.tensor_tensor(den, raw, den, ALU.max))
                    step(vec.reciprocal(den, den))
                    vec.tensor_scalar(lstm_h[:, m, h * LSTM_HD:(h + 1) * LSTM_HD], proj[:, h, 0:LSTM_HD], den, None, ALU.mult)\
                       .then_inc(proj_free, 1)
            n = 0
            for i, s in enumerate(by_name["lstm_o"]):
                for m in range(MT):
                    vec.wait_ge(proj_free, s.bank0 + m + 1)
                    h_ = lstm_h[:, m, i * NCOL:(i + 1) * NCOL]
                    vec.tensor_tensor(h_, h_, gate_tmp[:, n % 2, :], ALU.mult).then_inc(lstm_gated, 1)
                    n += 1
            scales("lstm", MT * H)
            n = 0
            for i, s in enumerate(by_name["lstm_z"]):
                for m in range(MT):
                    vec.wait_ge(proj_free, s.bank0 + m + 1)
                    for hh in range(2):
                        h = 2 * i + hh
                        h_ = lstm_h[:, m, h * LSTM_HD:(h + 1) * LSTM_HD]
                        ins = vec.scalar_tensor_tensor(h_, h_, rstd[:, m * 4 + h:m * 4 + h + 1],
                                                       gate_tmp[:, n % 2, hh * LSTM_HD:(hh + 1) * LSTM_HD], ALU.mult, ALU.mult)
                    ins.then_inc(ya_ready, 1)
                    n += 1
            fill_lo("aux", AUX_AT["ya"], KD, turn=True, gain=HN)

            for half in range(2):
                s = by_name["sb_q"][half]
                for h in range(4):
                    vec.tensor_scalar(sb_q[:, h, :], bank(s, h), HD ** -0.5, None, ALU.mult).then_inc(proj_free, 1)
                s = by_name["sb_k"][half]
                for h in range(4):
                    vec.tensor_copy(sb_k[:, h, :], bank(s, h)).then_inc(proj_free, 1)

                def terms(u):
                    nk = (u % 4 + 1) * P
                    z, l_, c_ = work[:, u % 2, 0:nk], sb_l[:, u % 2, 0:nk], sb_c[:, u % 2, 0:nk]
                    own = slice(nk - P, nk)
                    vec.wait_ge(sb_l1, u + 1)
                    step(vec.scalar_tensor_tensor(l_, z, 0.0, l_, ALU.max, ALU.add))
                    step(vec.tensor_tensor(l_[:, own], l_[:, own], before_ok[:], ALU.mult))
                    if u >= 2:
                        vec.wait_ge(sb_at_full, u - 1)
                    ones = one_col[:, 0:1].to_broadcast([P, nk])
                    step(vec.tensor_tensor_scan(c_[:, ::-1], ones, l_[:, ::-1], 0.0, ALU.mult, ALU.add))
                    step(vec.tensor_tensor(c_, z, c_, ALU.subtract))
                    vec.tensor_tensor(c_[:, own], c_[:, own], before_neg[:], ALU.add).then_inc(sb_t, 1)

                def values_out(u):
                    h, blk = 4 * (u // 16) + (u % 16) // 4, u % 4
                    vec.wait_ge(sb_o_full, u + 1)
                    vec.tensor_copy(sb_o[:, blk, h * HD:(h + 1) * HD], work[:, 3, 0:HD]).then_inc(sb_o_copied, 1)

                u0 = 16 * half
                for u in range(u0, u0 + 16):
                    terms(u)
                    if u > u0:
                        values_out(u - 1)
                values_out(u0 + 15)
            vec.wait_ge(sb_o_copied, 32)
            n = 0
            for i, s in enumerate(by_name["sb_z"]):
                for m in range(MT):
                    vec.wait_ge(proj_free, s.bank0 + m + 1)
                    o_ = sb_o[:, m, i * NCOL:(i + 1) * NCOL]
                    vec.tensor_tensor(o_, o_, gate_tmp[:, n % 2, :], ALU.mult).then_inc(yb_ready, 1)
                    n += 1

            def layer_out(name, first, second):
                for i, s in enumerate(by_name[first]):
                    for m in range(MT):
                        vec.tensor_copy(y[:, m, i * NCOL:(i + 1) * NCOL], bank(s, m)).then_inc(proj_free, 1)
                if name == "post0":
                    fill_lo("act", ACT_AT["yb"], KD, turn=True)
                else:
                    fill_lo("aux", AUX_AT["mixb"], KD, src=odd_z[:, KD:2 * KD, :])
                vec.wait_ge(proj_free, end(first))
                for i, s in enumerate(by_name[second]):
                    for m in range(MT):
                        ym = y[:, m, i * NCOL:(i + 1) * NCOL]
                        vec.tensor_tensor(ym, ym, bank(s, m), ALU.add).then_inc(proj_free, 1)
                scales(name, MT)
                vec.wait_ge(post_loaded, 32)
                for m in range(MT):
                    step(vec.scalar_tensor_tensor(y[:, m, :], y[:, m, :], rstd[:, m:m + 1],
                                                  post_row[0 if name == "post0" else 1], ALU.mult, ALU.mult))
                    vec.tensor_tensor(x[:, m, :], x[:, m, :], y[:, m, :], ALU.add).then_inc(x_final, 1)

            layer_out("post0", "even_out0", "even_out1")
            vec.wait_ge(x_final, 2 * MT)
            scaled_tokens("pre1")
            fill_lo("act", ACT_AT["pre1"], KD, turn=True, gain=PRE + 8)

            step(vec.memset(pool_raw[:, :, 0:POOL_PAD], 0.0))
            step(vec.memset(pool_sum[:, :, 0:POOL_PAD], 0.0))
            n = 0

            def pool_lo_of(n):
                vec.wait_ge(aux_hi_ready, AUX_AT["pool"] + n + 1)
                hi, lo = aux(n % 8)
                vec.tensor_tensor(lo, pooled[:, n % 2, :], hi.bitcast(F32), ALU.subtract).then_inc(aux_ready, 1)

            def pool_mixed(g):
                s = by_name["pool_mix"][g]
                for c in range(4):
                    t = odd_z[:, 4 * g + c, :]
                    vec.scalar_tensor_tensor(t, bank(s, c), cols[:, PS + 4 * g + c:PS + 4 * g + c + 1], t,
                                             ALU.mult, ALU.mult).then_inc(proj_free, 1)

            for g, s in enumerate(by_name["pool_in"]):
                w = POOL_WINDOWS[g]
                for c in range(4):
                    vec.wait_ge(proj_free, s.bank0 + c + 1)
                    raw = src = pool_raw[:, n % 2, :]
                    back, level = 1, 0
                    while back < w:
                        dst = pool_sum[:, level % 2, :]
                        step(vec.tensor_tensor(dst[:, POOL_PAD:], src[:, POOL_PAD:], src[:, POOL_PAD - back:PADDED - back], ALU.add))
                        src, back, level = dst, 2 * back, level + 1
                    first = src[:, POOL_PAD:2 * POOL_PAD]
                    step(vec.tensor_tensor(first, first, edges[:, g, :], ALU.mult))
                    vec.scalar_tensor_tensor(pooled[:, n % 2, :], src[:, POOL_PAD:], 1.0 / w, raw[:, POOL_PAD:],
                                             ALU.mult, ALU.subtract).then_inc(pool_done, 1)
                    vec.wait_ge(pool_done, n + 1)
                    if n:
                        pool_lo_of(n - 1)
                    n += 1
                if g == 3:
                    pool_lo_of(n - 1)
                if g:
                    pool_mixed(g - 1)
            pool_mixed(3)
            fill_lo("act", ACT_AT["mixa"], KD, src=odd_z)
            layer_out("post1", "odd_out0", "odd_out1")

        @block.tensor
        def _(pe):
            def three(out_, a_hi, a_lo, b_hi, b_lo, first, last):
                pe.matmul(out_, a_hi, b_hi, start=first, stop=False)
                pe.matmul(out_, a_hi, b_lo, start=False, stop=False)
                return pe.matmul(out_, a_lo, b_hi, start=False, stop=last)

            def natural(m):
                return slice(m * P, (m + 1) * P)

            def by_stride(z):
                return slice(z, SEQ, 4)

            def slab_block(s, j, kind, pair, k, tokens, wait_bank):
                slot = (s.first + j) % RING
                hi, lo = tile_of(pair)(k)
                wh, wl = w_hi[:, slot, :], w_lo[:, slot, :]
                for c in range(4):
                    if j == 0:
                        wait_bank(c)
                    f = slice(c * P, (c + 1) * P)
                    t = tokens(c)
                    a, b = ((hi[:, t], lo[:, t]), (wh, wl)) if kind == "tokens" else ((wh[:, f], wl[:, f]), (hi, lo))
                    ins = three(proj[:, c, :], *a, *b, j == 0, j == s.n - 1)
                    if j == s.n - 1:
                        ins.then_inc(proj_full, 1)
                ins if j == s.n - 1 else ins.then_inc(block_used, 1)

            def slab(s, kind, pair="act", ready=None, tokens=natural, k0=0):
                for j in range(s.n):
                    pe.wait_ge(lo_ready, s.first + j + 1)
                    if ready:
                        pe.wait_ge(ready[0], ready[1] + k0 + j + 1)

                    def wait_bank(c):
                        if s.need[c]:
                            pe.wait_ge(proj_free, s.need[c])

                    slab_block(s, j, kind, pair, k0 + j, tokens, wait_bank)

            def slabs_of(name, kind, pair="act", ready=None):
                ss = by_name[name]
                s0 = ss[0]
                assert s0.n == RING
                if slabs[s0.at - 1].banks != 4:
                    pe.wait_ge(proj_free, s0.bank0)
                if ready:
                    pe.wait_ge(ready[0], ready[1] + KD)
                with pe.Fori(0, len(ss)) as i:
                    for j in range(s0.n):
                        pe.wait_ge(lo_ready, i * s0.n + (s0.first + j + 1))
                        slab_block(s0, j, kind, pair, j, natural,
                                   lambda c: pe.wait_ge(proj_free, i * 4 + (s0.bank0 + c - 3)))

            def narrow_slab(s, phys, ready=None):
                for j in range(s.n):
                    pe.wait_ge(lo_ready, s.first + j + 1)
                    if j == 0 and s.need[0]:
                        pe.wait_ge(proj_free, s.need[0])
                    slot = (s.first + j) % RING
                    for kk in range(4):
                        k = 4 * j + kk
                        if ready:
                            pe.wait_ge(ready[0], ready[1] + k + 1)
                        f = slice(kk * P, (kk + 1) * P)
                        ins = three(proj[:, phys, :], w_hi[:, slot, f], w_lo[:, slot, f], act_hi[:, k, :], act_lo[:, k, :],
                                    k == 0, k == KD - 1)
                    ins.then_inc(proj_full if j == s.n - 1 else block_used, 1)

            def turn(src, n, ready_sem, base, m_ready):
                m_ready()
                for k in range(n):
                    if k >= 4:
                        pe.wait_ge(ready_sem, base + k - 3)
                    for m in range(MT):
                        ins = pe.transpose(work[:, k % 4, m * P:(m + 1) * P], src[:, m, k * P:(k + 1) * P], ident[:])
                    ins.then_inc(turned, 1)

            def turn_norm(name):
                turn(xs, KD, act_ready, ACT_AT[name], lambda: pe.wait_ge(scaled, MT * (NORM[name] + 1)))

            def ready_act(name):
                return act_ready, ACT_AT[name]

            pe.wait_ge(consts_ready, 1)
            pe.wait_ge(params_loaded, 16 * 15)
            pe.transpose(work[:, 0, 0:CONV_AT], rows1[0:CONV_AT, :], ident[0:CONV_AT, 0:CONV_AT])
            pe.transpose(work[:, 0, P:P + 64], rows2[0:64, :], ident[0:64, 0:64]).then_inc(cols_full, 1)
            pe.wait_ge(rel_ready, 1)
            for n in range(12):
                g, h = n // 4, n % 4
                if n >= 3:
                    pe.wait_ge(diag_copied, n - 2)
                pe.matmul(work[:, 1 + n % 3, 0:DIAG[g]], rel_wide[0:REL_BUCKETS + 1, 4 * g + h, :],
                          one_hot[0:REL_BUCKETS + 1, DIAG_AT[g]:DIAG_AT[g] + DIAG[g]], start=True, stop=True)\
                  .then_inc(diag_full, 1)
            pe.wait_ge(cols_ready, 1)
            pe.wait_ge(diag_copied, 12)
            turn_norm("ln1")

            narrow_slab(by_name["gla_a"][0], 0, ready=ready_act("ln1"))
            pe.wait_ge(proj_free, 1)
            for h in range(GLA_HEADS):
                pe.matmul(work[:, h, :], w_a2[0:GLA_RANK, h * P:(h + 1) * P], gla_a[0:GLA_RANK, :], start=True, stop=True)\
                  .then_inc(gate_full, 1)
            slab(by_name["gla_q"][0], "features")
            slab(by_name["gla_k"][0], "features")
            slabs_of("gla_v", "tokens")
            for h in range(GLA_HEADS):
                pe.wait_ge(proj_free, by_name["gla_k"][0].bank0 + h + 1)
                for m in range(MT):
                    ins = pe.transpose(work[:, h, m * P:(m + 1) * P], k_out[:, h, m * P:(m + 1) * P], ident[:])
                ins.then_inc(ktok_full, 1)
            for h in range(GLA_HEADS):
                pe.wait_ge(ktok_ready, h + 1)
                for m in range(MT):
                    t = natural(m)
                    ins = pe.matmul(work[:, h, t], k_in[:, h, t], q_dec[:, h, t], start=True, stop=True)
                ins.then_inc(gla_att_full, 1)
            pe.wait_ge(proj_free, end("gla_v"))
            pe.wait_ge(gla_att_ready, GLA_HEADS)
            for m in range(MT):
                if m:
                    pe.wait_ge(gla_o_copied, 2 * m)
                for h in range(GLA_HEADS):
                    pe.matmul(work[:, h // 2, (h % 2) * GLA_DV:(h % 2 + 1) * GLA_DV], gla_att[:, h, natural(m)],
                              gla_v[:, m, h * GLA_DV:(h + 1) * GLA_DV], start=(h % 2 == 0), stop=False, skip_group_check=True)
                for half in range(2):
                    n = 2 * m + half
                    rows = slice(half * CHUNK, (half + 1) * CHUNK)
                    if n < NCH - 1:
                        for h in range(GLA_HEADS):
                            if n and h % 2 == 0:
                                pe.wait_ge(gla_state_ready, 4 * (n - 1) + h + 2)
                            ins = pe.matmul(work[:, 2 + h // 2, (h % 2) * GLA_DV:(h % 2 + 1) * GLA_DV],
                                            k_tok[rows, h, natural(m)], gla_v[rows, m, h * GLA_DV:(h + 1) * GLA_DV],
                                            start=True, stop=True)
                            if h % 2:
                                ins.then_inc(gla_upd_full, 1)
                    for h in range(GLA_HEADS):
                        if n:
                            pe.wait_ge(gla_state_ready, 4 * (n - 1) + h + 1)
                            ins = pe.matmul(work[rows, h // 2, (h % 2) * GLA_DV:(h % 2 + 1) * GLA_DV],
                                            q_dec[:, h, n * CHUNK:(n + 1) * CHUNK], gla_state[:, n % 2, h, :],
                                            start=False, stop=(half == 1), skip_group_check=True)
                            if half and h % 2:
                                ins.then_inc(gla_o_full, 1)
            slabs_of("gla_r", "tokens")

            pe.wait_ge(gla_o_copied, 2 * MT)
            pe.wait_ge(gla_state_ready, 4 * (NCH - 1))
            for g in range(3):
                slab(by_name[f"att_q{g}"][0], "features")
                sk = by_name[f"att_k{g}"][0]
                slab(sk, "features")
                if g:
                    pe.wait_ge(biased, 4 * g)
                for h in range(ATT_HEADS):
                    pe.wait_ge(proj_free, sk.bank0 + h + 1)
                    if g == 0 and h >= 2:
                        pe.wait_ge(biased, h - 1)
                    for z in range(4):
                        q_ = att_q[:, h, natural(z)]
                        if g == 0:
                            k0 = max(z - 1, 0) * P
                            n_ = P if z == 0 else 2 * P
                            o_ = work[:, 2 * (h % 2) + z // 2, (z % 2) * 2 * P:(z % 2) * 2 * P + n_]
                            ins = pe.matmul(o_, q_, att_k[:, h, k0:k0 + n_], start=True, stop=True)
                        else:
                            ins = pe.matmul(work[:, h, natural(z)], q_, att_k[:, h, natural(z)], start=True, stop=True)
                    ins.then_inc(logits_full, 1)
            slab(by_name["att_v0"][0], "tokens")
            pe.wait_ge(lse_ready, 1)
            pe.wait_ge(biased, 12)
            for g in range(3):
                for z in range(4):
                    c = (g * 4 + z) * 4
                    ins = pe.transpose(work[0:4, g, natural(z)], att_tmp[:, c:c + 4], ident[:])
                ins.then_inc(lse_full, 1)
            slab(by_name["att_v1"][0], "tokens", tokens=by_stride)
            pe.wait_ge(share_ready, 1)
            for g in range(3):
                for z in range(4):
                    c = (g * 4 + z) * 4
                    t = natural(z) if g == 0 else by_stride(z)
                    ins = pe.transpose(work[:, 3, c:c + 4], lse_rows[0:4, g, t], ident[0:4, 0:4])
            ins.then_inc(share_full, 1)
            slab(by_name["att_v2"][0], "tokens", tokens=by_stride)
            pairs = [(z, kb) for z in range(4) for kb in ((z - 1, z) if z else (0,))]

            def probs_turned(u):
                h, g = u // 3, u % 3
                pe.wait_ge(p_scaled, u + 1)
                if g == 0:
                    if h:
                        pe.wait_ge(pt_copied[2], h)
                    for at, (z, kb) in enumerate(pairs):
                        k0 = z * KEYS[0] + (0 if kb < z else P)
                        ins = pe.transpose(work[:, at // 4, (at % 4) * P:(at % 4 + 1) * P], att_p[0][:, h, k0:k0 + P], ident[:])
                else:
                    if g == 2:
                        pe.wait_ge(pt_copied[0], 2 * h + 2)
                    elif h:
                        pe.wait_ge(pt_copied[1], h)
                    for z in range(4):
                        ins = pe.transpose(work[:, 2 if g == 1 else 0, natural(z)], att_p[g][:, h, natural(z)], ident[:])
                ins.then_inc(pt_full, 1)

            def values_weighted(u):
                h, g = u // 3, u % 3
                if g == 0 and h:
                    pe.wait_ge(att_o_copied, h)
                pe.wait_ge(pt_copied[g], 2 * h + 2 if g == 0 else h + 1)
                todo = [(at, kb, natural(z)) for at, (z, kb) in enumerate(pairs)] if g == 0 else \
                       [(z, z, by_stride(z)) for z in range(4)]
                for n, (at, kb, t) in enumerate(todo):
                    ins = pe.matmul(work[:, 3, t], att_v[g][:, kb, h * HD:(h + 1) * HD], att_pt[g][:, at * P:(at + 1) * P],
                                    start=(g == 0 and n == 0), stop=(g == 2 and n == 3), skip_group_check=True)
                ins.then_inc(pv_done, 1)

            pe.wait_ge(proj_free, end("att_v2"))
            probs_turned(0)
            for u in range(12):
                if u + 1 < 12:
                    probs_turned(u + 1)
                values_weighted(u)
            slabs_of("mix_gate", "features")
            turn(gla_o, KD, act_ready, ACT_AT["gla"], lambda: (pe.wait_ge(gla_gated, 2 * MT), pe.wait_ge(att_o_copied, 4)))
            slabs_of("gla_out", "features", ready=ready_act("gla"))
            for s in by_name["att_out"]:
                slab(s, "features", pair="aux0", ready=(aux_ready, AUX_AT["att"]))
            s = by_name["mix_out"][0]
            slab(s, "tokens", ready=ready_act("mix"))
            slab(by_name["mix_out"][1], "tokens")

            turn_norm("ln2")
            ups, downs = by_name["mlp_up"], by_name["mlp_down"]

            def down_pair(g):
                for i in range(2):
                    slab(downs[2 * g + i], "tokens", pair=f"aux{g % 2}", ready=(aux_ready, AUX_AT["mlp"] + 4 * g))

            slab(ups[0], "features", ready=ready_act("ln2"))
            slab(ups[1], "features")
            down_pair(0)
            with pe.Fori(0, LOOP_TURNS) as i:
                for at, s in enumerate(LOOP_SLABS):
                    t = at // 3
                    for j in range(s.n):
                        pe.wait_ge(lo_ready, i * LOOP_BLOCKS + (s.first + j + 1))
                        if at % 3:
                            pe.wait_ge(aux_ready, i * 8 + (AUX_AT["mlp"] + 4 * (1 + t) + j + 1))
                        slab_block(s, j, "tokens" if at % 3 else "features", f"aux{(1 + t) % 2}" if at % 3 else "act", j,
                                   natural, lambda c: pe.wait_ge(proj_free, i * LOOP_BANKS + s.need[c]))
            down_pair(D_FF // NCOL - 1)

            turn(ple_in, 2, aux_ready, AUX_AT["p"], lambda: pe.wait_ge(ple_loaded, 32))
            for s in by_name["ple_p"]:
                slab(s, "tokens", pair="aux0", ready=(aux_ready, AUX_AT["p"]))
            pe.wait_ge(aux_ready, AUX_AT["p"] + 2)
            turn_norm("ln3")
            slabs_of("ple_gate", "tokens", ready=ready_act("ln3"))

            turn_norm("pre0")
            narrow_slab(by_name["lstm_i"][0], 0, ready=ready_act("pre0"))
            narrow_slab(by_name["lstm_f"][0], 1)
            H = LSTM_HEADS
            slabs_of("lstm_q", "features")
            pe.wait_ge(lstm_exps, 4)
            pe.wait_ge(act_ready, ACT_AT["pre0"] + KD)
            for at, r in enumerate(("a", "wa", "emt")):
                for m in range(MT):
                    ins = pe.transpose(work[:, 0, 16 * at + 4 * m:16 * at + 4 * m + 4], row[r][:, natural(m)], ident[0:H, 0:H])
            ins.then_inc(lstm_cols_full, 1)
            for h in range(H):
                ins = pe.matmul(work[:, 1, h * NCH:(h + 1) * NCH], sel[:, h, :], lstm_dec[:], start=True, stop=True)
            ins.then_inc(lstm_cols_full, 1)
            slabs_of("lstm_k", "features")
            slabs_of("lstm_v", "tokens")
            pe.wait_ge(lstm_cols_ready, 2)
            for h in range(H):
                pe.wait_ge(conv_silu, 8 + 2 * h + 2)
                if h:
                    pe.wait_ge(s_ready, h)
                for m in range(MT):
                    for kk in range(2):
                        ins = pe.matmul(work[:, 0, natural(m)], lstm_k[:, 2 * h + kk, natural(m)], lstm_q[:, 2 * h + kk, natural(m)],
                                        start=(kk == 0), stop=(kk == 1))
                ins.then_inc(qk_full, 1)
                if h:
                    pe.wait_ge(w_masked, h)
                pe.matmul(work[:, 1, :], sel[:, h, :], row["neg_e"], start=True, stop=True).then_inc(neg_e_full, 1)
                if h:
                    pe.wait_ge(q_inter, h)
                pe.matmul(work[:, 2, :], sel[:, h, :], row["inter"], start=True, stop=True).then_inc(inter_full, 1)
                for pair in range(2):
                    if h or pair:
                        pe.wait_ge(lstm_kt_ready, 2 * h + pair)
                    for mm in range(2):
                        for kk in range(2):
                            at = mm * LSTM_HD + kk * P
                            ins = pe.transpose(work[:, 3, at:at + P], lstm_k[:, 2 * h + kk, natural(2 * pair + mm)], ident[:])
                    ins.then_inc(lstm_kt_full, 1)
            core = by_name["lstm_core"][0]
            va = lstm_v.rearrange("p m (h c) -> p m h c", h=H)
            pe.wait_ge(proj_free, end("lstm_v"))
            pe.wait_ge(s_ready, H)
            pe.wait_ge(lstm_kt_ready, 2 * H)
            for m in range(MT):
                for h in range(H):
                    if m:
                        pe.wait_ge(proj_free, core.need[4 * m + h])
                    pe.matmul(proj[:, h, 0:LSTM_HD + 1], lstm_s[:, h, natural(m)], va[:, m, h, :], start=True, stop=False,
                              skip_group_check=True)
                for half in range(2):
                    n = 2 * m + half
                    rows = slice(half * CHUNK, (half + 1) * CHUNK)
                    for h in range(H):
                        if n:
                            pe.wait_ge(lstm_c_ready, 8 * (n - 1) + 2 * h + 2)
                            for kk in range(2):
                                ins = pe.matmul(proj[rows, h, 0:LSTM_HD + 1], lstm_q[:, 2 * h + kk, n * CHUNK:(n + 1) * CHUNK],
                                                lstm_c[:, 2 * h + kk, :], start=False, stop=(half == 1 and kk == 1),
                                                skip_group_check=True)
                            if half:
                                ins.then_inc(proj_full, 1)
                        if n < NCH - 1:
                            for kk in range(2):
                                hk = 2 * h + kk
                                if 8 * n + hk >= 4:
                                    pe.wait_ge(lstm_c_ready, 8 * n + hk - 3)
                                pe.matmul(work[:, hk % 4, 0:LSTM_HD + 1], k_wa[rows, m, h * LSTM_HD + kk * P:h * LSTM_HD + (kk + 1) * P],
                                          va[rows, m, h, :], start=True, stop=True).then_inc(lstm_upd_full, 1)
            slabs_of("lstm_o", "tokens")
            slabs_of("lstm_z", "tokens")
            turn(lstm_h, KD, aux_ready, AUX_AT["ya"], lambda: (pe.wait_ge(ya_ready, 2 * MT), pe.wait_ge(lstm_c_ready, 8 * (NCH - 1))))

            for half in range(2):
                slab(by_name["sb_q"][half], "features")
                slab(by_name["sb_k"][half], "features")
                slab(by_name["sb_v"][half], "tokens")
                pe.wait_ge(proj_free, by_name["sb_v"][half].end)
                if half == 0:
                    pe.wait_ge(aux_ready, AUX_AT["ya"] + KD)

                def scores(u):
                    h, nk = (u % 16) // 4, (u % 4 + 1) * P
                    if u >= 2:
                        pe.wait_ge(sb_t, u - 1)
                    pe.matmul(work[:, u % 2, 0:nk], sb_q[:, h, natural(u % 4)], sb_k[:, h, 0:nk], start=True, stop=True)\
                      .then_inc(sb_z_full, 1)

                def values(u):
                    h, n_ = (u % 16) // 4, u % 4 + 1
                    pe.wait_ge(sb_a, u + 1)
                    if u:
                        pe.wait_ge(sb_at_ready, u)
                    for kb in range(n_):
                        ins = pe.transpose(work[:, 2, natural(kb)], sb_c[:, u % 2, natural(kb)], ident[:])
                    ins.then_inc(sb_at_full, 1)
                    pe.wait_ge(sb_at_ready, u + 1)
                    if u:
                        pe.wait_ge(sb_o_copied, u)
                    for kb in range(n_):
                        ins = pe.matmul(work[:, 3, 0:HD], sb_at[:, u % 2, natural(kb)], sb_v[:, kb, h * HD:(h + 1) * HD],
                                        start=(kb == 0), stop=(kb == n_ - 1))
                    ins.then_inc(sb_o_full, 1)

                u0 = 16 * half
                for u in range(u0, u0 + 16):
                    scores(u)
                    if u > u0:
                        values(u - 1)
                values(u0 + 15)
            slabs_of("sb_z", "tokens")
            for i, s in enumerate(by_name["even_out0"]):
                slab(s, "tokens", pair="aux", ready=(aux_ready, AUX_AT["ya"]))
            turn(sb_o, KD, act_ready, ACT_AT["yb"], lambda: (pe.wait_ge(yb_ready, 2 * MT), pe.wait_ge(sb_o_copied, 32)))
            slabs_of("even_out1", "tokens", ready=ready_act("yb"))

            turn_norm("pre1")
            slabs_of("odd_z", "features", ready=ready_act("pre1"))
            ins_, mixes = by_name["pool_in"], by_name["pool_mix"]
            slab(ins_[0], "features")
            for g in range(len(POOL_WINDOWS)):
                if g + 1 < len(POOL_WINDOWS):
                    slab(ins_[g + 1], "features")
                slab(mixes[g], "features", pair=f"aux{g % 2}", ready=(aux_ready, AUX_AT["pool"] + 4 * g))
            slabs_of("odd_out0", "tokens", ready=ready_act("mixa"))
            for s in by_name["odd_out1"]:
                slab(s, "tokens", pair="aux", ready=(aux_ready, AUX_AT["mixb"]))


_INS = ["x", "p", "ln1", "w_in", "w_a2", "b_a", "gla_gn", "w_o_gla", "w_o_attn", "w_out", "ln2", "w_mlp1", "w_mlp2",
        "ln3", "w_pp", "w_pg", "rel_bias", "ln_f", "pre_norm_g_2", "post_norm_g_2", "w_in_ab_2", "conv_qk_2",
        "bias_i_2", "bias_f_2", "head_norm_g_2", "w_out_ab_2", "w_in_c_2", "pool_w_2", "pool_scale_2", "w_out_c_2"]
_FLAT = {"w_in": (D, -1), "w_a2": (GLA_RANK, -1), "w_o_gla": (D, D), "w_o_attn": (-1, D), "w_out": (D, D),
         "w_mlp1": (D, D_FF), "w_mlp2": (D_FF, D), "w_pp": (PLE, D), "w_pg": (D, D), "w_in_ab_2": (D, -1),
         "w_out_ab_2": (2 * D, D), "w_in_c_2": (D, 2 * C_WIDTH), "pool_w_2": (C_WIDTH, -1), "w_out_c_2": (C_WIDTH, D),
         "conv_qk_2": (CONV, 2 * D)}


def kernel(**inputs):
    import concourse.bacc as bacc
    from concourse.bass_utils import run_bass_kernel_spmd

    nc = bacc.Bacc("TRN2", target_bir_lowering=False, num_devices=1)
    arrays, aps = {}, {}

    def give(name, a):
        arrays[f"in_{name}"] = a
        aps[name] = nc.dram_tensor(f"in_{name}", a.shape, mybir.dt.from_np(a.dtype), kind="ExternalInput").ap()

    for name in _INS:
        a = np.ascontiguousarray(inputs[name])
        give(name, a.reshape(_FLAT[name]) if name in _FLAT else a)
    give("bucket_one_hot", bucket_one_hot())
    give("pool_edges", pool_edges())
    out = nc.dram_tensor("out", (1, SEQ, D), F32, kind="ExternalOutput").ap()
    two_blocks(nc, aps, out)
    r = run_bass_kernel_spmd(nc, [arrays], core_ids=[0])
    return r.results[0]["out"]
```

```python
from contextlib import ExitStack

import numpy as np

import concourse.bass as bass
from concourse import mybir

F32 = mybir.dt.float32
F32R = mybir.dt.float32r
U32 = mybir.dt.uint32
ACT = mybir.ActivationFunctionType
ALU = mybir.AluOpType
AX = mybir.AxisListType.X

P = 128
SEQ = 512
MT = SEQ // P
D = 1024
KD = D // P
NCOL = 512
RING = 8
EPS = 1e-6
NEG = -1e30

GLA_HEADS, GLA_DK, GLA_DV, GLA_RANK, GLA_TAU, CHUNK = 4, 128, 256, 16, 16.0, 64
NCH = SEQ // CHUNK
ATT_HEADS, HD = 4, 128
ATT_GROUPS = ((128, 1), (512, 4), (2048, 16))
REL_BUCKETS, REL_MAX_DIST = 32, 2048
D_FF, PLE = 4 * D, 256
LSTM_HEADS, LSTM_HD, CONV = 4, 256, 4
SB_HEADS = 8
POOL_WINDOWS = (2, 4, 8, 16)
POOL_PAD = 16
C_WIDTH = 2 * D

DIAG = (3 * P - 1, 2 * P - 1, 2 * P - 1)
DIAG_AT = (0, DIAG[0], DIAG[0] + DIAG[1])
KEYS = (2 * P, P, P)


def bucket_one_hot():
    out = np.zeros((REL_BUCKETS + 1, sum(DIAG)), np.float32)
    half = REL_BUCKETS // 2
    for g, (window, dil) in enumerate(ATT_GROUPS):
        for e in range(DIAG[g]):
            steps = (2 * P - 1 - e) if g == 0 else (P - 1 - e)
            ok = 0 <= steps <= P if g < 2 else steps >= 0 and steps % 4 == 0
            row = REL_BUCKETS
            if ok:
                dist = steps * (1 if g == 0 else 4)
                far = half + int(np.int32(
                    np.log(np.float32(max(dist, 1)) / half) / np.log(REL_MAX_DIST / half) * (REL_BUCKETS - half)))
                row = dist if dist < half else min(far, REL_BUCKETS - 1)
            out[row, DIAG_AT[g] + e] = 1.0
    return out


def pool_edges():
    t = np.arange(POOL_PAD) + 1
    return np.stack([w / np.minimum(t, w) for w in POOL_WINDOWS]).astype(np.float32)


class Slab:

    def __init__(self, name, sources, banks):
        self.name, self.sources, self.banks = name, sources, banks
        self.n = len(sources)

    def phys(self, c):
        return 1 if self.name == "lstm_f" else c % 4


def plan_slabs(W):
    slabs = []

    def slab(name, w, col, row=0, rows=D, banks=MT):
        slabs.append(Slab(name, [w[row + k * P:row + (k + 1) * P, col:col + NCOL] for k in range(rows // P)], banks))

    def narrow(w, col):
        return [w[b * 512:(b + 1) * 512, col:col + P].rearrange("(k p) c -> p k c", p=P) for b in range(2)]

    w_in, w_ab, w_c = W["w_in"], W["w_in_ab_2"], W["w_in_c_2"]
    qk, dv = GLA_HEADS * GLA_DK, GLA_HEADS * GLA_DV
    at_a = 2 * qk + 2 * dv
    at_att = at_a + GLA_RANK
    at_gate = at_att + len(ATT_GROUPS) * 3 * ATT_HEADS * HD
    slabs.append(Slab("gla_a", narrow(w_in, at_a), 1))
    slab("gla_q", w_in, 0)
    slab("gla_k", w_in, qk)
    for i in range(2):
        slab("gla_v", w_in, 2 * qk + i * NCOL)
    for i in range(2):
        slab("gla_r", w_in, 2 * qk + dv + i * NCOL)
    for g in range(len(ATT_GROUPS)):
        for which in range(2):
            slab(f"att_{'qk'[which]}{g}", w_in, at_att + (3 * g + which) * NCOL)
    for g in range(len(ATT_GROUPS)):
        slab(f"att_v{g}", w_in, at_att + (3 * g + 2) * NCOL)
    for i in range(4):
        slab("mix_gate", w_in, at_gate + i * NCOL)
    for i in range(2):
        slab("gla_out", W["w_o_gla"], i * NCOL)
    for i in range(2):
        slab("att_out", W["w_o_attn"], i * NCOL, rows=ATT_HEADS * HD)
    for i in range(2):
        slab("mix_out", W["w_out"], i * NCOL)

    def up(g):
        slab("mlp_up", W["w_mlp1"], g * NCOL)

    def down(g):
        for i in range(2):
            slab("mlp_down", W["w_mlp2"], i * NCOL, row=g * NCOL, rows=NCOL)

    up(0)
    for g in range(1, D_FF // NCOL):
        up(g)
        down(g - 1)
    down(D_FF // NCOL - 1)
    for i in range(2):
        slab("ple_p", W["w_pp"], i * NCOL, rows=PLE)
    for i in range(2):
        slab("ple_gate", W["w_pg"], i * NCOL)

    at_if = 5 * D
    at_b = at_if + 2 * LSTM_HEADS
    slabs.append(Slab("lstm_i", narrow(w_ab, at_if), 1))
    slabs.append(Slab("lstm_f", narrow(w_ab, at_if + LSTM_HEADS), 1))
    for at, name in enumerate(("lstm_q", "lstm_k", "lstm_v")):
        for i in range(2):
            slab(name, w_ab, at * D + i * NCOL)
    slabs.append(Slab("lstm_core", [], MT * LSTM_HEADS))
    for at, name in enumerate(("lstm_o", "lstm_z")):
        for i in range(2):
            slab(name, w_ab, (3 + at) * D + i * NCOL)
    for half in range(2):
        for at, name in enumerate(("sb_q", "sb_k", "sb_v")):
            slab(name, w_ab, at_b + at * D + half * NCOL)
    for i in range(2):
        slab("sb_z", w_ab, at_b + 3 * D + i * NCOL)
        slab("even_out0", W["w_out_ab_2"], i * NCOL)
    for i in range(2):
        slab("even_out1", W["w_out_ab_2"], i * NCOL, row=D)

    for i in range(4):
        slab("odd_z", w_c, C_WIDTH + i * NCOL)

    def pool_in(g):
        slab("pool_in", w_c, g * NCOL)

    def pool_mix(g):
        slab("pool_mix", W["pool_w_2"], 0, row=g * NCOL, rows=NCOL)

    pool_in(0)
    for g in range(1, len(POOL_WINDOWS)):
        pool_in(g)
        pool_mix(g - 1)
    pool_mix(len(POOL_WINDOWS) - 1)
    for half in range(2):
        for i in range(2):
            slab(f"odd_out{half}", W["w_out_c_2"], i * NCOL, row=half * D)

    first = bank0 = used0 = 0
    filled = [0] * 4
    for at, s in enumerate(slabs):
        s.at, s.first, s.bank0, s.used0, s.end = at, first, bank0, used0, bank0 + s.banks
        s.need = []
        for c in range(s.banks):
            b = 1 if s.name == "lstm_f" else c % 4
            s.need.append(filled[b])
            filled[b] = bank0 + c + 1
        first += s.n
        bank0 += s.banks
        used0 += max(s.n - 1, 0)
    return slabs


def two_blocks(nc, W, out):
    slabs = plan_slabs(W)
    by_name = {}
    for s in slabs:
        by_name.setdefault(s.name, []).append(s)
    blocks = [(s, j) for s in slabs for j in range(s.n)]
    n_blocks = len(blocks)

    ctx = ExitStack()
    with ctx:
        def sb(name, shape, dt=F32):
            return ctx.enter_context(nc.sbuf_tensor(name, shape, dt))

        def sem(name):
            return ctx.enter_context(nc.semaphore(name))

        w_raw = sb("w_raw", [P, RING, NCOL])
        w_hi = sb("w_hi", [P, RING, NCOL], F32R)
        w_lo = sb("w_lo", [P, RING, NCOL], F32R)
        act_hi = sb("act_hi", [P, KD, SEQ], F32R)
        act_lo = sb("act_lo", [P, KD, SEQ], F32R)
        aux0_hi = sb("aux0_hi", [P, 4, SEQ], F32R)
        aux0_lo = sb("aux0_lo", [P, 4, SEQ], F32R)
        x = sb("x", [P, MT, D])
        ARENA = 22560
        arena_at = nc.sbuf_base
        arena = sb("arena", [P, ARENA])
        AUX1_AT = 18432

        ident = sb("ident", [P, P])
        chunk_ok = sb("chunk_ok", [P, P])
        chunk_neg = sb("chunk_neg", [P, P])
        before_ok = sb("before_ok", [P, P])
        before_neg = sb("before_neg", [P, P])
        sel = sb("sel", [LSTM_HEADS, LSTM_HEADS, P])
        cols = sb("cols", [P, 140])
        eps_col, one_col = sb("eps_col", [P, 1]), sb("one_col", [P, 1])
        stat = sb("stat", [P, 16])
        root = sb("root", [P, 16])
        rstd = sb("rstd", [P, 16])
        scale = sb("scale", [P, MT])
        att_negmax = sb("att_negmax", [P, 48])
        att_sum = sb("att_sum", [P, 48])
        att_tmp = sb("att_tmp", [P, 48])
        att_coef = sb("att_coef", [P, 48])
        decay = sb("decay", [P, 32])
        lstm_cols = sb("lstm_cols", [P, 48])
        lstm_den = sb("lstm_den", [P, 16])
        lstm_m = sb("lstm_m", [LSTM_HEADS, NCH + 1])
        lstm_dec = sb("lstm_dec", [LSTM_HEADS, NCH])
        lstm_b = sb("lstm_b", [LSTM_HEADS, 2])
        edges = sb("edges", [P, len(POOL_WINDOWS), POOL_PAD])

        proj = ctx.enter_context(nc.psum_tensor("proj", [P, 4, 512], F32))
        work = ctx.enter_context(nc.psum_tensor("work", [P, 4, 512], F32))

        def view(at, *shape):
            n = int(np.prod(shape))
            assert at + n <= ARENA, (at, shape)
            v = arena[:, at:at + n]
            names = "abc"[:len(shape)]
            if len(shape) == 1:
                return v
            return v.rearrange(f"p ({' '.join(names)}) -> p {' '.join(names)}", **{c: k for c, k in zip(names, shape)})

        aux1_hi = nc.alloc_sbuf_tensor_at("aux1_hi", [P, 4, SEQ], F32R, offset=arena_at + 4 * AUX1_AT)
        aux1_lo = nc.alloc_sbuf_tensor_at("aux1_lo", [P, 4, SEQ], F32R, offset=arena_at + 4 * (AUX1_AT + 4 * SEQ))

        rows1, rows2 = view(0, P), view(P, P)
        rel_rows, rel_wide = view(2 * P, 12), view(512, 12, P)
        one_hot, diag_stage = view(2048, sum(DIAG)), view(4096, 4 * sum(DIAG))
        squares = view(12288, 16, NCOL)
        root_diag = view(12288, MT, P)
        gla_o = view(0, MT, D)
        q_dec, k_in, k_out = view(4096, 4, SEQ), view(6144, 4, SEQ), view(8192, 4, SEQ)
        gla_b, k_tok = view(10240, 4, SEQ), view(10240, 4, SEQ)
        gla_v = view(12288, MT, D)
        gate_l1, gate_min = view(12288, 4, SEQ), view(14336, 4, SEQ)
        gla_state = view(16384, 2, GLA_HEADS, GLA_DV)
        reset, w_a2, gla_a = view(18432, SEQ), view(18944, SEQ), view(19456, SEQ)
        gla_att = view(18432, 4, SEQ)
        bias = [view(20480, 4, KEYS[0]), view(21504, 4, KEYS[1]), view(22016, 4, KEYS[2])]
        gla_silu = view(4096, 2, SEQ)
        att_p = [view(4096, 4, 4 * KEYS[0]), view(8192, 4, 4 * KEYS[1]), view(10240, 4, 4 * KEYS[2])]
        att_q, att_k = view(12288, 4, SEQ), view(14336, 4, SEQ)
        att_v = [view(12288, MT, SEQ), view(14336, MT, SEQ), view(16384, MT, SEQ)]
        att_pt = [view(18432, 7 * P), view(19328, 4 * P), view(19840, 4 * P)]
        lse_rows, lse_max = view(18432, 3, SEQ), view(19968, SEQ)
        att_o = view(20480, 4, SEQ)
        mix = view(4096, 16, SEQ)
        relu, relu_sq = view(0, 2, SEQ), view(1024, 2, SEQ)
        ple_pp, ple_in, ple_sig = view(0, MT, D), view(4096, MT, PLE), view(5120, 2, SEQ)
        ln_f_row = view(8192, D)
        lstm_q, lstm_k = view(0, KD, SEQ), view(4096, KD, SEQ)
        lstm_v, k_wa = view(8192, MT, LSTM_HEADS * (LSTM_HD + 1)), view(12304, MT, D)
        lstm_c = view(16400, 2 * LSTM_HEADS, LSTM_HD + 1)
        lstm_s, lstm_w = view(18456, 4, SEQ), view(20504, 2, SEQ)
        row = {k: view(16400 + i * SEQ, SEQ)[0:LSTM_HEADS, :] for i, k in enumerate(
            ("i", "f", "min", "l1", "b", "a", "e", "wa", "emt"))}
        row["neg_e"], row["inter"] = view(21528, SEQ)[0:LSTM_HEADS, :], view(22040, SEQ)[0:LSTM_HEADS, :]
        lstm_reset = view(21008, SEQ)
        lstm_h, gate_tmp = view(4096, MT, D), view(17408, 2, SEQ)
        sb_q, sb_k = [view(8192, 4, SEQ), view(4096, 4, SEQ)], [view(10240, 4, SEQ), view(6144, 4, SEQ)]
        sb_v, sb_o = [view(12288, MT, SEQ), view(14336, MT, SEQ)], view(0, MT, D)
        sb_l, sb_at = view(16384, 2, SEQ), view(17408, 2, SEQ)
        sb_gate = view(12288, MT, SEQ)
        y, y_gain = view(8192, MT, D), view(0, MT, D)
        post_row = [view(16384, D), view(17408, D)]
        odd_z = view(0, 16, SEQ)
        PADDED = POOL_PAD + SEQ
        pool_raw, pool_sum, pooled = view(8192, 2, PADDED), view(9248, 2, PADDED), view(10304, 2, SEQ)

        diag_dram = [nc.dram_tensor(f"bias_diag{g}", (4, P * DIAG[g]), F32, kind="Internal") for g in range(3)]

        LN1, LN2, LN3, PRE, GN, HN, BA, PS, CONV_AT = 0, 8, 16, 24, 40, 48, 56, 60, 76

        params_loaded, x_loaded = sem("params_loaded"), sem("x_loaded")
        consts_ready = sem("consts_ready")
        raw_loaded = [sem(f"raw_loaded{j}") for j in range(RING)]
        hi_ready, lo_ready = sem("hi_ready"), sem("lo_ready")
        block_used = sem("block_used")
        proj_full, proj_free = sem("proj_full"), sem("proj_free")
        act_hi_ready, act_ready = sem("act_hi_ready"), sem("act_ready")
        aux_hi_ready, aux_ready = sem("aux_hi_ready"), sem("aux_ready")
        turned = sem("turned")
        vec_step, act_step, pool_step = sem("vec_step"), sem("act_step"), sem("pool_step")
        cols_full, cols_ready = sem("cols_full"), sem("cols_ready")
        rel_ready, diag_full, diag_copied = sem("rel_ready"), sem("diag_full"), sem("diag_copied")
        diag_spilled = [sem(f"diag_spilled{g}") for g in range(3)]
        bias_loaded = sem("bias_loaded")
        sums_ready, sums_added = sem("sums_ready"), sem("sums_added")
        root_ready, scaled = sem("root_ready"), sem("scaled")
        x_gain_ready, scale_ready, y_added = sem("x_gain_ready"), sem("scale_ready"), sem("y_added")
        x_final = sem("x_final")
        gate_full, gate_l1_ready, gate_done = sem("gate_full"), sem("gate_l1_ready"), sem("gate_done")
        gla_exp, gla_rest = sem("gla_exp"), sem("gla_rest")
        ktok_full, ktok_ready = sem("ktok_full"), sem("ktok_ready")
        gla_att_full, gla_att_ready = sem("gla_att_full"), sem("gla_att_ready")
        gla_upd_full, gla_state_ready = sem("gla_upd_full"), sem("gla_state_ready")
        gla_o_full, gla_o_copied, gla_gated = sem("gla_o_full"), sem("gla_o_copied"), sem("gla_gated")
        logits_full, biased, max_ready, exp_ready = sem("logits_full"), sem("biased"), sem("max_ready"), sem("exp_ready")
        log_ready, lse_ready, lse_full = sem("log_ready"), sem("lse_ready"), sem("lse_full")
        lse_shifted, lse_exp, share_ready, share_full = sem("lse_shifted"), sem("lse_exp"), sem("share_ready"), sem("share_full")
        p_scaled, pt_full, pv_done, att_o_copied = sem("p_scaled"), sem("pt_full"), sem("pv_done"), sem("att_o_copied")
        pt_copied = [sem(f"pt_copied{g}") for g in range(3)]
        mix_ready = sem("mix_ready")
        squared = sem("squared")
        ple_loaded, ple_done = sem("ple_loaded"), sem("ple_done")
        lstm_f_ready, lstm_l1 = sem("lstm_f_ready"), sem("lstm_l1")
        lstm_rows, lstm_exps = sem("lstm_rows"), sem("lstm_exps")
        lstm_cols_full, lstm_cols_ready = sem("lstm_cols_full"), sem("lstm_cols_ready")
        conv_silu = sem("conv_silu")
        qk_full, neg_e_full, inter_full, lstm_kt_full = sem("qk_full"), sem("neg_e_full"), sem("inter_full"), sem("lstm_kt_full")
        w_masked, w_ready, s_ready, q_inter = sem("w_masked"), sem("w_ready"), sem("s_ready"), sem("q_inter")
        lstm_kt_ready, lstm_upd_full, lstm_c_ready = sem("lstm_kt_ready"), sem("lstm_upd_full"), sem("lstm_c_ready")
        lstm_gated, ya_ready = sem("lstm_gated"), sem("ya_ready")
        sb_z_full, sb_abs, sb_l1, sb_t, sb_a = sem("sb_z_full"), sem("sb_abs"), sem("sb_l1"), sem("sb_t"), sem("sb_a")
        sb_at_full, sb_at_ready, sb_o_full, sb_o_copied = sem("sb_at_full"), sem("sb_at_ready"), sem("sb_o_full"), sem("sb_o_copied")
        yb_ready, post_loaded = sem("yb_ready"), sem("post_loaded")
        pool_done = sem("pool_done")
        stored = sem("stored")

        def counted(fills):
            at, out_ = 0, {}
            for name, n in fills:
                out_[name] = at
                at += n
            return out_

        ACT_AT = counted([("ln1", 8), ("gla", 8), ("mix", 8), ("ln2", 8), ("ln3", 8), ("pre0", 8), ("yb", 8),
                          ("pre1", 8), ("mixa", 8)])
        AUX_AT = counted([("att", 4), ("mlp", 4 * (D_FF // NCOL)), ("p", 2), ("ya", 8), ("pool", 16), ("mixb", 8)])
        TURN_AT = counted([("ln1", 8), ("gla", 8), ("ln2", 8), ("p", 2), ("ln3", 8), ("pre0", 8), ("ya", 8), ("yb", 8),
                           ("pre1", 8)])
        NORM = {name: n for n, name in enumerate(("ln1", "ln2", "ln3", "pre0", "pre1"))}
        ROOT_AT = {name: n + 1 for n, name in enumerate(
            ("ln1", "gla", "ln2", "ln3", "ln_f", "pre0", "lstm", "post0", "pre1", "post1"))}
        SUMS_AT = {name: n + 1 for n, name in enumerate(("ln1", "ln2", "ln3", "ln_f", "post0", "pre1", "post1"))}

        def end(name, which=-1):
            return by_name[name][which].end

        def aux(tile):
            hi, lo = (aux0_hi, aux0_lo) if tile < 4 else (aux1_hi, aux1_lo)
            return hi[:, tile % 4, :], lo[:, tile % 4, :]

        def tile_of(pair):
            return {"act": lambda k: (act_hi[:, k, :], act_lo[:, k, :]), "aux0": aux, "aux1": lambda k: aux(k + 4),
                    "aux": aux}[pair]

        def wait_used(eng, block):
            s, j = blocks[block]
            if j == s.n - 1:
                eng.wait_ge(proj_full, s.end)
            else:
                eng.wait_ge(block_used, s.used0 + j + 1)

        SB_UNITS = SB_HEADS * MT
        SB_STEPS = SB_UNITS + 2
        sb_slabs = slabs[by_name["sb_q"][1].at:by_name["even_out0"][1].at + 1]
        todo = [(s, j) for s in sb_slabs for j in range(s.n)]
        beside = [todo[len(todo) * i // SB_STEPS:len(todo) * (i + 1) // SB_STEPS] for i in range(SB_STEPS)]

        first_up = by_name["mlp_up"][2]
        LOOP_TURNS = 3
        LOOP_SLABS = slabs[first_up.at:first_up.at + 6]
        LOOP_BLOCKS = sum(s.n for s in LOOP_SLABS)
        LOOP_BANKS = sum(s.banks for s in LOOP_SLABS)
        LOOP_USED = sum(s.n - 1 for s in LOOP_SLABS)

        block = ctx.enter_context(nc.Block())

        @block.sync
        def _(sp):
            for m in range(MT):
                sp.dma_start(x[:, m, :], W["x"][0, m * P:(m + 1) * P, :]).then_inc(x_loaded, 16)
            loads = [(rows1[LN1:LN1 + 8, :], W["ln1"].rearrange("a (k p) -> (a k) p", p=P)),
                     (rows1[LN2:LN2 + 8, :], W["ln2"].rearrange("a (k p) -> (a k) p", p=P)),
                     (rows1[LN3:LN3 + 8, :], W["ln3"].rearrange("a (k p) -> (a k) p", p=P)),
                     (rows1[PRE:PRE + 16, :], W["pre_norm_g_2"].rearrange("a (k p) -> (a k) p", p=P)),
                     (rows1[GN:GN + 8, :], W["gla_gn"].rearrange("a (k p) -> (a k) p", p=P)),
                     (rows1[HN:HN + 8, :], W["head_norm_g_2"].rearrange("a (k p) -> (a k) p", p=P)),
                     (rows1[BA:BA + 4, :], W["b_a"].rearrange("a (k p) -> (a k) p", p=P)),
                     (rows1[PS:PS + 16, :], W["pool_scale_2"].rearrange("a (k p) -> (a k) p", p=P)),
                     (rows2[0:64, :], W["conv_qk_2"].rearrange("t (k p) -> (t k) p", p=P)),
                     (rel_rows[0:REL_BUCKETS, :], W["rel_bias"]),
                     (one_hot[0:REL_BUCKETS + 1, :], W["bucket_one_hot"]),
                     (w_a2[0:GLA_RANK, :], W["w_a2"]),
                     (lstm_b[:, 0:1], W["bias_i_2"].rearrange("a h -> h a")),
                     (lstm_b[:, 1:2], W["bias_f_2"].rearrange("a h -> h a")),
                     (edges[:], bass.AP(W["pool_edges"].tensor, 0, [[0, P], [POOL_PAD, 4], [1, POOL_PAD]]))]
            for dst, src in loads:
                sp.dma_start(dst, src).then_inc(params_loaded, 16)

            def load(b, src):
                if b >= RING:
                    sp.wait_ge(lo_ready, b - RING + 1)
                sp.dma_start(w_raw[:, b % RING, :] if len(src.shape) == 2 else
                             w_raw[:, b % RING, :].rearrange("p (k c) -> p k c", c=P), src)\
                  .then_inc(raw_loaded[b % RING], 16)

            at = 0
            while at < len(slabs):
                s = slabs[at]
                if s is first_up:
                    g0 = 2
                    with sp.Fori(0, LOOP_TURNS) as i:
                        b = s.first
                        for t in range(2):
                            for k in range(KD):
                                sp.wait_ge(lo_ready, i * LOOP_BLOCKS + (b - RING + 1))
                                sp.dma_start(w_raw[:, b % RING, :], W["w_mlp1"][
                                    k * P:(k + 1) * P, bass.ds(i * (2 * NCOL) + (g0 + t) * NCOL, NCOL)])\
                                  .then_inc(raw_loaded[b % RING], 16)
                                b += 1
                            for c in range(2):
                                for k in range(4):
                                    sp.wait_ge(lo_ready, i * LOOP_BLOCKS + (b - RING + 1))
                                    sp.dma_start(w_raw[:, b % RING, :], W["w_mlp2"][
                                        bass.ds(i * (2 * NCOL) + (g0 + t - 1) * NCOL + k * P, P),
                                        c * NCOL:(c + 1) * NCOL]).then_inc(raw_loaded[b % RING], 16)
                                    b += 1
                    at += LOOP_TURNS * len(LOOP_SLABS)
                    continue
                for j, src in enumerate(s.sources):
                    load(s.first + j, src)
                at += 1
            for m in range(MT):
                sp.wait_ge(x_final, 2 * MT + m + 1)
                sp.dma_start(out[0, m * P:(m + 1) * P, :], x[:, m, :]).then_inc(stored, 16)
            sp.wait_ge(stored, 16 * MT)

        @block.gpsimd
        def _(pool):
            steps = [0]

            def step(ins):
                steps[0] += 1
                ins.then_inc(pool_step, 1)
                pool.wait_ge(pool_step, steps[0])

            step(pool.memset(ident[:], 0.0))
            step(pool.affine_select(out=ident[:], in_=ident[:], compare_op=ALU.not_equal, fill=1.0, base=0,
                                    pattern=[[-1, P]], channel_multiplier=1))
            for ok, fill, keep, far in ((chunk_ok, 1.0, 0.0, 0.0), (chunk_neg, 0.0, NEG, NEG)):
                step(pool.memset(ok[:], fill))
                step(pool.affine_select(out=ok[:], in_=ok[:], compare_op=ALU.is_ge, fill=keep, base=0,
                                        pattern=[[1, P]], channel_multiplier=-1))
                step(pool.memset(ok[0:CHUNK, CHUNK:P], far))
            for ok, fill, keep in ((before_ok, 1.0, 0.0), (before_neg, 0.0, NEG)):
                step(pool.memset(ok[:], fill))
                step(pool.affine_select(out=ok[:], in_=ok[:], compare_op=ALU.is_gt, fill=keep, base=0,
                                        pattern=[[-1, P]], channel_multiplier=1))
            step(pool.memset(sel[:], 0.0))
            step(pool.affine_select(out=sel[:], in_=sel[:], compare_op=ALU.not_equal, fill=1.0, base=0,
                                    pattern=[[-1, LSTM_HEADS], [0, P]], channel_multiplier=1))
            step(pool.memset(one_col[:], 1.0))
            pool.memset(eps_col[:], EPS).then_inc(consts_ready, 1)

            def rest(slot):
                return pool.tensor_tensor(w_lo[:, slot, :], w_raw[:, slot, :], w_hi[:, slot, :].bitcast(F32), ALU.subtract)

            with pool.Fori(0, n_blocks // RING) as turn:
                for slot in range(RING):
                    pool.wait_ge(hi_ready, turn * RING + (slot + 1))
                    rest(slot).then_inc(lo_ready, 1)
            for b in range(n_blocks - n_blocks % RING, n_blocks):
                pool.wait_ge(hi_ready, b + 1)
                rest(b % RING).then_inc(lo_ready, 1)

        @block.scalar
        def _(act):
            steps = [0]

            def step(ins):
                steps[0] += 1
                ins.then_inc(act_step, 1)
                act.wait_ge(act_step, steps[0])

            def w_hi_of(b):
                act.wait_ge(raw_loaded[b % RING], 16 * (b // RING + 1))
                if b >= RING:
                    wait_used(act, b - RING)
                act.copy(w_hi[:, b % RING, :], w_raw[:, b % RING, :]).then_inc(hi_ready, 1)

            prepared = [0]

            def prepare(end_):
                while prepared[0] < end_:
                    w_hi_of(prepared[0])
                    prepared[0] += 1

            def ahead(s):
                until = s
                while until.at + 1 < len(slabs) and (until is s or until.n == 0):
                    until = slabs[until.at + 1]
                prepare(s.first + s.n)
                prepare(min(until.first + until.n, s.first + s.n + RING - 2))

            def bank(s, c):
                act.wait_ge(proj_full, s.bank0 + c + 1)
                return proj[:, s.phys(c), :]

            def fill_hi(pair, base, n, turn=None, gain=None, src=None, ready=None, after=0):
                if after:
                    act.wait_ge(proj_full, after)
                sem_, tile = (act_hi_ready, tile_of(pair)) if pair == "act" else (aux_hi_ready, tile_of(pair))
                for k in range(n):
                    hi, _ = tile(k)
                    if turn is not None:
                        act.wait_ge(turned, turn + k + 1)
                        if gain is None:
                            act.copy(hi, work[:, k % 4, :]).then_inc(sem_, 1)
                        else:
                            act.activation(hi, work[:, k % 4, :], ACT.Copy, scale=cols[:, gain + k:gain + k + 1])\
                               .then_inc(sem_, 1)
                    else:
                        act.wait_ge(ready[0], ready[1](k))
                        act.copy(hi, src[:, k, :]).then_inc(sem_, 1)

            def head_roots(src):
                act.preload_act_table_set("sqrt_and_others")
                width = D // 4
                for r in range(16):
                    sq_ = squares[:, r // 2, (r % 2) * width:(r % 2 + 1) * width]
                    ins = act.activation(sq_, src(r), ACT.Square, accum_out=stat[:, r:r + 1])
                step(ins)
                act.activation(root[:], stat[:], ACT.Sqrt, bias=eps_col[:, 0:1], scale=1.0 / width).then_inc(root_ready, 1)

            def sum_squares(src, m, half, what=0):
                col = (what * 2 + half) * MT + m
                return act.activation(squares[:, col, :], src[:, m, half * NCOL:(half + 1) * NCOL], ACT.Square,
                                      accum_out=stat[:, col:col + 1])

            def halves_squared(src, half, ready):
                for m in range(MT):
                    act.wait_ge(ready[0], ready[1] + m + 1)
                    ins = sum_squares(src, m, half)
                return ins

            def token_roots(name):
                act.wait_ge(sums_added, SUMS_AT[name])
                act.activation(root[:, 0:MT], stat[:, 0:MT], ACT.Sqrt, bias=eps_col[:, 0:1], scale=1.0 / D)\
                   .then_inc(root_ready, 1)

            def sqrt_table():
                act.preload_act_table_set("sqrt_and_others")

            act.wait_ge(consts_ready, 1)
            act.wait_ge(x_loaded, 16 * MT)
            sqrt_table()
            for half in range(2):
                for m in range(MT):
                    ins = sum_squares(x, m, half)
            ins.then_inc(sums_ready, 1)
            token_roots("ln1")
            a_slab = by_name["gla_a"][0]
            prepare(a_slab.first + a_slab.n)
            act.wait_ge(cols_ready, 1)
            fill_hi("act", ACT_AT["ln1"], KD, turn=TURN_AT["ln1"], gain=LN1)
            ahead(a_slab)
            for g in range(3):
                act.wait_ge(diag_copied, 4 * (g + 1))
                act.dma_start(diag_dram[g].ap().rearrange("h (p e) -> p h e", p=P),
                              diag_stage[:, 4 * DIAG_AT[g]:4 * (DIAG_AT[g] + DIAG[g])].rearrange(
                                  "p (h e) -> p h e", h=4)).then_inc(diag_spilled[g], 16)
            for g in range(3):
                act.wait_ge(diag_spilled[g], 16)
                act.dma_start(bias[g], bass.AP(diag_dram[g], P - 1, [[DIAG[g] - 1, P], [P * DIAG[g], 4], [1, KEYS[g]]]))\
                   .then_inc(bias_loaded, 16)

            act.wait_ge(gate_full, GLA_HEADS)
            for h in range(GLA_HEADS):
                ins = act.activation(gate_l1[:, h, :], work[:, h, :], ACT.Abs, bias=cols[:, BA + h:BA + h + 1])
            step(ins)
            step(act.activation(gate_l1, gate_l1, ACT.Exp, scale=-1.0))
            act.activation(gate_l1, gate_l1, ACT.Ln, bias=1.0).then_inc(gate_l1_ready, 1)
            act.wait_ge(gate_done, 1)
            act.activation(q_dec, gla_b, ACT.Exp, scale=1.0 / GLA_TAU).then_inc(gla_exp, 1)
            act.activation(k_in, gla_b, ACT.Exp, scale=-1.0 / GLA_TAU).then_inc(gla_exp, 1)
            act.activation(decay[:, :].rearrange("p (h c) -> p h c", h=4),
                           gla_b.rearrange("p h (c t) -> p h c t", t=CHUNK)[:, :, :, CHUNK - 1],
                           ACT.Exp, scale=1.0 / GLA_TAU).then_inc(gla_exp, 1)
            act.wait_ge(gla_rest, 1)
            act.activation(k_out, gate_l1, ACT.Exp, scale=1.0 / GLA_TAU).then_inc(gla_exp, 1)
            ahead(by_name["gla_q"][0])
            ahead(by_name["gla_k"][0])
            for i, s in enumerate(by_name["gla_v"]):
                ahead(s)
                for m in range(MT):
                    act.copy(gla_v[:, m, i * NCOL:(i + 1) * NCOL], bank(s, m)).then_inc(proj_free, 1)
            for h in range(GLA_HEADS):
                act.wait_ge(ktok_full, h + 1)
                act.copy(k_tok[:, h, :], work[:, h, :]).then_inc(ktok_ready, 1)
            for m in range(MT):
                for b in range(2):
                    act.wait_ge(gla_o_full, 2 * m + b + 1)
                    act.copy(gla_o[:, m, b * 512:(b + 1) * 512], work[:, b, :]).then_inc(gla_o_copied, 1)
            act.wait_ge(gla_o_copied, 2 * MT)
            head_roots(lambda r: gla_o[:, r // GLA_HEADS, (r % GLA_HEADS) * GLA_DV:(r % GLA_HEADS + 1) * GLA_DV])
            n = 0
            for s in by_name["gla_r"]:
                ahead(s)
                for m in range(MT):
                    if n >= 2:
                        act.wait_ge(gla_gated, n - 1)
                    act.activation(gla_silu[:, n % 2, :], bank(s, m), ACT.Silu).then_inc(proj_free, 1)
                    n += 1

            for g in range(3):
                sq, sk = by_name[f"att_q{g}"][0], by_name[f"att_k{g}"][0]
                ahead(sq)
                ahead(sk)
                for h in range(ATT_HEADS):
                    bank(sk, h)
                    if g and h == 0:
                        act.wait_ge(logits_full, 4 * g)
                    src = proj[:, h, :] if g == 0 else proj[:, h, :].rearrange("p (l z) -> p z l", z=4)
                    dst = att_k[:, h, :] if g == 0 else att_k[:, h, :].rearrange("p (z l) -> p z l", z=4)
                    act.copy(dst, src).then_inc(proj_free, 1)
                for h in range(ATT_HEADS):
                    act.wait_ge(max_ready, 4 * g + h + 1)
                    for z in range(4):
                        c = (g * 4 + z) * 4 + h
                        p_ = att_p[g][:, h, z * KEYS[g]:(z + 1) * KEYS[g]]
                        ins = act.activation(p_, p_, ACT.Exp, bias=att_negmax[:, c:c + 1],
                                             accum_out=att_sum[:, c:c + 1])
                    ins.then_inc(exp_ready, 1)
            act.wait_ge(exp_ready, 12)
            act.activation(att_tmp[:], att_sum[:], ACT.Ln).then_inc(log_ready, 1)

            def values(g):
                s = by_name[f"att_v{g}"][0]
                ahead(s)
                for m in range(MT):
                    act.copy(att_v[g][:, m, :], bank(s, m)).then_inc(proj_free, 1)

            values(0)
            act.wait_ge(lse_shifted, 1)
            act.activation(lse_rows[0:4], lse_rows[0:4], ACT.Exp).then_inc(lse_exp, 1)
            values(1)
            values(2)
            for h in range(ATT_HEADS):
                act.wait_ge(pt_full, 3 * h + 1)
                if h:
                    act.wait_ge(pv_done, 3 * h - 2)
                act.copy(att_pt[0][:, 0:512], work[:, 0, :]).then_inc(pt_copied[0], 1)
                act.copy(att_pt[0][:, 512:7 * P], work[:, 1, 0:3 * P]).then_inc(pt_copied[0], 1)
            for i, s in enumerate(by_name["mix_gate"]):
                ahead(s)
                for c in range(4):
                    act.activation(mix[:, 4 * i + c, :], bank(s, c), ACT.Sigmoid).then_inc(proj_free, 1)
            fill_hi("aux0", AUX_AT["att"], 4, src=att_o, ready=(att_o_copied, lambda k: k + 1))
            fill_hi("act", ACT_AT["gla"], KD, turn=TURN_AT["gla"], gain=GN, after=end("mix_gate"))
            for s in by_name["gla_out"] + by_name["att_out"]:
                ahead(s)
            fill_hi("act", ACT_AT["mix"], KD, src=mix, ready=(mix_ready, lambda k: k + 1), after=end("gla_out"))
            mixes = by_name["mix_out"]
            ahead(mixes[0])
            sqrt_table()
            halves_squared(x, 0, (proj_free, mixes[0].bank0))
            ahead(mixes[1])
            halves_squared(x, 1, (proj_free, mixes[1].bank0)).then_inc(sums_ready, 1)
            token_roots("ln2")
            act.dma_start(ple_in, W["p"][0, 0].rearrange("(m p) c -> p m c", p=P)).then_inc(ple_loaded, 16)
            act.dma_start(ln_f_row, bass.AP(W["ln_f"].tensor, 0, [[0, P], [1, D]])).then_inc(ple_loaded, 16)
            fill_hi("act", ACT_AT["ln2"], KD, turn=TURN_AT["ln2"], gain=LN2, after=end("mix_out"))

            def mlp_turned(full, n, par, n0):
                for c in range(4):
                    act.wait_ge(proj_full, full + (c + 1))
                    if n0 + c >= 2:
                        act.wait_ge(squared, n + (c - 1))
                        act.wait_ge(aux_hi_ready, AUX_AT["mlp"] + n + (c - 1))
                    act.activation(relu[:, c % 2, :], proj[:, c, :], ACT.Relu).then_inc(proj_free, 1)
                    act.wait_ge(proj_free, full + (c + 1))
                    act.activation(aux(4 * par + c)[0], relu[:, c % 2, :], ACT.Square).then_inc(aux_hi_ready, 1)

            ups, downs = by_name["mlp_up"], by_name["mlp_down"]
            for g in range(2):
                ahead(ups[g])
                mlp_turned(ups[g].bank0, 4 * g, g, 4 * g)
            s0 = LOOP_SLABS[0]
            prepare(s0.first)
            with act.Fori(0, LOOP_TURNS) as i:
                b = s0.first

                def loop_hi(n):
                    nonlocal b
                    for _ in range(n):
                        act.wait_ge(raw_loaded[b % RING], i * (16 * LOOP_BLOCKS // RING) + 16 * (b // RING + 1))
                        r = b - RING
                        if r < s0.first:
                            rs, rj = blocks[r + LOOP_BLOCKS]
                            full, used = rs.end - LOOP_BANKS, rs.used0 - LOOP_USED
                        else:
                            rs, rj = blocks[r]
                            full, used = rs.end, rs.used0
                        if rj == rs.n - 1:
                            act.wait_ge(proj_full, i * LOOP_BANKS + full)
                        else:
                            act.wait_ge(block_used, i * LOOP_USED + (used + rj + 1))
                        act.copy(w_hi[:, b % RING, :], w_raw[:, b % RING, :]).then_inc(hi_ready, 1)
                        b += 1

                for t in range(2):
                    up = LOOP_SLABS[3 * t]
                    loop_hi(KD)
                    loop_hi(4)
                    mlp_turned(i * LOOP_BANKS + up.bank0, i * 8 + 4 * (2 + t), t, 8)
                    loop_hi(4)
            prepared[0] += LOOP_TURNS * LOOP_BLOCKS

            fill_hi("aux0", AUX_AT["p"], 2, turn=TURN_AT["p"])
            ahead(downs[-2])
            sqrt_table()
            halves_squared(x, 0, (proj_free, downs[-2].bank0))
            ahead(downs[-1])
            halves_squared(x, 1, (proj_free, downs[-1].bank0)).then_inc(sums_ready, 1)
            token_roots("ln3")
            for i, s in enumerate(by_name["ple_p"]):
                ahead(s)
                for m in range(MT):
                    act.copy(ple_pp[:, m, i * NCOL:(i + 1) * NCOL], bank(s, m)).then_inc(proj_free, 1)
            fill_hi("act", ACT_AT["ln3"], KD, turn=TURN_AT["ln3"], gain=LN3, after=end("mlp_up"))
            n = 0
            for s in by_name["ple_gate"]:
                ahead(s)
                for m in range(MT):
                    if n >= 2:
                        act.wait_ge(ple_done, n - 1)
                    act.activation(ple_sig[:, n % 2, :], bank(s, m), ACT.Sigmoid).then_inc(proj_free, 1)
                    n += 1
                    if s is by_name["ple_gate"][1] and m == MT - 1:
                        sqrt_table()
                for m in range(MT):
                    half = by_name["ple_gate"].index(s)
                    act.wait_ge(ple_done, half * MT + m + 1)
                    sum_squares(x, m, half)
                    act.wait_ge(x_gain_ready, half * MT + m + 1)
                    ins = sum_squares(ple_pp, m, half, what=1)
            ins.then_inc(sums_ready, 1)
            token_roots("ln_f")
            act.wait_ge(scale_ready, 1)
            act.activation(root[:, MT:2 * MT], scale[:], ACT.Sqrt, bias=eps_col[:, 0:1], scale=1.0 / D).then_inc(root_ready, 1)
            fill_hi("act", ACT_AT["pre0"], KD, turn=TURN_AT["pre0"], gain=PRE, after=end("ple_gate"))

            ahead(by_name["lstm_i"][0])
            ahead(by_name["lstm_f"][0])
            act.wait_ge(lstm_f_ready, 1)
            step(act.activation(row["l1"], row["f"], ACT.Abs))
            step(act.activation(row["l1"], row["l1"], ACT.Exp, scale=-1.0))
            act.activation(row["l1"], row["l1"], ACT.Ln, bias=1.0).then_inc(lstm_l1, 1)
            act.wait_ge(lstm_rows, 1)
            act.activation(row["inter"], row["inter"], ACT.Exp).then_inc(lstm_exps, 1)
            act.activation(row["wa"], row["wa"], ACT.Exp).then_inc(lstm_exps, 1)
            act.activation(row["emt"], row["emt"], ACT.Exp, scale=-1.0).then_inc(lstm_exps, 1)
            act.activation(lstm_dec[:], lstm_dec[:], ACT.Exp).then_inc(lstm_exps, 1)
            for dst, name in ((lstm_q, "lstm_q"), (lstm_k, "lstm_k")):
                for i, s in enumerate(by_name[name]):
                    ahead(s)
                    for c in range(4):
                        act.wait_ge(proj_free, s.bank0 + c + 1)
                        act.activation(dst[:, 4 * i + c, :], dst[:, 4 * i + c, :], ACT.Silu).then_inc(conv_silu, 1)
            v4 = lstm_v.rearrange("p m (h c) -> p m h c", h=LSTM_HEADS)
            for i, s in enumerate(by_name["lstm_v"]):
                ahead(s)
                for m in range(MT):
                    act.copy(v4[:, m, 2 * i:2 * i + 2, 0:LSTM_HD],
                             bank(s, m).rearrange("p (h c) -> p h c", h=2)).then_inc(proj_free, 1)
            for h in range(LSTM_HEADS):
                act.wait_ge(w_masked, h + 1)
                for m in range(MT):
                    w_ = lstm_w[:, h % 2, m * P:(m + 1) * P]
                    ins = act.activation(w_, w_, ACT.Exp, bias=lstm_cols[:, m * 4 + h:m * 4 + h + 1])
                ins.then_inc(w_ready, 1)
            n = 0
            for s in by_name["lstm_o"]:
                ahead(s)
                for m in range(MT):
                    if n >= 2:
                        act.wait_ge(lstm_gated, n - 1)
                    act.activation(gate_tmp[:, n % 2, :], bank(s, m), ACT.Sigmoid).then_inc(proj_free, 1)
                    n += 1
            act.wait_ge(lstm_gated, 2 * MT)
            head_roots(lambda r: lstm_h[:, r // LSTM_HEADS, (r % LSTM_HEADS) * LSTM_HD:(r % LSTM_HEADS + 1) * LSTM_HD])
            n = 0
            for s in by_name["lstm_z"]:
                ahead(s)
                for m in range(MT):
                    if n >= 2:
                        act.wait_ge(ya_ready, n - 1)
                    act.activation(gate_tmp[:, n % 2, :], bank(s, m), ACT.Silu).then_inc(proj_free, 1)
                    n += 1
            fill_hi("aux", AUX_AT["ya"], KD, turn=TURN_AT["ya"], gain=HN)

            for name in ("sb_q", "sb_k", "sb_v"):
                ahead(by_name[name][0])

            def log_terms(u):
                nk = (u % MT + 1) * P
                l_ = sb_l[:, u % 2, 0:nk]
                act.wait_ge(sb_z_full, u + 1)
                if u >= 2:
                    act.wait_ge(sb_at_full, u - 1)
                act.activation(l_, work[:, u % 2, 0:nk], ACT.Abs).then_inc(sb_abs, 1)
                act.wait_ge(sb_abs, u + 1)
                step(act.activation(l_, l_, ACT.Exp, scale=-1.0))
                act.activation(l_, l_, ACT.Ln, bias=1.0).then_inc(sb_l1, 1)

            def weights(u):
                act.wait_ge(sb_t, u + 1)
                l_ = sb_l[:, u % 2, 0:(u % MT + 1) * P]
                act.activation(l_, l_, ACT.Exp).then_inc(sb_a, 1)

            def weights_copied(u):
                nk = (u % MT + 1) * P
                act.wait_ge(sb_at_full, u + 1)
                if u >= 2:
                    act.wait_ge(sb_o_full, u - 1)
                act.copy(sb_at[:, u % 2, 0:nk], work[:, 2, 0:nk]).then_inc(sb_at_ready, 1)

            def values_copied(half):
                s = by_name["sb_v"][half]
                for m in range(MT):
                    act.copy(sb_v[half][:, m, :], bank(s, m)).then_inc(proj_free, 1)

            def gates(i):
                s = by_name["sb_z"][i]
                act.wait_ge(sb_o_full, SB_UNITS // 2)
                for m in range(MT):
                    if i:
                        act.wait_ge(yb_ready, m + 1)
                    act.activation(sb_gate[:, m, :], bank(s, m), ACT.Silu).then_inc(proj_free, 1)
                act.preload_act_table_set("natural_log_exp_and_others")

            values_copied(0)
            act.preload_act_table_set("natural_log_exp_and_others")
            for i in range(SB_STEPS):
                if i >= 2:
                    weights_copied(i - 2)
                if 1 <= i <= SB_UNITS:
                    weights(i - 1)
                if i < SB_UNITS:
                    log_terms(i)
                for s, j in [x_ for later in beside[i:i + 3] for x_ in later]:
                    prepare(s.first + j + 1)
                for s, j in beside[i]:
                    if j == s.n - 1 and s is by_name["sb_v"][1]:
                        values_copied(1)
                    elif j == s.n - 1 and s.name == "sb_z":
                        gates(by_name["sb_z"].index(s))
            ahead(by_name["even_out0"][1])
            act.wait_ge(yb_ready, 2 * MT)
            for r in range(2):
                act.dma_start(post_row[r], bass.AP(W["post_norm_g_2"].tensor, r * D, [[0, P], [1, D]]))\
                   .then_inc(post_loaded, 16)
            fill_hi("act", ACT_AT["yb"], KD, turn=TURN_AT["yb"], after=end("sb_z"))
            def layer_squared(second):
                for i, s in enumerate(by_name[second]):
                    ahead(s)
                    sqrt_table()
                    ins = halves_squared(y, i, (proj_free, s.bank0))
                ins.then_inc(sums_ready, 1)

            layer_squared("even_out1")
            token_roots("post0")
            for m in range(MT):
                act.wait_ge(x_final, MT + m + 1)
                for half in range(2):
                    ins = sum_squares(x, m, half)
            ins.then_inc(sums_ready, 1)
            token_roots("pre1")
            fill_hi("act", ACT_AT["pre1"], KD, turn=TURN_AT["pre1"], gain=PRE + 8, after=end("even_out1"))

            for i, s in enumerate(by_name["odd_z"]):
                ahead(s)
                for c in range(4):
                    act.activation(odd_z[:, 4 * i + c, :], bank(s, c), ACT.Silu).then_inc(proj_free, 1)
            def pool_hi_of(n):
                act.wait_ge(pool_done, n + 1)
                act.copy(aux(n % 8)[0], pooled[:, n % 2, :]).then_inc(aux_hi_ready, 1)

            n = 0
            for g, s in enumerate(by_name["pool_in"]):
                ahead(s)
                for c in range(4):
                    if n >= 2:
                        act.wait_ge(pool_done, n - 1)
                    act.copy(pool_raw[:, n % 2, POOL_PAD:PADDED], bank(s, c)).then_inc(proj_free, 1)
                    if n:
                        pool_hi_of(n - 1)
                    n += 1
                if g == 3:
                    pool_hi_of(n - 1)
                if g:
                    ahead(by_name["pool_mix"][g - 1])
            ahead(by_name["pool_mix"][3])
            fill_hi("act", ACT_AT["mixa"], KD, src=odd_z, after=end("pool_in"),
                    ready=(proj_free, lambda k: by_name["pool_mix"][k // 4].bank0 + k % 4 + 1))
            for s in by_name["odd_out0"]:
                ahead(s)
            fill_hi("aux", AUX_AT["mixb"], KD, src=odd_z[:, KD:2 * KD, :], after=end("pool_mix"),
                    ready=(proj_free, lambda k: by_name["pool_mix"][2 + k // 4].bank0 + k % 4 + 1))
            layer_squared("odd_out1")
            token_roots("post1")

        @block.vector
        def _(vec):
            steps = [0]

            def step(ins):
                steps[0] += 1
                ins.then_inc(vec_step, 1)
                vec.wait_ge(vec_step, steps[0])

            def bank(s, c):
                vec.wait_ge(proj_full, s.bank0 + c + 1)
                return proj[:, s.phys(c), :]

            def fill_lo(pair, base, n, turn=False, gain=None, src=None):
                hi_sem, sem_ = (act_hi_ready, act_ready) if pair == "act" else (aux_hi_ready, aux_ready)
                for k in range(n):
                    hi, lo = tile_of(pair)(k)
                    vec.wait_ge(hi_sem, base + k + 1)
                    v = work[:, k % 4, :] if turn else src[:, k, :]
                    if gain is None:
                        vec.tensor_tensor(lo, v, hi.bitcast(F32), ALU.subtract).then_inc(sem_, 1)
                    else:
                        vec.scalar_tensor_tensor(lo, v, cols[:, gain + k:gain + k + 1], hi.bitcast(F32),
                                                 ALU.mult, ALU.subtract).then_inc(sem_, 1)

            def head_scales(name):
                vec.wait_ge(root_ready, ROOT_AT[name])
                step(vec.reciprocal(rstd[:], root[:]))

            def token_scales(name):
                vec.wait_ge(sums_ready, SUMS_AT[name])
                vec.tensor_tensor(stat[:, 0:MT], stat[:, 0:MT], stat[:, MT:2 * MT], ALU.add).then_inc(sums_added, 1)
                vec.wait_ge(root_ready, ROOT_AT[name])
                step(vec.reciprocal(rstd[:, 0:MT], root[:, 0:MT]))

            def diagonals(by):
                for m in range(MT):
                    vec.tensor_scalar(root_diag[:, m, :], ident[:], by[:, m:m + 1], None, ALU.mult).then_inc(scaled, 1)

            def scaled_tokens(name):
                token_scales(name)
                diagonals(rstd)

            def add_to_x(s, i):
                for m in range(MT):
                    xm = x[:, m, i * NCOL:(i + 1) * NCOL]
                    vec.tensor_tensor(xm, xm, bank(s, m), ALU.add).then_inc(proj_free, 1)

            vec.wait_ge(params_loaded, 16 * 15)
            step(vec.memset(rel_rows[REL_BUCKETS:REL_BUCKETS + 1, :], NEG))
            vec.tensor_copy(rel_wide[0:REL_BUCKETS + 1], rel_rows[0:REL_BUCKETS + 1, :].unsqueeze(2).to_broadcast(
                [REL_BUCKETS + 1, 12, P])).then_inc(rel_ready, 1)
            vec.wait_ge(cols_full, 1)
            vec.tensor_copy(cols[:, 0:CONV_AT], work[:, 0, 0:CONV_AT])
            vec.tensor_copy(cols[:, CONV_AT:CONV_AT + 64], work[:, 0, P:P + 64]).then_inc(cols_ready, 1)
            vec.wait_ge(cols_ready, 1)
            for n in range(12):
                g, h = n // 4, n % 4
                vec.wait_ge(diag_full, n + 1)
                vec.tensor_copy(diag_stage[:, 4 * DIAG_AT[g] + h * DIAG[g]:4 * DIAG_AT[g] + (h + 1) * DIAG[g]],
                                work[:, 1 + n % 3, 0:DIAG[g]]).then_inc(diag_copied, 1)
            scaled_tokens("ln1")
            fill_lo("act", ACT_AT["ln1"], KD, turn=True, gain=LN1)

            step(vec.memset(reset, 1.0))
            step(vec.memset(reset.rearrange("p (c t) -> p c t", t=CHUNK)[:, :, 0:1], 0.0))
            vec.tensor_copy(gla_a[0:GLA_RANK, :], bank(by_name["gla_a"][0], 0)[0:GLA_RANK, :]).then_inc(proj_free, 1)
            vec.wait_ge(gate_l1_ready, 1)
            for h in range(GLA_HEADS):
                ins = vec.tensor_scalar(gate_min[:, h, :], work[:, h, :], cols[:, BA + h:BA + h + 1], 0.0, ALU.add, ALU.min)
            step(ins)
            step(vec.tensor_tensor(gate_min, gate_min, gate_l1, ALU.subtract))
            for h in range(GLA_HEADS):
                ins = vec.tensor_tensor_scan(gla_b[:, h, :], reset, gate_min[:, h, :], 0.0, ALU.mult, ALU.add)
            ins.then_inc(gate_done, 1)
            vec.wait_ge(gate_done, 1)
            b_chunks = gla_b.rearrange("p h (c t) -> p (h c) t", t=CHUNK)
            vec.tensor_tensor(gate_l1.rearrange("p h (c t) -> p (h c) t", t=CHUNK),
                              b_chunks[:, :, CHUNK - 1:CHUNK].to_broadcast([P, GLA_HEADS * NCH, CHUNK]),
                              b_chunks, ALU.subtract).then_inc(gla_rest, 1)
            vec.wait_ge(gate_full, GLA_HEADS)
            step(vec.memset(gla_att, 0.0))
            s = by_name["gla_q"][0]
            vec.wait_ge(gla_exp, 1)
            for h in range(GLA_HEADS):
                vec.scalar_tensor_tensor(q_dec[:, h, :], bank(s, h), GLA_DK ** -0.5, q_dec[:, h, :],
                                         ALU.mult, ALU.mult).then_inc(proj_free, 1)
            s = by_name["gla_k"][0]
            vec.wait_ge(gla_exp, 4)
            for h in range(GLA_HEADS):
                k_ = bank(s, h)
                vec.tensor_tensor(k_in[:, h, :], k_in[:, h, :], k_, ALU.mult)
                vec.tensor_tensor(k_out[:, h, :], k_out[:, h, :], k_, ALU.mult).then_inc(proj_free, 1)
            for h in range(GLA_HEADS):
                vec.wait_ge(gla_att_full, h + 1)
                vec.copy_predicated(gla_att[:, h, :].rearrange("p (m t) -> p m t", m=MT),
                                    chunk_ok[:].bitcast(U32).unsqueeze(1).to_broadcast([P, MT, P]),
                                    work[:, h, :].rearrange("p (m t) -> p m t", m=MT)).then_inc(gla_att_ready, 1)
            for n in range(NCH - 1):
                for h in range(GLA_HEADS):
                    if h % 2 == 0:
                        vec.wait_ge(gla_upd_full, 2 * n + h // 2 + 1)
                    upd = work[:, 2 + h // 2, (h % 2) * GLA_DV:(h % 2 + 1) * GLA_DV]
                    new = gla_state[:, (n + 1) % 2, h, :]
                    if n == 0:
                        vec.tensor_copy(new, upd).then_inc(gla_state_ready, 1)
                    else:
                        vec.wait_ge(gla_state_ready, 4 * (n - 1) + h + 1)
                        vec.scalar_tensor_tensor(new, gla_state[:, n % 2, h, :], decay[:, h * NCH + n:h * NCH + n + 1],
                                                 upd, ALU.mult, ALU.add).then_inc(gla_state_ready, 1)
            head_scales("gla")
            n = 0
            for i, s in enumerate(by_name["gla_r"]):
                for m in range(MT):
                    vec.wait_ge(proj_free, s.bank0 + m + 1)
                    for hh in range(2):
                        h = 2 * i + hh
                        o_ = gla_o[:, m, h * GLA_DV:(h + 1) * GLA_DV]
                        ins = vec.scalar_tensor_tensor(o_, o_, rstd[:, m * 4 + h:m * 4 + h + 1],
                                                       gla_silu[:, n % 2, hh * GLA_DV:(hh + 1) * GLA_DV], ALU.mult, ALU.mult)
                    ins.then_inc(gla_gated, 1)
                    n += 1

            vec.wait_ge(bias_loaded, 16 * 3)
            vec.wait_ge(gla_gated, 2 * MT)
            p0 = att_p[0].rearrange("p h (z k) -> p h z k", z=4)
            vec.memset(p0[:, :, 0, 0:P], NEG)
            for g in range(3):
                s = by_name[f"att_q{g}"][0]
                for h in range(ATT_HEADS):
                    src = bank(s, h)
                    if g and h == 0:
                        vec.wait_ge(logits_full, 4 * g)
                    dst = att_q[:, h, :]
                    if g:
                        src, dst = src.rearrange("p (l z) -> p z l", z=4), dst.rearrange("p (z l) -> p z l", z=4)
                    vec.tensor_copy(dst, src).then_inc(proj_free, 1)
                for h in range(ATT_HEADS):
                    vec.wait_ge(logits_full, 4 * g + h + 1)
                    b_ = bias[g][:, h, :]
                    p_ = att_p[g][:, h, :].rearrange("p (z k) -> p z k", z=4)

                    def biased_logits(dst, src, b):
                        return vec.scalar_tensor_tensor(dst, src, HD ** -0.5, b, ALU.mult, ALU.add)

                    if g == 0:
                        b0 = 2 * (h % 2)
                        biased_logits(p_[:, 0, P:2 * P], work[:, b0, 0:P], b_[:, P:2 * P])
                        biased_logits(p_[:, 1, :], work[:, b0, 2 * P:4 * P], b_)
                        ins = biased_logits(p_[:, 2:4, :], work[:, b0 + 1, :].rearrange("p (z k) -> p z k", z=2),
                                            b_.unsqueeze(1).to_broadcast([P, 2, 2 * P]))
                    else:
                        ins = biased_logits(p_, work[:, h, :].rearrange("p (z k) -> p z k", z=4),
                                            b_.unsqueeze(1).to_broadcast([P, 4, P]))
                    ins.then_inc(biased, 1)
                    vec.wait_ge(biased, 4 * g + h + 1)
                    nm = att_negmax[:, 16 * g:16 * g + 16].rearrange("p (z h) -> p z h", z=4)[:, :, h]
                    step(vec.tensor_reduce(nm, p_, AX, ALU.max))
                    vec.tensor_scalar(nm, nm, -1.0, None, ALU.mult).then_inc(max_ready, 1)
            vec.wait_ge(log_ready, 1)
            vec.tensor_tensor(att_tmp[:], att_tmp[:], att_negmax[:], ALU.subtract).then_inc(lse_ready, 1)
            for g in range(3):
                vec.wait_ge(lse_full, g + 1)
                src, dst = work[0:4, g, :], lse_rows[0:4, g, :]
                if g:
                    src, dst = src.rearrange("p (z l) -> p z l", z=4), dst.rearrange("p (l z) -> p z l", z=4)
                step(vec.tensor_copy(dst, src))
            top_ = lse_max[0:4, :]
            step(vec.tensor_tensor(top_, lse_rows[0:4, 0, :], lse_rows[0:4, 1, :], ALU.max))
            step(vec.tensor_tensor(top_, top_, lse_rows[0:4, 2, :], ALU.max))
            vec.tensor_tensor(lse_rows[0:4], lse_rows[0:4], top_.unsqueeze(1).to_broadcast([4, 3, SEQ]), ALU.subtract)\
               .then_inc(lse_shifted, 1)
            vec.wait_ge(lse_exp, 1)
            step(vec.tensor_tensor(top_, lse_rows[0:4, 0, :], lse_rows[0:4, 1, :], ALU.add))
            step(vec.tensor_tensor(top_, top_, lse_rows[0:4, 2, :], ALU.add))
            step(vec.reciprocal(top_, top_))
            vec.tensor_tensor(lse_rows[0:4], lse_rows[0:4], top_.unsqueeze(1).to_broadcast([4, 3, SEQ]), ALU.mult)\
               .then_inc(share_ready, 1)
            step(vec.reciprocal(att_coef[:], att_sum[:]))
            vec.wait_ge(share_full, 1)
            step(vec.tensor_tensor(att_coef[:], att_coef[:], work[:, 3, 0:48], ALU.mult))
            for h in range(ATT_HEADS):
                for g in range(3):
                    for z in range(4):
                        p_ = att_p[g][:, h, z * KEYS[g]:(z + 1) * KEYS[g]]
                        c = (g * 4 + z) * 4 + h
                        ins = vec.tensor_scalar(p_, p_, att_coef[:, c:c + 1], None, ALU.mult)
                    ins.then_inc(p_scaled, 1)
            for h in range(ATT_HEADS):
                for g in (1, 2):
                    vec.wait_ge(pt_full, 3 * h + g + 1)
                    if h:
                        vec.wait_ge(pv_done, 3 * (h - 1) + g + 1)
                    vec.tensor_copy(att_pt[g], work[:, 2 if g == 1 else 0, :]).then_inc(pt_copied[g], 1)
                vec.wait_ge(pv_done, 3 * h + 3)
                vec.tensor_copy(att_o[:, h, :], work[:, 3, :]).then_inc(att_o_copied, 1)
            fill_lo("aux0", AUX_AT["att"], 4, src=att_o)
            fill_lo("act", ACT_AT["gla"], KD, turn=True, gain=GN)
            for i, s in enumerate(by_name["gla_out"]):
                for c in range(4):
                    t = mix[:, 4 * i + c, :]
                    vec.tensor_tensor(t, t, bank(s, c), ALU.mult).then_inc(proj_free, 1)
            for i, s in enumerate(by_name["att_out"]):
                for c in range(4):
                    t, u = mix[:, 4 * i + c, :], mix[:, 8 + 4 * i + c, :]
                    vec.tensor_tensor(u, u, bank(s, c), ALU.mult).then_inc(proj_free, 1)
                    vec.wait_ge(proj_free, s.bank0 + c + 1)
                    vec.tensor_tensor(t, t, u, ALU.add).then_inc(mix_ready, 1)
            fill_lo("act", ACT_AT["mix"], KD, src=mix)
            for i, s in enumerate(by_name["mix_out"]):
                add_to_x(s, i)

            scaled_tokens("ln2")
            fill_lo("act", ACT_AT["ln2"], KD, turn=True, gain=LN2)
            ups, downs = by_name["mlp_up"], by_name["mlp_down"]

            def mlp_rest(full, n, par, n0):
                for c in range(4):
                    vec.wait_ge(proj_free, full + (c + 1))
                    if n0 + c >= 2:
                        vec.wait_ge(aux_ready, AUX_AT["mlp"] + n + (c - 1))
                    vec.tensor_tensor(relu_sq[:, c % 2, :], relu[:, c % 2, :], relu[:, c % 2, :], ALU.mult).then_inc(squared, 1)
                    vec.wait_ge(squared, n + (c + 1))
                    vec.wait_ge(aux_hi_ready, AUX_AT["mlp"] + n + (c + 1))
                    hi, lo = aux(4 * par + c)
                    vec.tensor_tensor(lo, relu_sq[:, c % 2, :], hi.bitcast(F32), ALU.subtract).then_inc(aux_ready, 1)

            def mlp_add(full, i):
                for m in range(MT):
                    xm = x[:, m, i * NCOL:(i + 1) * NCOL]
                    vec.wait_ge(proj_full, full + (m + 1))
                    vec.tensor_tensor(xm, xm, proj[:, m, :], ALU.add).then_inc(proj_free, 1)

            mlp_rest(ups[0].bank0, 0, 0, 0)
            mlp_rest(ups[1].bank0, 4, 1, 4)
            for i in range(2):
                mlp_add(downs[i].bank0, i)
            with vec.Fori(0, LOOP_TURNS) as turn:
                for t in range(2):
                    up, d0, d1 = LOOP_SLABS[3 * t:3 * t + 3]
                    mlp_rest(turn * LOOP_BANKS + up.bank0, turn * 8 + 4 * (2 + t), t, 8)
                    mlp_add(turn * LOOP_BANKS + d0.bank0, 0)
                    mlp_add(turn * LOOP_BANKS + d1.bank0, 1)
            fill_lo("aux0", AUX_AT["p"], 2, turn=True)
            for i in range(2):
                mlp_add(downs[-2 + i].bank0, i)

            scaled_tokens("ln3")
            fill_lo("act", ACT_AT["ln3"], KD, turn=True, gain=LN3)
            n = 0
            for i, s in enumerate(by_name["ple_gate"]):
                for m in range(MT):
                    vec.wait_ge(proj_free, s.bank0 + m + 1)
                    g_ = ple_sig[:, n % 2, :]
                    xm = x[:, m, i * NCOL:(i + 1) * NCOL]
                    step(vec.tensor_tensor(g_, g_, ple_pp[:, m, i * NCOL:(i + 1) * NCOL], ALU.mult))
                    vec.tensor_tensor(xm, xm, g_, ALU.add).then_inc(ple_done, 1)
                    vec.wait_ge(ple_done, n + 1)
                    vec.tensor_tensor(ple_pp[:, m, i * NCOL:(i + 1) * NCOL], xm, ln_f_row[:, i * NCOL:(i + 1) * NCOL], ALU.mult)\
                       .then_inc(x_gain_ready, 1)
                    n += 1
            vec.wait_ge(sums_ready, SUMS_AT["ln_f"])
            step(vec.tensor_tensor(stat[:, 2 * MT:3 * MT], stat[:, 2 * MT:3 * MT], stat[:, 3 * MT:4 * MT], ALU.add))
            token_scales("ln_f")
            step(vec.tensor_tensor(scale[:], stat[:, 2 * MT:3 * MT], rstd[:, 0:MT], ALU.mult))
            vec.tensor_tensor(scale[:], scale[:], rstd[:, 0:MT], ALU.mult).then_inc(scale_ready, 1)
            vec.wait_ge(root_ready, ROOT_AT["pre0"])
            step(vec.reciprocal(rstd[:, MT:2 * MT], root[:, MT:2 * MT]))
            step(vec.tensor_tensor(rstd[:, MT:2 * MT], rstd[:, MT:2 * MT], rstd[:, 0:MT], ALU.mult))
            diagonals(rstd[:, MT:2 * MT])
            for m in range(MT):
                vec.tensor_scalar(x[:, m, :], ple_pp[:, m, :], rstd[:, m:m + 1], None, ALU.mult).then_inc(x_final, 1)
            fill_lo("act", ACT_AT["pre0"], KD, turn=True, gain=PRE)

            H = LSTM_HEADS
            vec.tensor_scalar(row["i"], bank(by_name["lstm_i"][0], 0)[0:H, :], lstm_b[:, 0:1], None, ALU.add).then_inc(proj_free, 1)
            vec.tensor_scalar(row["f"], bank(by_name["lstm_f"][0], 0)[0:H, :], lstm_b[:, 1:2], None, ALU.add)\
               .then_inc(lstm_f_ready, 1)
            vec.wait_ge(lstm_f_ready, 1)
            vec.tensor_scalar(row["min"], row["f"], 0.0, None, ALU.min).then_inc(proj_free, 1)
            step(vec.memset(lstm_reset, 1.0))
            step(vec.memset(lstm_reset.rearrange("p (c t) -> p c t", t=CHUNK)[:, :, 0:1], 0.0))
            step(vec.memset(lstm_m[:, 0:1], 0.0))
            vec.wait_ge(lstm_l1, 1)
            step(vec.tensor_tensor(row["min"], row["min"], row["l1"], ALU.subtract))
            step(vec.tensor_tensor_scan(row["b"], lstm_reset[0:H, :], row["min"], 0.0, ALU.mult, ALU.add))
            step(vec.tensor_tensor(row["a"], row["i"], row["b"], ALU.subtract))
            for c in range(NCH):
                t0, t1 = c * CHUNK, (c + 1) * CHUNK
                step(vec.tensor_tensor_scan(row["e"][:, t0:t1], row["a"][:, t0:t1], row["a"][:, t0:t1],
                                            lstm_m[:, c:c + 1], ALU.max, ALU.max))
                step(vec.tensor_tensor(lstm_m[:, c + 1:c + 2], row["b"][:, t1 - 1:t1], row["e"][:, t1 - 1:t1], ALU.add))

            def chunks(r):
                return row[r].rearrange("p (c t) -> p c t", t=CHUNK)

            e_last = chunks("e")[:, :, CHUNK - 1:CHUNK]
            vec.tensor_scalar(row["neg_e"], row["e"], -1.0, None, ALU.mult)
            vec.tensor_tensor(chunks("inter"), lstm_m[:, 0:NCH].unsqueeze(2).to_broadcast([H, NCH, CHUNK]), chunks("e"), ALU.subtract)
            vec.tensor_tensor(chunks("wa"), chunks("a"), e_last.to_broadcast([H, NCH, CHUNK]), ALU.subtract)
            vec.tensor_tensor(row["emt"], row["b"], row["e"], ALU.add)
            vec.tensor_tensor(lstm_dec[:], lstm_m[:, 0:NCH], e_last[:, :, 0], ALU.subtract).then_inc(lstm_rows, 1)
            for at, (dst, name) in enumerate(((lstm_q, "lstm_q"), (lstm_k, "lstm_k"))):
                for i, s in enumerate(by_name[name]):
                    for c in range(4):
                        u, o_ = bank(s, c), dst[:, 4 * i + c, :]
                        tap = [cols[:, CONV_AT + k * 16 + 8 * at + 4 * i + c:CONV_AT + k * 16 + 8 * at + 4 * i + c + 1]
                               for k in range(CONV)]
                        step(vec.tensor_scalar(o_, u, tap[CONV - 1], None, ALU.mult))
                        for back in range(1, CONV):
                            ins = vec.scalar_tensor_tensor(o_[:, back:], u[:, 0:SEQ - back], tap[CONV - 1 - back], o_[:, back:],
                                                           ALU.mult, ALU.add)
                            if back < CONV - 1:
                                step(ins)
                        ins.then_inc(proj_free, 1)
            vec.wait_ge(lstm_cols_full, 1)
            vec.tensor_copy(lstm_cols[:], work[:, 0, 0:48]).then_inc(lstm_cols_ready, 1)
            vec.wait_ge(lstm_cols_full, 2)
            vec.tensor_copy(decay[:], work[:, 1, 0:32]).then_inc(lstm_cols_ready, 1)
            vec.wait_ge(lstm_cols_ready, 2)
            va = lstm_v.rearrange("p m (h c) -> p m h c", h=H)
            step(vec.memset(va[:, :, :, LSTM_HD:LSTM_HD + 1], 1.0))
            for h in range(H):
                vec.wait_ge(neg_e_full, h + 1)
                vec.tensor_tensor(lstm_w[:, h % 2, :].rearrange("p (m t) -> p m t", m=MT),
                                  work[:, 1, :].rearrange("p (m t) -> p m t", m=MT),
                                  chunk_neg[:].unsqueeze(1).to_broadcast([P, MT, P]), ALU.add).then_inc(w_masked, 1)
                vec.wait_ge(qk_full, h + 1)
                vec.wait_ge(inter_full, h + 1)
                for kk in range(2):
                    q_ = lstm_q[:, 2 * h + kk, :]
                    ins = vec.tensor_tensor(q_, q_, work[:, 2, :], ALU.mult)
                ins.then_inc(q_inter, 1)
                for pair in range(2):
                    vec.wait_ge(lstm_kt_full, 2 * h + pair + 1)
                    for mm in range(2):
                        m = 2 * pair + mm
                        ins = vec.tensor_scalar(k_wa[:, m, h * LSTM_HD:(h + 1) * LSTM_HD],
                                                work[:, 3, mm * LSTM_HD:(mm + 1) * LSTM_HD],
                                                lstm_cols[:, 16 + m * 4 + h:16 + m * 4 + h + 1], LSTM_HD ** -0.5,
                                                ALU.mult, ALU.mult)
                    ins.then_inc(lstm_kt_ready, 1)
                vec.wait_ge(w_ready, h + 1)
                vec.scalar_tensor_tensor(lstm_s[:, h, :], work[:, 0, :], LSTM_HD ** -0.5, lstm_w[:, h % 2, :],
                                         ALU.mult, ALU.mult).then_inc(s_ready, 1)
            core = by_name["lstm_core"][0]
            for m in range(MT):
                for n in (2 * m, 2 * m + 1):
                    if n == NCH - 1:
                        continue
                    for hk in range(2 * H):
                        vec.wait_ge(lstm_upd_full, 8 * n + hk + 1)
                        c_ = lstm_c[:, hk, :]
                        upd = work[:, hk % 4, 0:LSTM_HD + 1]
                        if n == 0:
                            vec.tensor_copy(c_, upd).then_inc(lstm_c_ready, 1)
                        else:
                            vec.wait_ge(lstm_c_ready, 8 * (n - 1) + hk + 1)
                            d = (hk // 2) * NCH + n
                            vec.scalar_tensor_tensor(c_, c_, decay[:, d:d + 1], upd, ALU.mult, ALU.add).then_inc(lstm_c_ready, 1)
                for h in range(H):
                    vec.wait_ge(proj_full, core.bank0 + 4 * m + h + 1)
                    den = lstm_den[:, m * 4 + h:m * 4 + h + 1]
                    raw = proj[:, h, LSTM_HD:LSTM_HD + 1]
                    step(vec.scalar_tensor_tensor(den, raw, -1.0, lstm_cols[:, 32 + m * 4 + h:32 + m * 4 + h + 1],
                                                  ALU.mult, ALU.max))
                    step(vec.tensor_tensor(den, raw, den, ALU.max))
                    step(vec.reciprocal(den, den))
                    vec.tensor_scalar(lstm_h[:, m, h * LSTM_HD:(h + 1) * LSTM_HD], proj[:, h, 0:LSTM_HD], den, None, ALU.mult)\
                       .then_inc(proj_free, 1)
            n = 0
            for i, s in enumerate(by_name["lstm_o"]):
                for m in range(MT):
                    vec.wait_ge(proj_free, s.bank0 + m + 1)
                    h_ = lstm_h[:, m, i * NCOL:(i + 1) * NCOL]
                    vec.tensor_tensor(h_, h_, gate_tmp[:, n % 2, :], ALU.mult).then_inc(lstm_gated, 1)
                    n += 1
            head_scales("lstm")
            n = 0
            for i, s in enumerate(by_name["lstm_z"]):
                for m in range(MT):
                    vec.wait_ge(proj_free, s.bank0 + m + 1)
                    for hh in range(2):
                        h = 2 * i + hh
                        h_ = lstm_h[:, m, h * LSTM_HD:(h + 1) * LSTM_HD]
                        ins = vec.scalar_tensor_tensor(h_, h_, rstd[:, m * 4 + h:m * 4 + h + 1],
                                                       gate_tmp[:, n % 2, hh * LSTM_HD:(hh + 1) * LSTM_HD], ALU.mult, ALU.mult)
                    ins.then_inc(ya_ready, 1)
                    n += 1
            fill_lo("aux", AUX_AT["ya"], KD, turn=True, gain=HN)

            def queries(half):
                s = by_name["sb_q"][half]
                for h in range(4):
                    vec.tensor_scalar(sb_q[half][:, h, :], bank(s, h), HD ** -0.5, None, ALU.mult).then_inc(proj_free, 1)

            def keys(half):
                s = by_name["sb_k"][half]
                for h in range(4):
                    vec.tensor_copy(sb_k[half][:, h, :], bank(s, h)).then_inc(proj_free, 1)

            def terms(u):
                nk = (u % MT + 1) * P
                z, l_ = work[:, u % 2, 0:nk], sb_l[:, u % 2, 0:nk]
                own = slice(nk - P, nk)
                vec.wait_ge(sb_l1, u + 1)
                step(vec.scalar_tensor_tensor(l_, z, 0.0, l_, ALU.max, ALU.add))
                step(vec.tensor_tensor(l_[:, own], l_[:, own], before_ok[:], ALU.mult))
                ones = one_col[:, 0:1].to_broadcast([P, nk])
                step(vec.tensor_tensor_scan(l_[:, ::-1], ones, l_[:, ::-1], 0.0, ALU.mult, ALU.add))
                step(vec.tensor_tensor(l_, z, l_, ALU.subtract))
                vec.tensor_tensor(l_[:, own], l_[:, own], before_neg[:], ALU.add).then_inc(sb_t, 1)

            def output(u):
                h, blk = u // MT, u % MT
                vec.wait_ge(sb_o_full, u + 1)
                vec.tensor_copy(sb_o[:, blk, h * HD:(h + 1) * HD], work[:, 3, 0:HD]).then_inc(sb_o_copied, 1)

            def gated(i):
                vec.wait_ge(sb_o_copied, SB_UNITS // 2 * (i + 1))
                for m in range(MT):
                    vec.wait_ge(proj_free, by_name["sb_z"][i].bank0 + m + 1)
                    o_ = sb_o[:, m, i * NCOL:(i + 1) * NCOL]
                    vec.tensor_tensor(o_, o_, sb_gate[:, m, :], ALU.mult).then_inc(yb_ready, 1)

            def first_out(i):
                s = by_name["even_out0"][i]
                for m in range(MT):
                    vec.tensor_copy(y[:, m, i * NCOL:(i + 1) * NCOL], bank(s, m)).then_inc(proj_free, 1)

            queries(0)
            keys(0)
            for i in range(SB_STEPS):
                if i >= 3:
                    output(i - 3)
                if i < SB_UNITS:
                    terms(i)
                for s, j in beside[i]:
                    if j < s.n - 1:
                        continue
                    if s is by_name["sb_q"][1]:
                        queries(1)
                    elif s is by_name["sb_k"][1]:
                        keys(1)
                    elif s is by_name["sb_z"][0]:
                        gated(0)
                    elif s is by_name["even_out0"][0]:
                        first_out(0)
            output(SB_UNITS - 1)
            gated(1)
            first_out(1)

            def layer_out(name, first, second):
                if name == "post0":
                    fill_lo("act", ACT_AT["yb"], KD, turn=True)
                else:
                    for i, s in enumerate(by_name[first]):
                        for m in range(MT):
                            vec.tensor_copy(y[:, m, i * NCOL:(i + 1) * NCOL], bank(s, m)).then_inc(proj_free, 1)
                    fill_lo("aux", AUX_AT["mixb"], KD, src=odd_z[:, KD:2 * KD, :])
                vec.wait_ge(proj_free, end(first))
                vec.wait_ge(post_loaded, 32)
                for i, s in enumerate(by_name[second]):
                    part = slice(i * NCOL, (i + 1) * NCOL)
                    for m in range(MT):
                        vec.tensor_tensor(y[:, m, part], y[:, m, part], bank(s, m), ALU.add).then_inc(proj_free, 1)
                    for m in range(MT):
                        vec.wait_ge(proj_free, s.bank0 + m + 1)
                        ins = vec.tensor_tensor(y_gain[:, m, part], y[:, m, part],
                                                post_row[0 if name == "post0" else 1][:, part], ALU.mult)
                step(ins)
                token_scales(name)
                for m in range(MT):
                    vec.scalar_tensor_tensor(x[:, m, :], y_gain[:, m, :], rstd[:, m:m + 1], x[:, m, :], ALU.mult, ALU.add)\
                       .then_inc(x_final, 1)

            layer_out("post0", "even_out0", "even_out1")
            scaled_tokens("pre1")
            fill_lo("act", ACT_AT["pre1"], KD, turn=True, gain=PRE + 8)

            step(vec.memset(pool_raw[:, :, 0:POOL_PAD], 0.0))
            step(vec.memset(pool_sum[:, :, 0:POOL_PAD], 0.0))
            n = 0

            def pool_lo_of(n):
                vec.wait_ge(aux_hi_ready, AUX_AT["pool"] + n + 1)
                hi, lo = aux(n % 8)
                vec.tensor_tensor(lo, pooled[:, n % 2, :], hi.bitcast(F32), ALU.subtract).then_inc(aux_ready, 1)

            def pool_mixed(g):
                s = by_name["pool_mix"][g]
                for c in range(4):
                    t = odd_z[:, 4 * g + c, :]
                    vec.scalar_tensor_tensor(t, bank(s, c), cols[:, PS + 4 * g + c:PS + 4 * g + c + 1], t,
                                             ALU.mult, ALU.mult).then_inc(proj_free, 1)

            for g, s in enumerate(by_name["pool_in"]):
                w = POOL_WINDOWS[g]
                for c in range(4):
                    vec.wait_ge(proj_free, s.bank0 + c + 1)
                    raw = src = pool_raw[:, n % 2, :]
                    back, level = 1, 0
                    while back < w:
                        dst = pool_sum[:, level % 2, :]
                        step(vec.tensor_tensor(dst[:, POOL_PAD:], src[:, POOL_PAD:], src[:, POOL_PAD - back:PADDED - back], ALU.add))
                        src, back, level = dst, 2 * back, level + 1
                    first = src[:, POOL_PAD:2 * POOL_PAD]
                    step(vec.tensor_tensor(first, first, edges[:, g, :], ALU.mult))
                    vec.scalar_tensor_tensor(pooled[:, n % 2, :], src[:, POOL_PAD:], 1.0 / w, raw[:, POOL_PAD:],
                                             ALU.mult, ALU.subtract).then_inc(pool_done, 1)
                    vec.wait_ge(pool_done, n + 1)
                    if n:
                        pool_lo_of(n - 1)
                    n += 1
                if g == 3:
                    pool_lo_of(n - 1)
                if g:
                    pool_mixed(g - 1)
            pool_mixed(3)
            fill_lo("act", ACT_AT["mixa"], KD, src=odd_z)
            layer_out("post1", "odd_out0", "odd_out1")

        @block.tensor
        def _(pe):
            def three(out_, a_hi, a_lo, b_hi, b_lo, first, last):
                pe.matmul(out_, a_hi, b_hi, start=first, stop=False)
                pe.matmul(out_, a_hi, b_lo, start=False, stop=False)
                return pe.matmul(out_, a_lo, b_hi, start=False, stop=last)

            def natural(m):
                return slice(m * P, (m + 1) * P)

            def by_stride(z):
                return slice(z, SEQ, 4)

            def slab_block(s, j, kind, pair, k, tokens, wait_bank):
                slot = (s.first + j) % RING
                hi, lo = tile_of(pair)(k)
                wh, wl = w_hi[:, slot, :], w_lo[:, slot, :]
                for c in range(4):
                    if j == 0:
                        wait_bank(c)
                    f = slice(c * P, (c + 1) * P)
                    t = tokens(c)
                    a, b = ((hi[:, t], lo[:, t]), (wh, wl)) if kind == "tokens" else ((wh[:, f], wl[:, f]), (hi, lo))
                    ins = three(proj[:, c, :], *a, *b, j == 0, j == s.n - 1)
                    if j == s.n - 1:
                        ins.then_inc(proj_full, 1)
                ins if j == s.n - 1 else ins.then_inc(block_used, 1)

            def slab(s, kind, pair="act", ready=None, tokens=natural, k0=0, before=None):
                for j in range(s.n):
                    if before:
                        before(j)
                    pe.wait_ge(lo_ready, s.first + j + 1)
                    if ready:
                        pe.wait_ge(ready[0], ready[1] + k0 + j + 1)

                    def wait_bank(c):
                        if s.need[c]:
                            pe.wait_ge(proj_free, s.need[c])

                    slab_block(s, j, kind, pair, k0 + j, tokens, wait_bank)

            def slabs_of(name, kind, pair="act", ready=None, skip=0):
                ss = by_name[name][skip:]
                s0 = ss[0]
                assert s0.n == RING
                if slabs[s0.at - 1].banks != 4:
                    pe.wait_ge(proj_free, s0.bank0)
                if ready:
                    pe.wait_ge(ready[0], ready[1] + KD)
                with pe.Fori(0, len(ss)) as i:
                    for j in range(s0.n):
                        pe.wait_ge(lo_ready, i * s0.n + (s0.first + j + 1))
                        slab_block(s0, j, kind, pair, j, natural,
                                   lambda c: pe.wait_ge(proj_free, i * 4 + (s0.bank0 + c - 3)))

            def narrow_slab(s, phys, ready=None, before=None):
                for j in range(s.n):
                    pe.wait_ge(lo_ready, s.first + j + 1)
                    if j == 0 and s.need[0]:
                        pe.wait_ge(proj_free, s.need[0])
                    slot = (s.first + j) % RING
                    for kk in range(4):
                        k = 4 * j + kk
                        if before:
                            before(k)
                        if ready:
                            pe.wait_ge(ready[0], ready[1] + k + 1)
                        f = slice(kk * P, (kk + 1) * P)
                        ins = three(proj[:, phys, :], w_hi[:, slot, f], w_lo[:, slot, f], act_hi[:, k, :], act_lo[:, k, :],
                                    k == 0, k == KD - 1)
                    ins.then_inc(proj_full if j == s.n - 1 else block_used, 1)

            def turn_tile(src, k, ready_sem, base, by_root=False):
                if k >= 4:
                    pe.wait_ge(ready_sem, base + k - 3)
                for m in range(MT):
                    o_, i_ = work[:, k % 4, m * P:(m + 1) * P], src[:, m, k * P:(k + 1) * P]
                    ins = pe.matmul(o_, i_, root_diag[:, m, :], start=True, stop=True) if by_root else \
                        pe.transpose(o_, i_, ident[:])
                ins.then_inc(turned, 1)

            def ahead_of(tile):
                def before(k):
                    for t in range(0 if k == 0 else k + 2, min(k + 3, KD)):
                        tile(t)
                return before

            def turn(src, ready_sem, base):
                return ahead_of(lambda k: turn_tile(src, k, ready_sem, base))

            def turn_norm(name, src=x):
                pe.wait_ge(scaled, MT * (NORM[name] + 1))
                return ahead_of(lambda k: turn_tile(src, k, act_ready, ACT_AT[name], by_root=True))

            def ready_act(name):
                return act_ready, ACT_AT[name]

            pe.wait_ge(consts_ready, 1)
            pe.wait_ge(params_loaded, 16 * 15)
            pe.transpose(work[:, 0, 0:CONV_AT], rows1[0:CONV_AT, :], ident[0:CONV_AT, 0:CONV_AT])
            pe.transpose(work[:, 0, P:P + 64], rows2[0:64, :], ident[0:64, 0:64]).then_inc(cols_full, 1)
            pe.wait_ge(rel_ready, 1)
            for n in range(12):
                g, h = n // 4, n % 4
                if n >= 3:
                    pe.wait_ge(diag_copied, n - 2)
                pe.matmul(work[:, 1 + n % 3, 0:DIAG[g]], rel_wide[0:REL_BUCKETS + 1, 4 * g + h, :],
                          one_hot[0:REL_BUCKETS + 1, DIAG_AT[g]:DIAG_AT[g] + DIAG[g]], start=True, stop=True)\
                  .then_inc(diag_full, 1)
            pe.wait_ge(cols_ready, 1)
            pe.wait_ge(diag_copied, 12)
            narrow_slab(by_name["gla_a"][0], 0, ready=ready_act("ln1"), before=turn_norm("ln1"))
            pe.wait_ge(proj_free, 1)
            for h in range(GLA_HEADS):
                pe.matmul(work[:, h, :], w_a2[0:GLA_RANK, h * P:(h + 1) * P], gla_a[0:GLA_RANK, :], start=True, stop=True)\
                  .then_inc(gate_full, 1)
            slab(by_name["gla_q"][0], "features")
            slab(by_name["gla_k"][0], "features")
            slabs_of("gla_v", "tokens")
            for h in range(GLA_HEADS):
                pe.wait_ge(proj_free, by_name["gla_k"][0].bank0 + h + 1)
                for m in range(MT):
                    ins = pe.transpose(work[:, h, m * P:(m + 1) * P], k_out[:, h, m * P:(m + 1) * P], ident[:])
                ins.then_inc(ktok_full, 1)
            for h in range(GLA_HEADS):
                pe.wait_ge(ktok_ready, h + 1)
                for m in range(MT):
                    t = natural(m)
                    ins = pe.matmul(work[:, h, t], k_in[:, h, t], q_dec[:, h, t], start=True, stop=True)
                ins.then_inc(gla_att_full, 1)
            pe.wait_ge(proj_free, end("gla_v"))
            pe.wait_ge(gla_att_ready, GLA_HEADS)
            for m in range(MT):
                if m:
                    pe.wait_ge(gla_o_copied, 2 * m)
                for h in range(GLA_HEADS):
                    pe.matmul(work[:, h // 2, (h % 2) * GLA_DV:(h % 2 + 1) * GLA_DV], gla_att[:, h, natural(m)],
                              gla_v[:, m, h * GLA_DV:(h + 1) * GLA_DV], start=(h % 2 == 0), stop=False, skip_group_check=True)
                for half in range(2):
                    n = 2 * m + half
                    rows = slice(half * CHUNK, (half + 1) * CHUNK)
                    if n < NCH - 1:
                        for h in range(GLA_HEADS):
                            if n and h % 2 == 0:
                                pe.wait_ge(gla_state_ready, 4 * (n - 1) + h + 2)
                            ins = pe.matmul(work[:, 2 + h // 2, (h % 2) * GLA_DV:(h % 2 + 1) * GLA_DV],
                                            k_tok[rows, h, natural(m)], gla_v[rows, m, h * GLA_DV:(h + 1) * GLA_DV],
                                            start=True, stop=True)
                            if h % 2:
                                ins.then_inc(gla_upd_full, 1)
                    for h in range(GLA_HEADS):
                        if n:
                            pe.wait_ge(gla_state_ready, 4 * (n - 1) + h + 1)
                            ins = pe.matmul(work[rows, h // 2, (h % 2) * GLA_DV:(h % 2 + 1) * GLA_DV],
                                            q_dec[:, h, n * CHUNK:(n + 1) * CHUNK], gla_state[:, n % 2, h, :],
                                            start=False, stop=(half == 1), skip_group_check=True)
                            if half and h % 2:
                                ins.then_inc(gla_o_full, 1)
            slabs_of("gla_r", "tokens")

            pe.wait_ge(gla_o_copied, 2 * MT)
            pe.wait_ge(gla_state_ready, 4 * (NCH - 1))
            for g in range(3):
                slab(by_name[f"att_q{g}"][0], "features")
                sk = by_name[f"att_k{g}"][0]
                slab(sk, "features")
                if g:
                    pe.wait_ge(biased, 4 * g)
                for h in range(ATT_HEADS):
                    pe.wait_ge(proj_free, sk.bank0 + h + 1)
                    if g == 0 and h >= 2:
                        pe.wait_ge(biased, h - 1)
                    for z in range(4):
                        q_ = att_q[:, h, natural(z)]
                        if g == 0:
                            k0 = max(z - 1, 0) * P
                            n_ = P if z == 0 else 2 * P
                            o_ = work[:, 2 * (h % 2) + z // 2, (z % 2) * 2 * P:(z % 2) * 2 * P + n_]
                            ins = pe.matmul(o_, q_, att_k[:, h, k0:k0 + n_], start=True, stop=True)
                        else:
                            ins = pe.matmul(work[:, h, natural(z)], q_, att_k[:, h, natural(z)], start=True, stop=True)
                    ins.then_inc(logits_full, 1)
            slab(by_name["att_v0"][0], "tokens")
            pe.wait_ge(lse_ready, 1)
            pe.wait_ge(biased, 12)
            for g in range(3):
                for z in range(4):
                    c = (g * 4 + z) * 4
                    ins = pe.transpose(work[0:4, g, natural(z)], att_tmp[:, c:c + 4], ident[:])
                ins.then_inc(lse_full, 1)
            slab(by_name["att_v1"][0], "tokens", tokens=by_stride)
            pe.wait_ge(share_ready, 1)
            for g in range(3):
                for z in range(4):
                    c = (g * 4 + z) * 4
                    t = natural(z) if g == 0 else by_stride(z)
                    ins = pe.transpose(work[:, 3, c:c + 4], lse_rows[0:4, g, t], ident[0:4, 0:4])
            ins.then_inc(share_full, 1)
            slab(by_name["att_v2"][0], "tokens", tokens=by_stride)
            pairs = [(z, kb) for z in range(4) for kb in ((z - 1, z) if z else (0,))]

            def probs_turned(u):
                h, g = u // 3, u % 3
                pe.wait_ge(p_scaled, u + 1)
                if g == 0:
                    if h:
                        pe.wait_ge(pt_copied[2], h)
                    for at, (z, kb) in enumerate(pairs):
                        k0 = z * KEYS[0] + (0 if kb < z else P)
                        ins = pe.transpose(work[:, at // 4, (at % 4) * P:(at % 4 + 1) * P], att_p[0][:, h, k0:k0 + P], ident[:])
                else:
                    if g == 2:
                        pe.wait_ge(pt_copied[0], 2 * h + 2)
                    elif h:
                        pe.wait_ge(pt_copied[1], h)
                    for z in range(4):
                        ins = pe.transpose(work[:, 2 if g == 1 else 0, natural(z)], att_p[g][:, h, natural(z)], ident[:])
                ins.then_inc(pt_full, 1)

            def values_weighted(u):
                h, g = u // 3, u % 3
                if g == 0 and h:
                    pe.wait_ge(att_o_copied, h)
                pe.wait_ge(pt_copied[g], 2 * h + 2 if g == 0 else h + 1)
                todo = [(at, kb, natural(z)) for at, (z, kb) in enumerate(pairs)] if g == 0 else \
                       [(z, z, by_stride(z)) for z in range(4)]
                for n, (at, kb, t) in enumerate(todo):
                    ins = pe.matmul(work[:, 3, t], att_v[g][:, kb, h * HD:(h + 1) * HD], att_pt[g][:, at * P:(at + 1) * P],
                                    start=(g == 0 and n == 0), stop=(g == 2 and n == 3), skip_group_check=True)
                ins.then_inc(pv_done, 1)

            pe.wait_ge(proj_free, end("att_v2"))
            probs_turned(0)
            for u in range(12):
                if u + 1 < 12:
                    probs_turned(u + 1)
                values_weighted(u)
            slabs_of("mix_gate", "features")
            pe.wait_ge(gla_gated, 2 * MT)
            pe.wait_ge(att_o_copied, ATT_HEADS)
            slab(by_name["gla_out"][0], "features", ready=ready_act("gla"), before=turn(gla_o, act_ready, ACT_AT["gla"]))
            slab(by_name["gla_out"][1], "features")
            for s in by_name["att_out"]:
                slab(s, "features", pair="aux0", ready=(aux_ready, AUX_AT["att"]))
            s = by_name["mix_out"][0]
            slab(s, "tokens", ready=ready_act("mix"))
            slab(by_name["mix_out"][1], "tokens")

            ups, downs = by_name["mlp_up"], by_name["mlp_down"]

            def down_pair(g):
                for i in range(2):
                    slab(downs[2 * g + i], "tokens", pair=f"aux{g % 2}", ready=(aux_ready, AUX_AT["mlp"] + 4 * g))

            slab(ups[0], "features", ready=ready_act("ln2"), before=turn_norm("ln2"))
            slab(ups[1], "features")
            down_pair(0)
            with pe.Fori(0, LOOP_TURNS) as i:
                for at, s in enumerate(LOOP_SLABS):
                    t = at // 3
                    for j in range(s.n):
                        pe.wait_ge(lo_ready, i * LOOP_BLOCKS + (s.first + j + 1))
                        if at % 3:
                            pe.wait_ge(aux_ready, i * 8 + (AUX_AT["mlp"] + 4 * (1 + t) + j + 1))
                        slab_block(s, j, "tokens" if at % 3 else "features", f"aux{(1 + t) % 2}" if at % 3 else "act", j,
                                   natural, lambda c: pe.wait_ge(proj_free, i * LOOP_BANKS + s.need[c]))
            pe.wait_ge(ple_loaded, 32)
            for k in range(PLE // P):
                turn_tile(ple_in, k, aux_ready, AUX_AT["p"])
            down_pair(D_FF // NCOL - 1)

            for s in by_name["ple_p"]:
                slab(s, "tokens", pair="aux0", ready=(aux_ready, AUX_AT["p"]))
            pe.wait_ge(aux_ready, AUX_AT["p"] + 2)
            slab(by_name["ple_gate"][0], "tokens", ready=ready_act("ln3"), before=turn_norm("ln3"))
            slab(by_name["ple_gate"][1], "tokens")

            narrow_slab(by_name["lstm_i"][0], 0, ready=ready_act("pre0"), before=turn_norm("pre0", ple_pp))
            narrow_slab(by_name["lstm_f"][0], 1)
            H = LSTM_HEADS
            slabs_of("lstm_q", "features")
            pe.wait_ge(lstm_exps, 4)
            pe.wait_ge(act_ready, ACT_AT["pre0"] + KD)
            for at, r in enumerate(("a", "wa", "emt")):
                for m in range(MT):
                    ins = pe.transpose(work[:, 0, 16 * at + 4 * m:16 * at + 4 * m + 4], row[r][:, natural(m)], ident[0:H, 0:H])
            ins.then_inc(lstm_cols_full, 1)
            for h in range(H):
                ins = pe.matmul(work[:, 1, h * NCH:(h + 1) * NCH], sel[:, h, :], lstm_dec[:], start=True, stop=True)
            ins.then_inc(lstm_cols_full, 1)
            slabs_of("lstm_k", "features")
            slabs_of("lstm_v", "tokens")
            pe.wait_ge(lstm_cols_ready, 2)
            for h in range(H):
                pe.wait_ge(conv_silu, 8 + 2 * h + 2)
                if h:
                    pe.wait_ge(s_ready, h)
                for m in range(MT):
                    for kk in range(2):
                        ins = pe.matmul(work[:, 0, natural(m)], lstm_k[:, 2 * h + kk, natural(m)], lstm_q[:, 2 * h + kk, natural(m)],
                                        start=(kk == 0), stop=(kk == 1))
                ins.then_inc(qk_full, 1)
                if h:
                    pe.wait_ge(w_masked, h)
                pe.matmul(work[:, 1, :], sel[:, h, :], row["neg_e"], start=True, stop=True).then_inc(neg_e_full, 1)
                if h:
                    pe.wait_ge(q_inter, h)
                pe.matmul(work[:, 2, :], sel[:, h, :], row["inter"], start=True, stop=True).then_inc(inter_full, 1)
                for pair in range(2):
                    if h or pair:
                        pe.wait_ge(lstm_kt_ready, 2 * h + pair)
                    for mm in range(2):
                        for kk in range(2):
                            at = mm * LSTM_HD + kk * P
                            ins = pe.transpose(work[:, 3, at:at + P], lstm_k[:, 2 * h + kk, natural(2 * pair + mm)], ident[:])
                    ins.then_inc(lstm_kt_full, 1)
            core = by_name["lstm_core"][0]
            va = lstm_v.rearrange("p m (h c) -> p m h c", h=H)
            pe.wait_ge(proj_free, end("lstm_v"))
            pe.wait_ge(s_ready, H)
            pe.wait_ge(lstm_kt_ready, 2 * H)
            for m in range(MT):
                for h in range(H):
                    if m:
                        pe.wait_ge(proj_free, core.need[4 * m + h])
                    pe.matmul(proj[:, h, 0:LSTM_HD + 1], lstm_s[:, h, natural(m)], va[:, m, h, :], start=True, stop=False,
                              skip_group_check=True)
                for half in range(2):
                    n = 2 * m + half
                    rows = slice(half * CHUNK, (half + 1) * CHUNK)
                    for h in range(H):
                        if n:
                            pe.wait_ge(lstm_c_ready, 8 * (n - 1) + 2 * h + 2)
                            for kk in range(2):
                                ins = pe.matmul(proj[rows, h, 0:LSTM_HD + 1], lstm_q[:, 2 * h + kk, n * CHUNK:(n + 1) * CHUNK],
                                                lstm_c[:, 2 * h + kk, :], start=False, stop=(half == 1 and kk == 1),
                                                skip_group_check=True)
                            if half:
                                ins.then_inc(proj_full, 1)
                        if n < NCH - 1:
                            for kk in range(2):
                                hk = 2 * h + kk
                                if 8 * n + hk >= 4:
                                    pe.wait_ge(lstm_c_ready, 8 * n + hk - 3)
                                pe.matmul(work[:, hk % 4, 0:LSTM_HD + 1], k_wa[rows, m, h * LSTM_HD + kk * P:h * LSTM_HD + (kk + 1) * P],
                                          va[rows, m, h, :], start=True, stop=True).then_inc(lstm_upd_full, 1)
            slabs_of("lstm_o", "tokens")
            slabs_of("lstm_z", "tokens")
            pe.wait_ge(ya_ready, 2 * MT)
            pe.wait_ge(lstm_c_ready, 8 * (NCH - 1))

            slab(by_name["sb_q"][0], "features", before=turn(lstm_h, aux_ready, AUX_AT["ya"]))
            slab(by_name["sb_k"][0], "features")
            slab(by_name["sb_v"][0], "tokens")
            pe.wait_ge(aux_ready, AUX_AT["ya"] + KD)

            def scores(u):
                half, h, nk = u // 16, u % 16 // MT, (u % MT + 1) * P
                if u % 16 == 0:
                    pe.wait_ge(proj_free, by_name["sb_k"][half].end)
                if u >= 2:
                    pe.wait_ge(sb_t, u - 1)
                pe.matmul(work[:, u % 2, 0:nk], sb_q[half][:, h, natural(u % MT)], sb_k[half][:, h, 0:nk],
                          start=True, stop=True).then_inc(sb_z_full, 1)

            def weights_turned(u):
                pe.wait_ge(sb_a, u + 1)
                if u:
                    pe.wait_ge(sb_at_ready, u)
                for kb in range(u % MT + 1):
                    ins = pe.transpose(work[:, 2, natural(kb)], sb_l[:, u % 2, natural(kb)], ident[:])
                ins.then_inc(sb_at_full, 1)

            def values(u):
                half, h, n_ = u // 16, u % 16 // MT, u % MT + 1
                if u % 16 == 0:
                    pe.wait_ge(proj_free, by_name["sb_v"][half].end)
                pe.wait_ge(sb_at_ready, u + 1)
                if u:
                    pe.wait_ge(sb_o_copied, u)
                for kb in range(n_):
                    ins = pe.matmul(work[:, 3, 0:HD], sb_at[:, u % 2, natural(kb)], sb_v[half][:, kb, h * HD:(h + 1) * HD],
                                    start=(kb == 0), stop=(kb == n_ - 1))
                ins.then_inc(sb_o_full, 1)

            for i in range(SB_STEPS):
                if i < SB_UNITS:
                    scores(i)
                for s, j in beside[i]:
                    pe.wait_ge(lo_ready, s.first + j + 1)
                    slab_block(s, j, "features" if s.name in ("sb_q", "sb_k") else "tokens",
                               "aux" if s.name == "even_out0" else "act", j, natural,
                               lambda c: pe.wait_ge(proj_free, s.need[c]))
                if 1 <= i <= SB_UNITS:
                    weights_turned(i - 1)
                if i >= 2:
                    values(i - 2)
            pe.wait_ge(yb_ready, 2 * MT)
            slab(by_name["even_out1"][0], "tokens", ready=ready_act("yb"), before=turn(sb_o, act_ready, ACT_AT["yb"]))
            slab(by_name["even_out1"][1], "tokens")

            slab(by_name["odd_z"][0], "features", ready=ready_act("pre1"), before=turn_norm("pre1"))
            slabs_of("odd_z", "features", skip=1)
            ins_, mixes = by_name["pool_in"], by_name["pool_mix"]
            slab(ins_[0], "features")
            for g in range(len(POOL_WINDOWS)):
                if g + 1 < len(POOL_WINDOWS):
                    slab(ins_[g + 1], "features")
                slab(mixes[g], "features", pair=f"aux{g % 2}", ready=(aux_ready, AUX_AT["pool"] + 4 * g))
            slabs_of("odd_out0", "tokens", ready=ready_act("mixa"))
            for s in by_name["odd_out1"]:
                slab(s, "tokens", pair="aux", ready=(aux_ready, AUX_AT["mixb"]))


_INS = ["x", "p", "ln1", "w_in", "w_a2", "b_a", "gla_gn", "w_o_gla", "w_o_attn", "w_out", "ln2", "w_mlp1", "w_mlp2",
        "ln3", "w_pp", "w_pg", "rel_bias", "ln_f", "pre_norm_g_2", "post_norm_g_2", "w_in_ab_2", "conv_qk_2",
        "bias_i_2", "bias_f_2", "head_norm_g_2", "w_out_ab_2", "w_in_c_2", "pool_w_2", "pool_scale_2", "w_out_c_2"]
_FLAT = {"w_in": (D, -1), "w_a2": (GLA_RANK, -1), "w_o_gla": (D, D), "w_o_attn": (-1, D), "w_out": (D, D),
         "w_mlp1": (D, D_FF), "w_mlp2": (D_FF, D), "w_pp": (PLE, D), "w_pg": (D, D), "w_in_ab_2": (D, -1),
         "w_out_ab_2": (2 * D, D), "w_in_c_2": (D, 2 * C_WIDTH), "pool_w_2": (C_WIDTH, -1), "w_out_c_2": (C_WIDTH, D),
         "conv_qk_2": (CONV, 2 * D)}


def kernel(**inputs):
    import concourse.bacc as bacc
    from concourse.bass_utils import run_bass_kernel_spmd

    nc = bacc.Bacc("TRN2", target_bir_lowering=False, num_devices=1)
    arrays, aps = {}, {}

    def give(name, a):
        arrays[f"in_{name}"] = a
        aps[name] = nc.dram_tensor(f"in_{name}", a.shape, mybir.dt.from_np(a.dtype), kind="ExternalInput").ap()

    for name in _INS:
        a = np.ascontiguousarray(inputs[name])
        give(name, a.reshape(_FLAT[name]) if name in _FLAT else a)
    give("bucket_one_hot", bucket_one_hot())
    give("pool_edges", pool_edges())
    out = nc.dram_tensor("out", (1, SEQ, D), F32, kind="ExternalOutput").ap()
    two_blocks(nc, aps, out)
    r = run_bass_kernel_spmd(nc, [arrays], core_ids=[0])
    return r.results[0]["out"]
```

```python
from contextlib import ExitStack

import numpy as np

import concourse.bass as bass
from concourse import mybir

F32 = mybir.dt.float32
F32R = mybir.dt.float32r
U32 = mybir.dt.uint32
ACT = mybir.ActivationFunctionType
ALU = mybir.AluOpType
AX = mybir.AxisListType.X

P = 128
SEQ = 512
MT = SEQ // P
D = 1024
KD = D // P
NCOL = 512
RING = 8
EPS = 1e-6
NEG = -1e30

GLA_HEADS, GLA_DK, GLA_DV, GLA_RANK, GLA_TAU, CHUNK = 4, 128, 256, 16, 16.0, 64
NCH = SEQ // CHUNK
ATT_HEADS, HD = 4, 128
ATT_GROUPS = ((128, 1), (512, 4), (2048, 16))
REL_BUCKETS, REL_MAX_DIST = 32, 2048
D_FF, PLE = 4 * D, 256
LSTM_HEADS, LSTM_HD, CONV = 4, 256, 4
SB_HEADS = 8
POOL_WINDOWS = (2, 4, 8, 16)
POOL_PAD = 16
C_WIDTH = 2 * D

DIAG = (3 * P - 1, 2 * P - 1, 2 * P - 1)
DIAG_AT = (0, DIAG[0], DIAG[0] + DIAG[1])
KEYS = (2 * P, P, P)


def bucket_one_hot():
    out = np.zeros((REL_BUCKETS + 1, sum(DIAG)), np.float32)
    half = REL_BUCKETS // 2
    for g, (window, dil) in enumerate(ATT_GROUPS):
        for e in range(DIAG[g]):
            steps = (2 * P - 1 - e) if g == 0 else (P - 1 - e)
            ok = 0 <= steps <= P if g < 2 else steps >= 0 and steps % 4 == 0
            row = REL_BUCKETS
            if ok:
                dist = steps * (1 if g == 0 else 4)
                far = half + int(np.int32(
                    np.log(np.float32(max(dist, 1)) / half) / np.log(REL_MAX_DIST / half) * (REL_BUCKETS - half)))
                row = dist if dist < half else min(far, REL_BUCKETS - 1)
            out[row, DIAG_AT[g] + e] = 1.0
    return out


def pool_edges():
    t = np.arange(POOL_PAD) + 1
    return np.stack([w / np.minimum(t, w) for w in POOL_WINDOWS]).astype(np.float32)


class Slab:

    def __init__(self, name, sources, banks):
        self.name, self.sources, self.banks = name, sources, banks
        self.n = len(sources)

    def phys(self, c):
        return c % 4


def plan_slabs(W):
    slabs = []

    def slab(name, w, col, row=0, rows=D, banks=MT):
        slabs.append(Slab(name, [w[row + k * P:row + (k + 1) * P, col:col + NCOL] for k in range(rows // P)], banks))

    def narrow(w, col):
        return [w[b * 512:(b + 1) * 512, col:col + P].rearrange("(k p) c -> p k c", p=P) for b in range(2)]

    w_in, w_ab, w_c = W["w_in"], W["w_in_ab_2"], W["w_in_c_2"]
    qk, dv = GLA_HEADS * GLA_DK, GLA_HEADS * GLA_DV
    at_a = 2 * qk + 2 * dv
    at_att = at_a + GLA_RANK
    at_gate = at_att + len(ATT_GROUPS) * 3 * ATT_HEADS * HD
    slabs.append(Slab("gla_a", narrow(w_in, at_a), 1))
    slab("gla_q", w_in, 0)
    slab("gla_k", w_in, qk)
    for i in range(2):
        slab("gla_v", w_in, 2 * qk + i * NCOL)
    for i in range(2):
        slab("gla_r", w_in, 2 * qk + dv + i * NCOL)
    for g in range(len(ATT_GROUPS)):
        for which in range(2):
            slab(f"att_{'qk'[which]}{g}", w_in, at_att + (3 * g + which) * NCOL)
    for g in range(len(ATT_GROUPS)):
        slab(f"att_v{g}", w_in, at_att + (3 * g + 2) * NCOL)
    for i in range(4):
        slab("mix_gate", w_in, at_gate + i * NCOL)
    slab("att_out", W["w_o_attn"], 0, rows=ATT_HEADS * HD)
    for i in range(2):
        slab("gla_out", W["w_o_gla"], i * NCOL)
    slab("att_out", W["w_o_attn"], NCOL, rows=ATT_HEADS * HD)
    for i in range(2):
        slab("mix_out", W["w_out"], i * NCOL)

    def up(g):
        slab("mlp_up", W["w_mlp1"], g * NCOL)

    def down(g):
        for i in range(2):
            slab("mlp_down", W["w_mlp2"], i * NCOL, row=g * NCOL, rows=NCOL)

    up(0)
    for g in range(1, D_FF // NCOL):
        up(g)
        down(g - 1)
    down(D_FF // NCOL - 1)
    for i in range(2):
        slab("ple_p", W["w_pp"], i * NCOL, rows=PLE)
    for i in range(2):
        slab("ple_gate", W["w_pg"], i * NCOL)

    at_if = 5 * D
    at_b = at_if + 2 * LSTM_HEADS
    slabs.append(Slab("lstm_if", narrow(w_ab, at_if), 1))
    for at, name in enumerate(("lstm_q", "lstm_k", "lstm_v")):
        for i in range(2):
            slab(name, w_ab, at * D + i * NCOL)
    slabs.append(Slab("lstm_core", [], MT * LSTM_HEADS))
    for at, name in enumerate(("lstm_o", "lstm_z")):
        for i in range(2):
            slab(name, w_ab, (3 + at) * D + i * NCOL)
    for half in range(2):
        for at, name in enumerate(("sb_q", "sb_k", "sb_v")):
            slab(name, w_ab, at_b + at * D + half * NCOL)
    for i in range(2):
        slab("sb_z", w_ab, at_b + 3 * D + i * NCOL)
        slab("even_out0", W["w_out_ab_2"], i * NCOL)
    for i in range(2):
        slab("even_out1", W["w_out_ab_2"], i * NCOL, row=D)

    for i in range(4):
        slab("odd_z", w_c, C_WIDTH + i * NCOL)

    def pool_in(g):
        slab("pool_in", w_c, g * NCOL)

    def pool_mix(g):
        slab("pool_mix", W["pool_w_2"], 0, row=g * NCOL, rows=NCOL)

    pool_in(0)
    for g in range(1, len(POOL_WINDOWS)):
        pool_in(g)
        pool_mix(g - 1)
    slab("odd_out0", W["w_out_c_2"], 0)
    pool_mix(len(POOL_WINDOWS) - 1)
    slab("odd_out0", W["w_out_c_2"], NCOL)
    for i in range(2):
        slab("odd_out1", W["w_out_c_2"], i * NCOL, row=D)

    first = bank0 = used0 = 0
    filled = [0] * 4
    for at, s in enumerate(slabs):
        s.at, s.first, s.bank0, s.used0, s.end = at, first, bank0, used0, bank0 + s.banks
        s.need = []
        for c in range(s.banks):
            b = s.phys(c)
            s.need.append(filled[b])
            filled[b] = bank0 + c + 1
        first += s.n
        bank0 += s.banks
        used0 += max(s.n - 1, 0)
    return slabs


def two_blocks(nc, W, out):
    slabs = plan_slabs(W)
    by_name = {}
    for s in slabs:
        by_name.setdefault(s.name, []).append(s)
    blocks = [(s, j) for s in slabs for j in range(s.n)]
    n_blocks = len(blocks)

    ctx = ExitStack()
    with ctx:
        def sb(name, shape, dt=F32):
            return ctx.enter_context(nc.sbuf_tensor(name, shape, dt))

        def sem(name):
            return ctx.enter_context(nc.semaphore(name))

        w_raw = sb("w_raw", [P, RING, NCOL])
        w_hi = sb("w_hi", [P, RING, NCOL], F32R)
        w_lo = sb("w_lo", [P, RING, NCOL], F32R)
        act_hi = sb("act_hi", [P, KD, SEQ], F32R)
        act_lo = sb("act_lo", [P, KD, SEQ], F32R)
        aux0_at = nc.sbuf_base
        aux0_hi = sb("aux0_hi", [P, 4, SEQ], F32R)
        aux0_lo = sb("aux0_lo", [P, 4, SEQ], F32R)
        x = sb("x", [P, MT, D])
        ARENA = 22560
        arena_at = nc.sbuf_base
        arena = sb("arena", [P, ARENA])
        AUX1_AT = 18432

        ident = sb("ident", [P, P])
        chunk_ok = sb("chunk_ok", [P, P])
        upto_neg = sb("upto_neg", [P, P])
        before_ok = sb("before_ok", [P, P])
        before_neg = sb("before_neg", [P, P])
        sel = sb("sel", [LSTM_HEADS, LSTM_HEADS, P])
        cols = sb("cols", [P, 140])
        eps_col, eps_sq_col, one_col = sb("eps_col", [P, 1]), sb("eps_sq_col", [P, 1]), sb("one_col", [P, 1])
        stat = sb("stat", [P, 16])
        root = sb("root", [P, 16])
        rstd = sb("rstd", [P, 16])
        scale = sb("scale", [P, MT])
        att_negmax = sb("att_negmax", [P, 48])
        att_sum = sb("att_sum", [P, 48])
        att_tmp = sb("att_tmp", [P, 48])
        att_coef = sb("att_coef", [P, 48])
        decay = sb("decay", [P, 32])
        lstm_cols = sb("lstm_cols", [P, 48])
        lstm_den = sb("lstm_den", [P, 16])
        lstm_m = sb("lstm_m", [LSTM_HEADS, MT + 1])
        lstm_dec = sb("lstm_dec", [LSTM_HEADS, MT])
        lstm_b = sb("lstm_b", [LSTM_HEADS, 2])
        edges = sb("edges", [P, len(POOL_WINDOWS), POOL_PAD])

        proj = ctx.enter_context(nc.psum_tensor("proj", [P, 4, 512], F32))
        work = ctx.enter_context(nc.psum_tensor("work", [P, 4, 512], F32))

        def view(at, *shape):
            n = int(np.prod(shape))
            assert at + n <= ARENA, (at, shape)
            v = arena[:, at:at + n]
            names = "abc"[:len(shape)]
            if len(shape) == 1:
                return v
            return v.rearrange(f"p ({' '.join(names)}) -> p {' '.join(names)}", **{c: k for c, k in zip(names, shape)})

        aux1_hi = nc.alloc_sbuf_tensor_at("aux1_hi", [P, 4, SEQ], F32R, offset=arena_at + 4 * AUX1_AT)
        early = nc.alloc_sbuf_tensor_at("early", [P, 2 * 4 * SEQ], F32, offset=aux0_at)
        diag_rows = early[0:ATT_HEADS, 0:sum(DIAG)]
        gla_silu = early[:].rearrange("p (m c) -> p m c", m=MT)
        aux1_lo = nc.alloc_sbuf_tensor_at("aux1_lo", [P, 4, SEQ], F32R, offset=arena_at + 4 * (AUX1_AT + 4 * SEQ))

        rows1, rows2 = view(0, P), view(P, P)
        rel_rows = view(2 * P, 12)
        one_hot = view(2048, sum(DIAG))
        squares = view(12288, 16, NCOL)
        DIAG_TILES = 3
        root_diag = view(12288, MT, P)
        scaled_x = view(16384, MT, D - DIAG_TILES * P)
        scaled_x1 = view(18432, MT, D - DIAG_TILES * P)
        gla_o = view(0, MT, D)
        q_dec, k_in, k_out = view(4096, 4, SEQ), view(6144, 4, SEQ), view(8192, 4, SEQ)
        gla_b, k_tok = view(10240, 4, SEQ), view(10240, 4, SEQ)
        gla_v = view(12288, MT, D)
        gate_l1, gate_min = view(12288, 4, SEQ), view(14336, 4, SEQ)
        gla_state = view(16384, 2, GLA_HEADS, GLA_DV)
        reset, w_a2, gla_a = view(18432, SEQ), view(18944, SEQ), view(19456, SEQ)
        gla_att = view(18432, 4, SEQ)
        bias = [view(20480, 4, KEYS[0]), view(21504, 4, KEYS[1]), view(22016, 4, KEYS[2])]
        att_p = [view(4096, 4, 4 * KEYS[0]), view(8192, 4, 4 * KEYS[1]), view(10240, 4, 4 * KEYS[2])]
        att_q, att_k = view(12288, 4, SEQ), view(14336, 4, SEQ)
        att_v = [view(12288, MT, SEQ), view(14336, MT, SEQ), view(16384, MT, SEQ)]
        att_pt = [view(18432, 7 * P), view(19328, 4 * P), view(19840, 4 * P)]
        lse_rows, lse_max = view(18432, 3, SEQ), view(19968, SEQ)
        att_o = view(20480, 4, SEQ)
        mix = view(4096, 16, SEQ)
        relu, relu_sq = view(0, 2, SEQ), view(1024, 2, SEQ)
        ple_pp, ple_in, ple_sig = view(0, MT, D), view(4096, MT, PLE), view(5120, 2, SEQ)
        ln_f_row = view(8192, D)
        lstm_q, lstm_k = view(0, KD, SEQ), view(4096, KD, SEQ)
        conv_raw = view(8192, 4, SEQ)
        lstm_v, k_wa = view(8192, MT, LSTM_HEADS * (LSTM_HD + 1)), view(12304, MT, D)
        lstm_c = view(16400, 2 * LSTM_HEADS, LSTM_HD + 1)
        lstm_s, lstm_w = view(18456, 4, SEQ), view(20504, 2, SEQ)
        row = {k: view(16400 + i * SEQ, SEQ)[0:LSTM_HEADS, :] for i, k in enumerate(
            ("i", "f", "min", "l1", "b", "a", "e", "wa", "emt"))}
        row["neg_e"], row["inter"] = view(21528, SEQ)[0:LSTM_HEADS, :], view(22040, SEQ)[0:LSTM_HEADS, :]
        if_rows = view(16400 + 8 * SEQ, SEQ)[0:2 * LSTM_HEADS, :]
        lstm_reset = view(21008, SEQ)
        lstm_h, gate_tmp = view(4096, MT, D), view(17408, 2, SEQ)
        sb_q, sb_k = [view(8192, 4, SEQ), view(4096, 4, SEQ)], [view(10240, 4, SEQ), view(6144, 4, SEQ)]
        sb_v, sb_o = [view(12288, MT, SEQ), view(14336, MT, SEQ)], view(0, MT, D)
        sb_l, sb_at = view(16384, 2, SEQ), view(17408, 2, SEQ)
        sb_gate = view(12288, MT, SEQ)
        y, y_gain = view(8192, MT, D), view(0, MT, D)
        post_row = [view(16384, D), view(17408, D)]
        odd_z = view(0, 16, SEQ)
        PADDED = POOL_PAD + SEQ
        pool_raw, pool_sum, pooled = view(8192, 4, PADDED), view(10304, 2, PADDED), view(12800, 4, SEQ)

        diag_dram = [nc.dram_tensor(f"bias_diag{g}", (4, P * DIAG[g]), F32, kind="Internal") for g in range(3)]

        LN1, LN2, LN3, PRE, GN, HN, BA, PS, CONV_AT = 0, 8, 16, 24, 40, 48, 56, 60, 76

        params_loaded, x_loaded = sem("params_loaded"), [sem(f"x_loaded{m}") for m in range(MT)]
        consts_ready = sem("consts_ready")
        raw_loaded = [sem(f"raw_loaded{j}") for j in range(RING)]
        hi_ready, lo_ready = sem("hi_ready"), sem("lo_ready")
        block_used = sem("block_used")
        proj_full, proj_free = sem("proj_full"), sem("proj_free")
        act_hi_ready, act_ready = sem("act_hi_ready"), sem("act_ready")
        aux_hi_ready, aux_ready = sem("aux_hi_ready"), sem("aux_ready")
        turned = sem("turned")
        vec_step, act_step, pool_step = sem("vec_step"), sem("act_step"), sem("pool_step")
        cols_full, cols_ready = sem("cols_full"), sem("cols_ready")
        rel_ready, diag_full, diag_copied = sem("rel_ready"), sem("diag_full"), sem("diag_copied")
        diag_spilled = [sem(f"diag_spilled{g}") for g in range(3)]
        bias_loaded = sem("bias_loaded")
        sums_ready, sums_added, root_ready = sem("sums_ready"), sem("sums_added"), sem("root_ready")
        sums2_ready, sums2_added, root2_ready = sem("sums2_ready"), sem("sums2_added"), sem("root2_ready")
        head_root_ready, scaled, x_scaled = sem("head_root_ready"), sem("scaled"), sem("x_scaled")
        x_gain_ready, scale_ready, y_added = sem("x_gain_ready"), sem("scale_ready"), sem("y_added")
        x_final, x_half = sem("x_final"), sem("x_half")
        gate_full, gate_l1_ready, gate_done = sem("gate_full"), sem("gate_l1_ready"), sem("gate_done")
        gla_exp, gla_rest = sem("gla_exp"), sem("gla_rest")
        ktok_full, ktok_ready = sem("ktok_full"), sem("ktok_ready")
        gla_att_full, gla_att_ready = sem("gla_att_full"), sem("gla_att_ready")
        gla_upd_full, gla_state_ready = sem("gla_upd_full"), sem("gla_state_ready")
        gla_o_full, gla_o_copied, gla_gated = sem("gla_o_full"), sem("gla_o_copied"), sem("gla_gated")
        logits_full, biased, max_ready, exp_ready = sem("logits_full"), sem("biased"), sem("max_ready"), sem("exp_ready")
        log_ready, lse_ready, lse_full = sem("log_ready"), sem("lse_ready"), sem("lse_full")
        lse_shifted, lse_exp, share_ready, share_full = sem("lse_shifted"), sem("lse_exp"), sem("share_ready"), sem("share_full")
        p_scaled, pt_full, pv_done, att_o_copied = sem("p_scaled"), sem("pt_full"), sem("pv_done"), sem("att_o_copied")
        pt_copied = [sem(f"pt_copied{g}") for g in range(3)]
        mix_ready = sem("mix_ready")
        squared = sem("squared")
        ple_loaded, ple_done = sem("ple_loaded"), sem("ple_done")
        lstm_if_copied, lstm_f_moved = sem("lstm_if_copied"), sem("lstm_f_moved")
        lstm_f_ready, lstm_l1 = sem("lstm_f_ready"), sem("lstm_l1")
        lstm_rows, lstm_exps = sem("lstm_rows"), sem("lstm_exps")
        lstm_cols_full, lstm_cols_ready = sem("lstm_cols_full"), sem("lstm_cols_ready")
        conv_done, conv_silu = sem("conv_done"), sem("conv_silu")
        qk_full, neg_e_full, inter_full, lstm_kt_full = sem("qk_full"), sem("neg_e_full"), sem("inter_full"), sem("lstm_kt_full")
        w_masked, w_ready, s_ready, q_inter = sem("w_masked"), sem("w_ready"), sem("s_ready"), sem("q_inter")
        lstm_kt_ready, lstm_upd_full, lstm_c_ready = sem("lstm_kt_ready"), sem("lstm_upd_full"), sem("lstm_c_ready")
        lstm_gated, ya_ready = sem("lstm_gated"), sem("ya_ready")
        sb_z_full, sb_abs, sb_l1, sb_t, sb_a = sem("sb_z_full"), sem("sb_abs"), sem("sb_l1"), sem("sb_t"), sem("sb_a")
        sb_at_full, sb_at_ready, sb_o_full, sb_o_copied = sem("sb_at_full"), sem("sb_at_ready"), sem("sb_o_full"), sem("sb_o_copied")
        yb_ready, post_loaded = sem("yb_ready"), sem("post_loaded")
        pool_done = sem("pool_done")
        stored = sem("stored")

        def counted(fills):
            at, out_ = 0, {}
            for name, n in fills:
                out_[name] = at
                at += n
            return out_

        ACT_AT = counted([("ln1", 8), ("gla", 8), ("mix", 8), ("ln2", 8), ("ln3", 8), ("pre0", 8), ("yb", 8),
                          ("pre1", 8), ("mixa", 8)])
        AUX_AT = counted([("att", 4), ("mlp", 4 * (D_FF // NCOL)), ("p", 2), ("ya", 8), ("pool", 16), ("mixb", 8)])
        TURN_AT = counted([("ln1", 8), ("gla", 8), ("ln2", 8), ("p", 2), ("ln3", 8), ("pre0", 8), ("ya", 8), ("yb", 8),
                           ("pre1", 8)])
        NORM = {name: n for n, name in enumerate(("ln1", "ln2", "ln3", "pre0", "pre1"))}
        SUMS_AT = counted([("ln1", 1), ("ln2", 1), ("ln3", 1), ("ln_f", 1), ("post0", MT), ("post1", MT)])
        ALL = slice(0, MT)

        def tile(m):
            return slice(m, m + 1)

        SUMS2_AT = {"pre0": 0, "pre1": 1}

        def end(name, which=-1):
            return by_name[name][which].end

        def aux(tile):
            hi, lo = (aux0_hi, aux0_lo) if tile < 4 else (aux1_hi, aux1_lo)
            return hi[:, tile % 4, :], lo[:, tile % 4, :]

        def tile_of(pair):
            return {"act": lambda k: (act_hi[:, k, :], act_lo[:, k, :]), "aux0": aux, "aux1": lambda k: aux(k + 4),
                    "aux": aux}[pair]

        def wait_used(eng, block):
            s, j = blocks[block]
            if j == s.n - 1:
                eng.wait_ge(proj_full, s.end)
            else:
                eng.wait_ge(block_used, s.used0 + j + 1)

        SB_UNITS = SB_HEADS * MT
        SB_STEPS = SB_UNITS + 2
        def spread(group, n):
            todo = [(s, j) for s in group for j in range(s.n)]
            return [todo[len(todo) * i // n:len(todo) * (i + 1) // n] for i in range(n)]

        beside = spread(slabs[by_name["sb_q"][1].at:by_name["even_out0"][1].at + 1], SB_STEPS + 1)
        heads_beside = spread(by_name["lstm_v"], LSTM_HEADS + 1)
        gla_beside = spread(by_name["gla_r"], NCH - 1) + [[]]

        probs_beside = spread(by_name["mix_gate"][:1], 3 * ATT_HEADS)

        first_up = by_name["mlp_up"][2]
        LOOP_TURNS = 3
        LOOP_SLABS = slabs[first_up.at:first_up.at + 6]
        LOOP_BLOCKS = sum(s.n for s in LOOP_SLABS)
        LOOP_BANKS = sum(s.banks for s in LOOP_SLABS)
        LOOP_USED = sum(s.n - 1 for s in LOOP_SLABS)

        block = ctx.enter_context(nc.Block())

        @block.sync
        def _(sp):
            for m in range(MT):
                sp.dma_start(x[:, m, :], W["x"][0, m * P:(m + 1) * P, :]).then_inc(x_loaded[m], 16)
            loads = [(rows1[LN1:LN1 + 8, :], W["ln1"].rearrange("a (k p) -> (a k) p", p=P)),
                     (rows1[LN2:LN2 + 8, :], W["ln2"].rearrange("a (k p) -> (a k) p", p=P)),
                     (rows1[LN3:LN3 + 8, :], W["ln3"].rearrange("a (k p) -> (a k) p", p=P)),
                     (rows1[PRE:PRE + 16, :], W["pre_norm_g_2"].rearrange("a (k p) -> (a k) p", p=P)),
                     (rows1[GN:GN + 8, :], W["gla_gn"].rearrange("a (k p) -> (a k) p", p=P)),
                     (rows1[HN:HN + 8, :], W["head_norm_g_2"].rearrange("a (k p) -> (a k) p", p=P)),
                     (rows1[BA:BA + 4, :], W["b_a"].rearrange("a (k p) -> (a k) p", p=P)),
                     (rows1[PS:PS + 16, :], W["pool_scale_2"].rearrange("a (k p) -> (a k) p", p=P)),
                     (rows2[0:64, :], W["conv_qk_2"].rearrange("t (k p) -> (t k) p", p=P)),
                     (rel_rows[0:REL_BUCKETS, :], W["rel_bias"]),
                     (one_hot[0:REL_BUCKETS + 1, :], W["bucket_one_hot"]),
                     (w_a2[0:GLA_RANK, :], W["w_a2"]),
                     (lstm_b[:, 0:1], W["bias_i_2"].rearrange("a h -> h a")),
                     (lstm_b[:, 1:2], W["bias_f_2"].rearrange("a h -> h a")),
                     (edges[:], bass.AP(W["pool_edges"].tensor, 0, [[0, P], [POOL_PAD, 4], [1, POOL_PAD]]))]
            for dst, src in loads:
                sp.dma_start(dst, src).then_inc(params_loaded, 16)

            def load(b, src):
                if b >= RING:
                    sp.wait_ge(lo_ready, b - RING + 1)
                sp.dma_start(w_raw[:, b % RING, :] if len(src.shape) == 2 else
                             w_raw[:, b % RING, :].rearrange("p (k c) -> p k c", c=P), src)\
                  .then_inc(raw_loaded[b % RING], 16)

            at = 0
            while at < len(slabs):
                s = slabs[at]
                if s is first_up:
                    g0 = 2
                    with sp.Fori(0, LOOP_TURNS) as i:
                        b = s.first
                        for t in range(2):
                            for k in range(KD):
                                sp.wait_ge(lo_ready, i * LOOP_BLOCKS + (b - RING + 1))
                                sp.dma_start(w_raw[:, b % RING, :], W["w_mlp1"][
                                    k * P:(k + 1) * P, bass.ds(i * (2 * NCOL) + (g0 + t) * NCOL, NCOL)])\
                                  .then_inc(raw_loaded[b % RING], 16)
                                b += 1
                            for c in range(2):
                                for k in range(4):
                                    sp.wait_ge(lo_ready, i * LOOP_BLOCKS + (b - RING + 1))
                                    sp.dma_start(w_raw[:, b % RING, :], W["w_mlp2"][
                                        bass.ds(i * (2 * NCOL) + (g0 + t - 1) * NCOL + k * P, P),
                                        c * NCOL:(c + 1) * NCOL]).then_inc(raw_loaded[b % RING], 16)
                                    b += 1
                    at += LOOP_TURNS * len(LOOP_SLABS)
                    continue
                for j, src in enumerate(s.sources):
                    load(s.first + j, src)
                at += 1
            for m in range(MT):
                sp.wait_ge(x_final, 2 * MT + m + 1)
                sp.dma_start(out[0, m * P:(m + 1) * P, :], x[:, m, :]).then_inc(stored, 16)
            sp.wait_ge(stored, 16 * MT)

        @block.gpsimd
        def _(pool):
            steps = [0]

            def step(ins):
                steps[0] += 1
                ins.then_inc(pool_step, 1)
                pool.wait_ge(pool_step, steps[0])

            step(pool.memset(ident[:], 0.0))
            step(pool.affine_select(out=ident[:], in_=ident[:], compare_op=ALU.not_equal, fill=1.0, base=0,
                                    pattern=[[-1, P]], channel_multiplier=1))
            for ok, fill, keep in ((chunk_ok, 1.0, 0.0), (upto_neg, 0.0, NEG)):
                step(pool.memset(ok[:], fill))
                step(pool.affine_select(out=ok[:], in_=ok[:], compare_op=ALU.is_ge, fill=keep, base=0,
                                        pattern=[[1, P]], channel_multiplier=-1))
            step(pool.memset(chunk_ok[0:CHUNK, CHUNK:P], 0.0))
            for ok, fill, keep in ((before_ok, 1.0, 0.0), (before_neg, 0.0, NEG)):
                step(pool.memset(ok[:], fill))
                step(pool.affine_select(out=ok[:], in_=ok[:], compare_op=ALU.is_gt, fill=keep, base=0,
                                        pattern=[[-1, P]], channel_multiplier=1))
            step(pool.memset(sel[:], 0.0))
            step(pool.affine_select(out=sel[:], in_=sel[:], compare_op=ALU.not_equal, fill=1.0, base=0,
                                    pattern=[[-1, LSTM_HEADS], [0, P]], channel_multiplier=1))
            step(pool.memset(one_col[:], 1.0))
            pool.memset(eps_sq_col[:], EPS * EPS)
            pool.memset(eps_col[:], EPS).then_inc(consts_ready, 1)

            def rest(slot):
                return pool.tensor_tensor(w_lo[:, slot, :], w_raw[:, slot, :], w_hi[:, slot, :].bitcast(F32), ALU.subtract)

            with pool.Fori(0, n_blocks // RING) as turn:
                for slot in range(RING):
                    pool.wait_ge(hi_ready, turn * RING + (slot + 1))
                    rest(slot).then_inc(lo_ready, 1)
            for b in range(n_blocks - n_blocks % RING, n_blocks):
                pool.wait_ge(hi_ready, b + 1)
                rest(b % RING).then_inc(lo_ready, 1)

        @block.scalar
        def _(act):
            steps = [0]

            def step(ins):
                steps[0] += 1
                ins.then_inc(act_step, 1)
                act.wait_ge(act_step, steps[0])

            def w_hi_of(b):
                act.wait_ge(raw_loaded[b % RING], 16 * (b // RING + 1))
                if b >= RING:
                    wait_used(act, b - RING)
                act.copy(w_hi[:, b % RING, :], w_raw[:, b % RING, :]).then_inc(hi_ready, 1)

            prepared = [0]

            def prepare(end_):
                while prepared[0] < end_:
                    w_hi_of(prepared[0])
                    prepared[0] += 1

            def ahead(s):
                until = s
                while until.at + 1 < len(slabs) and (until is s or until.n == 0):
                    until = slabs[until.at + 1]
                prepare(s.first + s.n)
                prepare(min(until.first + until.n, s.first + s.n + RING - 2))

            def bank(s, c):
                act.wait_ge(proj_full, s.bank0 + c + 1)
                return proj[:, s.phys(c), :]

            def fill_hi(pair, base, n, turn=None, gain=None, src=None, ready=None, after=0, k0=0):
                if after:
                    act.wait_ge(proj_full, after)
                sem_, tile = (act_hi_ready, tile_of(pair)) if pair == "act" else (aux_hi_ready, tile_of(pair))
                for k in range(k0, n):
                    hi, _ = tile(k)
                    if turn is not None:
                        act.wait_ge(turned, turn + k + 1)
                        if gain is None:
                            act.copy(hi, work[:, k % 4, :]).then_inc(sem_, 1)
                        else:
                            act.activation(hi, work[:, k % 4, :], ACT.Copy, scale=cols[:, gain + k:gain + k + 1])\
                               .then_inc(sem_, 1)
                    else:
                        act.wait_ge(ready[0], ready[1](k))
                        act.copy(hi, src[:, k, :]).then_inc(sem_, 1)

            def head_roots(src):
                act.preload_act_table_set("sqrt_and_others")
                width = D // 4
                for r in range(16):
                    sq_ = squares[:, r // 2, (r % 2) * width:(r % 2 + 1) * width]
                    ins = act.activation(sq_, src(r), ACT.Square, accum_out=stat[:, r:r + 1])
                step(ins)
                act.activation(root[:], stat[:], ACT.Sqrt, bias=eps_col[:, 0:1], scale=1.0 / width)\
                   .then_inc(head_root_ready, 1)

            def sum_squares(src, m, half, what=0, scratch=None):
                col = (what * 2 + half) * MT + m
                return act.activation(squares[:, col if scratch is None else scratch, :], src[:, m, half * NCOL:(half + 1) * NCOL], ACT.Square,
                                      accum_out=stat[:, col:col + 1])

            def half_squared(src, half, ready):
                for m in range(MT):
                    act.wait_ge(ready[0], ready[1] + m + 1)
                    ins = sum_squares(src, m, half)
                return ins

            def token_root(name, which=ALL):
                act.wait_ge(sums_added, SUMS_AT[name] + which.start + 1)
                act.activation(root[:, which], stat[:, which], ACT.Sqrt, bias=eps_col[:, 0:1], scale=1.0 / D)\
                   .then_inc(root_ready, 1)

            def second_root(src, m=0, n=1, eps=eps_col):
                act.activation(root[:, MT + m:MT + m + n], src, ACT.Sqrt, bias=eps[:, 0:1], scale=1.0 / D)\
                   .then_inc(root2_ready, 1)

            def rest_squared(name, src, s, then=None):
                for m in range(MT):
                    act.wait_ge(proj_free, s.bank0 + m + 1)
                    sum_squares(src, m, 1).then_inc(sums_ready, 1)
                    token_root(name, tile(m))
                    if m == MT - 2:
                        prepare(min(s.first + s.n + 2, n_blocks))
                    if then:
                        then(m)
                prepare(min(s.first + s.n + 4, n_blocks))

            def sqrt_table():
                act.preload_act_table_set("sqrt_and_others")

            sqrt_table()
            for m in range(MT):
                act.wait_ge(x_loaded[m], 16)
                sum_squares(x, m, 0)
                ins = sum_squares(x, m, 1)
            ins.then_inc(sums_ready, 1)
            act.wait_ge(consts_ready, 1)
            token_root("ln1")
            a_slab = by_name["gla_a"][0]
            prepare(a_slab.first + a_slab.n)
            act.wait_ge(cols_ready, 1)
            fill_hi("act", ACT_AT["ln1"], KD, turn=TURN_AT["ln1"], gain=LN1)
            ahead(a_slab)

            act.preload_act_table_set("natural_log_exp_and_others")
            act.wait_ge(gate_full, GLA_HEADS)
            prepare(by_name["gla_q"][0].first + KD)
            for h in range(GLA_HEADS):
                ins = act.activation(gate_l1[:, h, :], work[:, h, :], ACT.Abs, bias=cols[:, BA + h:BA + h + 1])
            step(ins)
            step(act.activation(gate_l1, gate_l1, ACT.Exp, scale=-1.0))
            act.activation(gate_l1, gate_l1, ACT.Ln, bias=1.0).then_inc(gate_l1_ready, 1)
            act.wait_ge(gate_done, 1)
            act.activation(q_dec, gla_b, ACT.Exp, scale=1.0 / GLA_TAU).then_inc(gla_exp, 1)
            act.activation(k_in, gla_b, ACT.Exp, scale=-1.0 / GLA_TAU).then_inc(gla_exp, 1)
            act.activation(decay[:, :].rearrange("p (h c) -> p h c", h=4),
                           gla_b.rearrange("p h (c t) -> p h c t", t=CHUNK)[:, :, :, CHUNK - 1],
                           ACT.Exp, scale=1.0 / GLA_TAU).then_inc(gla_exp, 1)
            act.wait_ge(gla_rest, 1)
            act.activation(k_out, gate_l1, ACT.Exp, scale=1.0 / GLA_TAU).then_inc(gla_exp, 1)
            ahead(by_name["gla_q"][0])
            for g in range(3):
                act.wait_ge(diag_copied, g + 1)
                act.dma_start(diag_dram[g].ap().rearrange("h (p e) -> h p e", p=P),
                              diag_rows[:, DIAG_AT[g]:DIAG_AT[g] + DIAG[g]].unsqueeze(1).to_broadcast([ATT_HEADS, P, DIAG[g]]))\
                   .then_inc(diag_spilled[g], 16)
            ahead(by_name["gla_k"][0])
            for i, s in enumerate(by_name["gla_v"]):
                ahead(s)
                for m in range(MT):
                    act.copy(gla_v[:, m, i * NCOL:(i + 1) * NCOL], bank(s, m)).then_inc(proj_free, 1)
            for g in range(3):
                act.wait_ge(diag_spilled[g], 16)
                act.dma_start(bias[g], bass.AP(diag_dram[g], P - 1, [[DIAG[g] - 1, P], [P * DIAG[g], 4], [1, KEYS[g]]]))\
                   .then_inc(bias_loaded, 16)

            for h in range(GLA_HEADS):
                act.wait_ge(ktok_full, h + 1)
                act.copy(k_tok[:, h, :], work[:, h, :]).then_inc(ktok_ready, 1)
            act.preload_act_table_set("silu_and_others")

            def output_copied(m):
                for b in range(2):
                    act.wait_ge(gla_o_full, 2 * m + b + 1)
                    act.copy(gla_o[:, m, b * 512:(b + 1) * 512], work[:, b, :]).then_inc(gla_o_copied, 1)

            for m in range(MT):
                for s, j in gla_beside[min(2 * m + 2, NCH - 1)]:
                    prepare(s.first + j + 1)
                if m == MT - 1:
                    ahead(by_name["gla_r"][1])
                for s, j in gla_beside[2 * m] + gla_beside[2 * m + 1]:
                    if j == s.n - 1:
                        i = by_name["gla_r"].index(s)
                        for t in range(MT):
                            act.activation(gla_silu[:, t, i * NCOL:(i + 1) * NCOL], bank(s, t), ACT.Silu).then_inc(proj_free, 1)
                output_copied(m)
            act.wait_ge(gla_o_copied, 2 * MT)
            head_roots(lambda r: gla_o[:, r // GLA_HEADS, (r % GLA_HEADS) * GLA_DV:(r % GLA_HEADS + 1) * GLA_DV])

            for g in range(3):
                sq, sk = by_name[f"att_q{g}"][0], by_name[f"att_k{g}"][0]
                ahead(sq)
                ahead(sk)
                for h in range(ATT_HEADS):
                    bank(sk, h)
                    if g and h == 0:
                        act.wait_ge(logits_full, 4 * g)
                    src = proj[:, h, :] if g == 0 else proj[:, h, :].rearrange("p (l z) -> p z l", z=4)
                    dst = att_k[:, h, :] if g == 0 else att_k[:, h, :].rearrange("p (z l) -> p z l", z=4)
                    act.copy(dst, src).then_inc(proj_free, 1)
                for h in range(ATT_HEADS):
                    act.wait_ge(max_ready, 4 * g + h + 1)
                    for z in range(4):
                        c = (g * 4 + z) * 4 + h
                        p_ = att_p[g][:, h, z * KEYS[g]:(z + 1) * KEYS[g]]
                        ins = act.activation(p_, p_, ACT.Exp, bias=att_negmax[:, c:c + 1],
                                             accum_out=att_sum[:, c:c + 1])
                    ins.then_inc(exp_ready, 1)
            act.wait_ge(exp_ready, 12)
            act.activation(att_tmp[:], att_sum[:], ACT.Ln).then_inc(log_ready, 1)

            def values(g):
                s = by_name[f"att_v{g}"][0]
                ahead(s)
                for m in range(MT):
                    act.copy(att_v[g][:, m, :], bank(s, m)).then_inc(proj_free, 1)

            values(0)
            act.wait_ge(lse_shifted, 1)
            act.activation(lse_rows[0:4], lse_rows[0:4], ACT.Exp).then_inc(lse_exp, 1)
            values(1)
            values(2)
            for h in range(ATT_HEADS):
                act.wait_ge(pt_full, 3 * h + 1)
                if h:
                    act.wait_ge(pv_done, 3 * h - 2)
                act.copy(att_pt[0][:, 0:512], work[:, 0, :]).then_inc(pt_copied[0], 1)
                act.copy(att_pt[0][:, 512:7 * P], work[:, 1, 0:3 * P]).then_inc(pt_copied[0], 1)
            act.preload_act_table_set("sigmoid_and_others")
            for i, s in enumerate(by_name["mix_gate"]):
                ahead(s)
                for c in range(4):
                    act.activation(mix[:, 4 * i + c, :], bank(s, c), ACT.Sigmoid).then_inc(proj_free, 1)
            fill_hi("aux0", AUX_AT["att"], 4, src=att_o, ready=(att_o_copied, lambda k: k + 1))
            fill_hi("act", ACT_AT["gla"], KD, turn=TURN_AT["gla"], gain=GN, after=end("mix_gate"))
            for s in [by_name["att_out"][0]] + by_name["gla_out"]:
                ahead(s)
            fill_hi("act", ACT_AT["mix"], 4, src=mix, ready=(mix_ready, lambda k: k + 1), after=end("gla_out"))
            ahead(by_name["att_out"][1])
            fill_hi("act", ACT_AT["mix"], KD, src=mix, ready=(mix_ready, lambda k: k + 1), k0=4)
            mixes = by_name["mix_out"]
            ahead(mixes[0])
            sqrt_table()
            half_squared(x, 0, (proj_free, mixes[0].bank0))
            ahead(mixes[1])
            half_squared(x, 1, (proj_free, mixes[1].bank0)).then_inc(sums_ready, 1)
            token_root("ln2")
            act.dma_start(ple_in, W["p"][0, 0].rearrange("(m p) c -> p m c", p=P)).then_inc(ple_loaded, 16)
            act.dma_start(ln_f_row, bass.AP(W["ln_f"].tensor, 0, [[0, P], [1, D]])).then_inc(ple_loaded, 16)
            fill_hi("act", ACT_AT["ln2"], KD, turn=TURN_AT["ln2"], gain=LN2, after=end("mix_out"))

            def mlp_turned(full, n, par, n0):
                for c in range(4):
                    act.wait_ge(proj_full, full + (c + 1))
                    if n0 + c >= 2:
                        act.wait_ge(squared, n + (c - 1))
                        act.wait_ge(aux_hi_ready, AUX_AT["mlp"] + n + (c - 1))
                    act.activation(relu[:, c % 2, :], proj[:, c, :], ACT.Relu).then_inc(proj_free, 1)
                    act.wait_ge(proj_free, full + (c + 1))
                    act.activation(aux(4 * par + c)[0], relu[:, c % 2, :], ACT.Square).then_inc(aux_hi_ready, 1)

            ups, downs = by_name["mlp_up"], by_name["mlp_down"]
            for g in range(2):
                ahead(ups[g])
                mlp_turned(ups[g].bank0, 4 * g, g, 4 * g)
            s0 = LOOP_SLABS[0]
            prepare(s0.first)
            with act.Fori(0, LOOP_TURNS) as i:
                b = s0.first

                def loop_hi(n):
                    nonlocal b
                    for _ in range(n):
                        act.wait_ge(raw_loaded[b % RING], i * (16 * LOOP_BLOCKS // RING) + 16 * (b // RING + 1))
                        r = b - RING
                        if r < s0.first:
                            rs, rj = blocks[r + LOOP_BLOCKS]
                            full, used = rs.end - LOOP_BANKS, rs.used0 - LOOP_USED
                        else:
                            rs, rj = blocks[r]
                            full, used = rs.end, rs.used0
                        if rj == rs.n - 1:
                            act.wait_ge(proj_full, i * LOOP_BANKS + full)
                        else:
                            act.wait_ge(block_used, i * LOOP_USED + (used + rj + 1))
                        act.copy(w_hi[:, b % RING, :], w_raw[:, b % RING, :]).then_inc(hi_ready, 1)
                        b += 1

                for t in range(2):
                    up = LOOP_SLABS[3 * t]
                    loop_hi(KD)
                    loop_hi(4)
                    mlp_turned(i * LOOP_BANKS + up.bank0, i * 8 + 4 * (2 + t), t, 8)
                    loop_hi(4)
            prepared[0] += LOOP_TURNS * LOOP_BLOCKS

            prepare(downs[-2].first + RING - 2)
            fill_hi("aux0", AUX_AT["p"], 2, turn=TURN_AT["p"])
            ahead(downs[-2])
            sqrt_table()
            half_squared(x, 0, (proj_free, downs[-2].bank0))
            ahead(downs[-1])
            half_squared(x, 1, (proj_free, downs[-1].bank0)).then_inc(sums_ready, 1)
            token_root("ln3")
            for i, s in enumerate(by_name["ple_p"]):
                ahead(s)
                for m in range(MT):
                    act.copy(ple_pp[:, m, i * NCOL:(i + 1) * NCOL], bank(s, m)).then_inc(proj_free, 1)
            fill_hi("act", ACT_AT["ln3"], KD, turn=TURN_AT["ln3"], gain=LN3, after=end("mlp_up"))
            def embedding_gate(s, m, n):
                if n >= 2:
                    act.wait_ge(ple_done, n - 1)
                act.activation(ple_sig[:, n % 2, :], bank(s, m), ACT.Sigmoid).then_inc(proj_free, 1)

            def both_squared(m, half):
                act.wait_ge(ple_done, half * MT + m + 1)
                sum_squares(x, m, half)
                act.wait_ge(x_gain_ready, half * MT + m + 1)
                return sum_squares(ple_pp, m, half, what=1)

            act.preload_act_table_set("sigmoid_and_others")
            first, second = by_name["ple_gate"]
            ahead(first)
            for m in range(MT):
                embedding_gate(first, m, m)
            prepare(second.first + second.n)
            for m in range(MT):
                both_squared(m, 0)
            for m in range(MT):
                if m == MT - 1:
                    prepare(second.first + second.n + 2)
                embedding_gate(second, m, MT + m)
                if m == MT - 1:
                    sqrt_table()
                ins = both_squared(m, 1)
            ins.then_inc(sums_ready, 1)
            act.wait_ge(scale_ready, 1)
            second_root(scale[:], 0, MT, eps=eps_sq_col)
            token_root("ln_f")
            prepare(second.first + second.n + 5)
            fill_hi("act", ACT_AT["pre0"], KD, turn=TURN_AT["pre0"], gain=PRE, after=end("ple_gate"))

            ahead(by_name["lstm_if"][0])
            act.preload_act_table_set("natural_log_exp_and_others")
            act.wait_ge(lstm_if_copied, 1)
            act.dma_start(row["f"], if_rows[LSTM_HEADS:]).then_inc(lstm_f_moved, 16)
            act.wait_ge(lstm_f_ready, 1)
            step(act.activation(row["l1"], row["f"], ACT.Abs))
            step(act.activation(row["l1"], row["l1"], ACT.Exp, scale=-1.0))
            act.activation(row["l1"], row["l1"], ACT.Ln, bias=1.0).then_inc(lstm_l1, 1)
            act.wait_ge(lstm_rows, 1)
            act.activation(row["inter"], row["inter"], ACT.Exp).then_inc(lstm_exps, 1)
            act.activation(row["wa"], row["wa"], ACT.Exp).then_inc(lstm_exps, 1)
            act.activation(row["emt"], row["emt"], ACT.Exp, scale=-1.0).then_inc(lstm_exps, 1)
            act.activation(lstm_dec[:], lstm_dec[:], ACT.Exp).then_inc(lstm_exps, 1)
            conv_slabs = by_name["lstm_q"] + by_name["lstm_k"]

            def convolved(n):
                for c in range(4):
                    act.wait_ge(conv_done, 4 * n + c + 1)
                    t = (lstm_q, lstm_k)[n // 2][:, 4 * (n % 2) + c, :]
                    act.activation(t, t, ACT.Silu).then_inc(conv_silu, 1)

            for n, s in enumerate(conv_slabs):
                ahead(s)
                for c in range(4):
                    if n:
                        act.wait_ge(conv_done, 4 * (n - 1) + c + 1)
                    act.copy(conv_raw[:, c, :], bank(s, c)).then_inc(proj_free, 1)
                if n:
                    convolved(n - 1)
            for s, j in heads_beside[0] + heads_beside[1]:
                prepare(s.first + j + 1)
            convolved(3)
            v4 = lstm_v.rearrange("p m (h c) -> p m h c", h=LSTM_HEADS)
            for h in range(LSTM_HEADS):
                if h + 1 < LSTM_HEADS:
                    for s, j in heads_beside[h + 2]:
                        prepare(s.first + j + 1)
                else:
                    ahead(by_name["lstm_v"][1])
                act.wait_ge(w_masked, h + 1)
                for m in range(MT):
                    w_ = lstm_w[:, h % 2, m * P:(m + 1) * P]
                    ins = act.activation(w_, w_, ACT.Exp, bias=lstm_cols[:, m * 4 + h:m * 4 + h + 1])
                ins.then_inc(w_ready, 1)
                for s, j in heads_beside[h + 1]:
                    if j == s.n - 1:
                        i = by_name["lstm_v"].index(s)
                        for m in range(MT):
                            act.copy(v4[:, m, 2 * i:2 * i + 2, 0:LSTM_HD],
                                     bank(s, m).rearrange("p (h c) -> p h c", h=2)).then_inc(proj_free, 1)
            n = 0
            act.preload_act_table_set("sigmoid_and_others")
            for s in by_name["lstm_o"]:
                ahead(s)
                for m in range(MT):
                    if n >= 2:
                        act.wait_ge(lstm_gated, n - 1)
                    act.activation(gate_tmp[:, n % 2, :], bank(s, m), ACT.Sigmoid).then_inc(proj_free, 1)
                    n += 1
            act.wait_ge(lstm_gated, 2 * MT)
            head_roots(lambda r: lstm_h[:, r // LSTM_HEADS, (r % LSTM_HEADS) * LSTM_HD:(r % LSTM_HEADS + 1) * LSTM_HD])
            n = 0
            act.preload_act_table_set("silu_and_others")
            for s in by_name["lstm_z"]:
                ahead(s)
                for m in range(MT):
                    if n >= 2:
                        act.wait_ge(ya_ready, n - 1)
                    act.activation(gate_tmp[:, n % 2, :], bank(s, m), ACT.Silu).then_inc(proj_free, 1)
                    n += 1

            ahead(by_name["sb_q"][0])
            fill_hi("aux", AUX_AT["ya"], KD, turn=TURN_AT["ya"], gain=HN)
            ahead(by_name["sb_k"][0])
            ahead(by_name["sb_v"][0])

            def log_terms(u):
                nk = (u % MT + 1) * P
                l_ = sb_l[:, u % 2, 0:nk]
                act.wait_ge(sb_z_full, u + 1)
                if u >= 2:
                    act.wait_ge(sb_at_full, u - 1)
                act.activation(l_, work[:, u % 2, 0:nk], ACT.Abs).then_inc(sb_abs, 1)
                act.wait_ge(sb_abs, u + 1)
                step(act.activation(l_, l_, ACT.Exp, scale=-1.0))
                act.activation(l_, l_, ACT.Ln, bias=1.0).then_inc(sb_l1, 1)

            def weights(u):
                act.wait_ge(sb_t, u + 1)
                l_ = sb_l[:, u % 2, 0:(u % MT + 1) * P]
                act.activation(l_, l_, ACT.Exp).then_inc(sb_a, 1)

            def weights_copied(u):
                nk = (u % MT + 1) * P
                act.wait_ge(sb_at_full, u + 1)
                if u >= 2:
                    act.wait_ge(sb_o_full, u - 1)
                act.copy(sb_at[:, u % 2, 0:nk], work[:, 2, 0:nk]).then_inc(sb_at_ready, 1)

            def values_copied(half):
                s = by_name["sb_v"][half]
                for m in range(MT):
                    act.copy(sb_v[half][:, m, :], bank(s, m)).then_inc(proj_free, 1)

            def gates(i):
                s = by_name["sb_z"][i]
                act.wait_ge(sb_o_full, SB_UNITS // 2)
                for m in range(MT):
                    if i:
                        act.wait_ge(yb_ready, m + 1)
                    act.activation(sb_gate[:, m, :], bank(s, m), ACT.Silu).then_inc(proj_free, 1)
                act.preload_act_table_set("natural_log_exp_and_others")

            values_copied(0)
            act.preload_act_table_set("natural_log_exp_and_others")
            for i in range(SB_STEPS + 1):
                if 2 <= i < SB_STEPS:
                    weights_copied(i - 2)
                if 1 <= i <= SB_UNITS:
                    weights(i - 1)
                if i < SB_UNITS:
                    log_terms(i)
                for s, j in [x_ for later in beside[i:i + 3] for x_ in later]:
                    prepare(s.first + j + 1)
                for s, j in beside[i]:
                    if j == s.n - 1 and s is by_name["sb_v"][1]:
                        values_copied(1)
                    elif j == s.n - 1 and s.name == "sb_z":
                        gates(by_name["sb_z"].index(s))
            ahead(by_name["even_out0"][1])
            act.wait_ge(yb_ready, 2 * MT)
            for r in range(2):
                act.dma_start(post_row[r], bass.AP(W["post_norm_g_2"].tensor, r * D, [[0, P], [1, D]]))\
                   .then_inc(post_loaded, 16)
            fill_hi("act", ACT_AT["yb"], KD, turn=TURN_AT["yb"], after=end("sb_z"))
            def layer_squared(name, slabs_, then=None):
                ahead(slabs_[0])
                sqrt_table()
                prepare(slabs_[1].first + slabs_[1].n)
                half_squared(y, 0, (proj_free, slabs_[0].bank0))
                rest_squared(name, y, slabs_[1], then)

            def next_squared(m):
                act.wait_ge(x_half, m + 1)
                sum_squares(x, m, 0, 1, scratch=m)
                act.wait_ge(x_final, MT + m + 1)
                sum_squares(x, m, 1, 1, scratch=MT + m).then_inc(sums2_ready, 1)
                act.wait_ge(sums2_added, m + 1)
                second_root(stat[:, 2 * MT + m:2 * MT + m + 1], m)

            layer_squared("post0", by_name["even_out1"], next_squared)
            fill_hi("act", ACT_AT["pre1"], 4, turn=TURN_AT["pre1"], gain=PRE + 8, after=end("even_out1"))
            prepare(by_name["odd_z"][0].first + KD)
            fill_hi("act", ACT_AT["pre1"], KD, turn=TURN_AT["pre1"], gain=PRE + 8, k0=4)

            act.preload_act_table_set("silu_and_others")
            for i, s in enumerate(by_name["odd_z"]):
                ahead(s)
                for c in range(4):
                    act.activation(odd_z[:, 4 * i + c, :], bank(s, c), ACT.Silu).then_inc(proj_free, 1)
            def pool_hi_of(n):
                act.wait_ge(pool_done, n + 1)
                act.copy(aux(n % 8)[0], pooled[:, n % 4, :]).then_inc(aux_hi_ready, 1)

            for g, s in enumerate(by_name["pool_in"]):
                ahead(s)
                for c in range(4):
                    if g:
                        act.wait_ge(pool_done, 4 * (g - 1) + c + 1)
                    act.copy(pool_raw[:, c, POOL_PAD:PADDED], bank(s, c)).then_inc(proj_free, 1)
                if g + 1 == len(POOL_WINDOWS):
                    fill_hi("act", ACT_AT["mixa"], KD, src=odd_z, after=end("pool_in"),
                            ready=(proj_free, lambda k: by_name["pool_mix"][k // 4].bank0 + k % 4 + 1))
                if g:
                    ahead(by_name["pool_mix"][g - 1])
                for c in range(4):
                    pool_hi_of(4 * g + c)
                    if c == 1 and g + 1 < len(POOL_WINDOWS):
                        prepare(by_name["pool_in"][g + 1].first + KD)
            ahead(by_name["odd_out0"][0])
            ahead(by_name["pool_mix"][3])
            fill_hi("aux", AUX_AT["mixb"], KD, src=odd_z[:, KD:2 * KD, :], after=end("pool_mix"),
                    ready=(proj_free, lambda k: by_name["pool_mix"][2 + k // 4].bank0 + k % 4 + 1))
            ahead(by_name["odd_out0"][1])
            layer_squared("post1", by_name["odd_out1"])

        @block.vector
        def _(vec):
            steps = [0]

            def step(ins):
                steps[0] += 1
                ins.then_inc(vec_step, 1)
                vec.wait_ge(vec_step, steps[0])

            def bank(s, c):
                vec.wait_ge(proj_full, s.bank0 + c + 1)
                return proj[:, s.phys(c), :]

            def fill_lo(pair, base, n, turn=False, gain=None, src=None, k0=0):
                hi_sem, sem_ = (act_hi_ready, act_ready) if pair == "act" else (aux_hi_ready, aux_ready)
                for k in range(k0, n):
                    hi, lo = tile_of(pair)(k)
                    vec.wait_ge(hi_sem, base + k + 1)
                    v = work[:, k % 4, :] if turn else src[:, k, :]
                    if gain is None:
                        vec.tensor_tensor(lo, v, hi.bitcast(F32), ALU.subtract).then_inc(sem_, 1)
                    else:
                        vec.scalar_tensor_tensor(lo, v, cols[:, gain + k:gain + k + 1], hi.bitcast(F32),
                                                 ALU.mult, ALU.subtract).then_inc(sem_, 1)

            def head_scales(n):
                vec.wait_ge(head_root_ready, n)
                step(vec.reciprocal(rstd[:], root[:]))

            def token_scale(name, which=ALL):
                at = SUMS_AT[name] + which.start + 1
                vec.wait_ge(sums_ready, at)
                vec.tensor_tensor(stat[:, which], stat[:, which], stat[:, MT + which.start:MT + which.stop], ALU.add)\
                   .then_inc(sums_added, 1)
                vec.wait_ge(root_ready, at)
                step(vec.reciprocal(rstd[:, which], root[:, which]))

            def second_scale(name, which=ALL):
                vec.wait_ge(root2_ready, SUMS2_AT[name] + which.start + 1)
                second = slice(MT + which.start, MT + which.stop)
                step(vec.reciprocal(rstd[:, second], root[:, second]))

            def diagonal(by, m):
                vec.tensor_scalar(root_diag[:, m, :], ident[:], by, None, ALU.mult).then_inc(scaled, 1)

            def scale_rest(dst, src, by, m):
                vec.tensor_scalar(dst[:, m, :], src[:, m, DIAG_TILES * P:], by, None, ALU.mult).then_inc(x_scaled, 1)

            def scaled_tokens(name):
                token_scale(name)
                for m in range(MT):
                    diagonal(rstd[:, m:m + 1], m)

            def scaled_rest():
                for m in range(MT):
                    scale_rest(scaled_x, x, rstd[:, m:m + 1], m)

            def add_to_x(s, i, norm=None):
                for m in range(MT):
                    xm = x[:, m, i * NCOL:(i + 1) * NCOL]
                    vec.tensor_tensor(xm, xm, bank(s, m), ALU.add).then_inc(proj_free, 1)
                if norm:
                    scaled_tokens(norm)
                    scaled_rest()

            scaled_tokens("ln1")
            vec.wait_ge(params_loaded, 16 * 15)
            vec.memset(rel_rows[REL_BUCKETS:REL_BUCKETS + 1, :], NEG).then_inc(rel_ready, 1)
            vec.wait_ge(cols_full, 1)
            vec.tensor_copy(cols[:, 0:CONV_AT], work[:, 3, 0:CONV_AT])
            vec.tensor_copy(cols[:, CONV_AT:CONV_AT + 64], work[:, 3, P:P + 64]).then_inc(cols_ready, 1)
            scaled_rest()
            vec.wait_ge(cols_ready, 1)
            fill_lo("act", ACT_AT["ln1"], KD, turn=True, gain=LN1)

            step(vec.memset(reset, 1.0))
            step(vec.memset(reset.rearrange("p (c t) -> p c t", t=CHUNK)[:, :, 0:1], 0.0))
            vec.tensor_copy(gla_a[0:GLA_RANK, :], bank(by_name["gla_a"][0], 0)[0:GLA_RANK, :]).then_inc(proj_free, 1)
            vec.wait_ge(gate_l1_ready, 1)
            for h in range(GLA_HEADS):
                ins = vec.tensor_scalar(gate_min[:, h, :], work[:, h, :], cols[:, BA + h:BA + h + 1], 0.0, ALU.add, ALU.min)
            step(ins)
            step(vec.tensor_tensor(gate_min, gate_min, gate_l1, ALU.subtract))
            for h in range(GLA_HEADS):
                ins = vec.tensor_tensor_scan(gla_b[:, h, :], reset, gate_min[:, h, :], 0.0, ALU.mult, ALU.add)
            ins.then_inc(gate_done, 1)
            vec.wait_ge(gate_done, 1)
            b_chunks = gla_b.rearrange("p h (c t) -> p (h c) t", t=CHUNK)
            vec.tensor_tensor(gate_l1.rearrange("p h (c t) -> p (h c) t", t=CHUNK),
                              b_chunks[:, :, CHUNK - 1:CHUNK].to_broadcast([P, GLA_HEADS * NCH, CHUNK]),
                              b_chunks, ALU.subtract).then_inc(gla_rest, 1)
            vec.wait_ge(gate_full, GLA_HEADS)
            step(vec.memset(gla_att, 0.0))
            s = by_name["gla_q"][0]
            vec.wait_ge(gla_exp, 1)
            for h in range(GLA_HEADS):
                vec.scalar_tensor_tensor(q_dec[:, h, :], bank(s, h), GLA_DK ** -0.5, q_dec[:, h, :],
                                         ALU.mult, ALU.mult).then_inc(proj_free, 1)
            for g in range(3):
                vec.wait_ge(diag_full, g + 1)
                vec.tensor_copy(diag_rows[:, DIAG_AT[g]:DIAG_AT[g] + DIAG[g]], work[0:ATT_HEADS, 1 + g, 0:DIAG[g]])\
                   .then_inc(diag_copied, 1)
            s = by_name["gla_k"][0]
            vec.wait_ge(gla_exp, 4)
            for h in range(GLA_HEADS):
                k_ = bank(s, h)
                vec.tensor_tensor(k_in[:, h, :], k_in[:, h, :], k_, ALU.mult)
                vec.tensor_tensor(k_out[:, h, :], k_out[:, h, :], k_, ALU.mult).then_inc(proj_free, 1)
            for h in range(GLA_HEADS):
                vec.wait_ge(gla_att_full, h + 1)
                vec.copy_predicated(gla_att[:, h, :].rearrange("p (m t) -> p m t", m=MT),
                                    chunk_ok[:].bitcast(U32).unsqueeze(1).to_broadcast([P, MT, P]),
                                    work[:, h, :].rearrange("p (m t) -> p m t", m=MT)).then_inc(gla_att_ready, 1)
            for n in range(NCH - 1):
                for h in range(GLA_HEADS):
                    if h % 2 == 0:
                        vec.wait_ge(gla_upd_full, 2 * n + h // 2 + 1)
                    upd = work[:, 2 + h // 2, (h % 2) * GLA_DV:(h % 2 + 1) * GLA_DV]
                    new = gla_state[:, (n + 1) % 2, h, :]
                    if n == 0:
                        vec.tensor_copy(new, upd).then_inc(gla_state_ready, 1)
                    else:
                        vec.wait_ge(gla_state_ready, 4 * (n - 1) + h + 1)
                        vec.scalar_tensor_tensor(new, gla_state[:, n % 2, h, :], decay[:, h * NCH + n:h * NCH + n + 1],
                                                 upd, ALU.mult, ALU.add).then_inc(gla_state_ready, 1)
            head_scales(1)
            for i, s in enumerate(by_name["gla_r"]):
                for m in range(MT):
                    vec.wait_ge(proj_free, s.bank0 + m + 1)
                    for h in (2 * i, 2 * i + 1):
                        own = slice(h * GLA_DV, (h + 1) * GLA_DV)
                        ins = vec.scalar_tensor_tensor(gla_o[:, m, own], gla_o[:, m, own], rstd[:, m * 4 + h:m * 4 + h + 1],
                                                       gla_silu[:, m, own], ALU.mult, ALU.mult)
                    ins.then_inc(gla_gated, 1)

            vec.wait_ge(bias_loaded, 16 * 3)
            vec.wait_ge(gla_gated, 2 * MT)
            p0 = att_p[0].rearrange("p h (z k) -> p h z k", z=4)
            vec.memset(p0[:, :, 0, 0:P], NEG)
            for g in range(3):
                s = by_name[f"att_q{g}"][0]
                for h in range(ATT_HEADS):
                    src = bank(s, h)
                    if g and h == 0:
                        vec.wait_ge(logits_full, 4 * g)
                    dst = att_q[:, h, :]
                    if g:
                        src, dst = src.rearrange("p (l z) -> p z l", z=4), dst.rearrange("p (z l) -> p z l", z=4)
                    vec.tensor_copy(dst, src).then_inc(proj_free, 1)
                for h in range(ATT_HEADS):
                    vec.wait_ge(logits_full, 4 * g + h + 1)
                    b_ = bias[g][:, h, :]
                    p_ = att_p[g][:, h, :].rearrange("p (z k) -> p z k", z=4)

                    def biased_logits(dst, src, b):
                        return vec.scalar_tensor_tensor(dst, src, HD ** -0.5, b, ALU.mult, ALU.add)

                    if g == 0:
                        b0 = 2 * (h % 2)
                        biased_logits(p_[:, 0, P:2 * P], work[:, b0, 0:P], b_[:, P:2 * P])
                        biased_logits(p_[:, 1, :], work[:, b0, 2 * P:4 * P], b_)
                        ins = biased_logits(p_[:, 2:4, :], work[:, b0 + 1, :].rearrange("p (z k) -> p z k", z=2),
                                            b_.unsqueeze(1).to_broadcast([P, 2, 2 * P]))
                    else:
                        ins = biased_logits(p_, work[:, h, :].rearrange("p (z k) -> p z k", z=4),
                                            b_.unsqueeze(1).to_broadcast([P, 4, P]))
                    ins.then_inc(biased, 1)
                    vec.wait_ge(biased, 4 * g + h + 1)
                    nm = att_negmax[:, 16 * g:16 * g + 16].rearrange("p (z h) -> p z h", z=4)[:, :, h]
                    step(vec.tensor_reduce(nm, p_, AX, ALU.max))
                    vec.tensor_scalar(nm, nm, -1.0, None, ALU.mult).then_inc(max_ready, 1)
            vec.wait_ge(log_ready, 1)
            vec.tensor_tensor(att_tmp[:], att_tmp[:], att_negmax[:], ALU.subtract).then_inc(lse_ready, 1)
            for g in range(3):
                vec.wait_ge(lse_full, g + 1)
                src, dst = work[0:4, g, :], lse_rows[0:4, g, :]
                if g:
                    src, dst = src.rearrange("p (z l) -> p z l", z=4), dst.rearrange("p (l z) -> p z l", z=4)
                step(vec.tensor_copy(dst, src))
            top_ = lse_max[0:4, :]
            step(vec.tensor_tensor(top_, lse_rows[0:4, 0, :], lse_rows[0:4, 1, :], ALU.max))
            step(vec.tensor_tensor(top_, top_, lse_rows[0:4, 2, :], ALU.max))
            vec.tensor_tensor(lse_rows[0:4], lse_rows[0:4], top_.unsqueeze(1).to_broadcast([4, 3, SEQ]), ALU.subtract)\
               .then_inc(lse_shifted, 1)
            vec.wait_ge(lse_exp, 1)
            step(vec.tensor_tensor(top_, lse_rows[0:4, 0, :], lse_rows[0:4, 1, :], ALU.add))
            step(vec.tensor_tensor(top_, top_, lse_rows[0:4, 2, :], ALU.add))
            step(vec.reciprocal(top_, top_))
            vec.tensor_tensor(lse_rows[0:4], lse_rows[0:4], top_.unsqueeze(1).to_broadcast([4, 3, SEQ]), ALU.mult)\
               .then_inc(share_ready, 1)
            step(vec.reciprocal(att_coef[:], att_sum[:]))
            vec.wait_ge(share_full, 1)
            step(vec.tensor_tensor(att_coef[:], att_coef[:], work[:, 3, 0:48], ALU.mult))
            for h in range(ATT_HEADS):
                for g in range(3):
                    for z in range(4):
                        p_ = att_p[g][:, h, z * KEYS[g]:(z + 1) * KEYS[g]]
                        c = (g * 4 + z) * 4 + h
                        ins = vec.tensor_scalar(p_, p_, att_coef[:, c:c + 1], None, ALU.mult)
                    ins.then_inc(p_scaled, 1)
            for h in range(ATT_HEADS):
                for g in (1, 2):
                    vec.wait_ge(pt_full, 3 * h + g + 1)
                    if h:
                        vec.wait_ge(pv_done, 3 * (h - 1) + g + 1)
                    vec.tensor_copy(att_pt[g], work[:, 2 if g == 1 else 0, :]).then_inc(pt_copied[g], 1)
                vec.wait_ge(pv_done, 3 * h + 3)
                vec.tensor_copy(att_o[:, h, :], work[:, 3, :]).then_inc(att_o_copied, 1)
            fill_lo("aux0", AUX_AT["att"], 4, src=att_o)
            fill_lo("act", ACT_AT["gla"], KD, turn=True, gain=GN)
            def through_gate(s, first):
                for c in range(4):
                    t = mix[:, first + c, :]
                    vec.tensor_tensor(t, t, bank(s, c), ALU.mult).then_inc(proj_free, 1)

            def mixed(s, first):
                for c in range(4):
                    t, u = mix[:, first + c, :], mix[:, KD + first + c, :]
                    vec.wait_ge(proj_free, s.bank0 + c + 1)
                    vec.tensor_tensor(t, t, u, ALU.add).then_inc(mix_ready, 1)

            (att0, att1), (gla0, gla1) = by_name["att_out"], by_name["gla_out"]
            through_gate(att0, KD)
            through_gate(gla0, 0)
            mixed(gla0, 0)
            through_gate(gla1, 4)
            fill_lo("act", ACT_AT["mix"], 4, src=mix)
            through_gate(att1, KD + 4)
            mixed(att1, 4)
            fill_lo("act", ACT_AT["mix"], KD, src=mix, k0=4)
            for i, s in enumerate(by_name["mix_out"]):
                add_to_x(s, i, "ln2" if i else None)

            fill_lo("act", ACT_AT["ln2"], KD, turn=True, gain=LN2)
            ups, downs = by_name["mlp_up"], by_name["mlp_down"]

            def mlp_rest(full, n, par, n0):
                for c in range(4):
                    vec.wait_ge(proj_free, full + (c + 1))
                    if n0 + c >= 2:
                        vec.wait_ge(aux_ready, AUX_AT["mlp"] + n + (c - 1))
                    vec.tensor_tensor(relu_sq[:, c % 2, :], relu[:, c % 2, :], relu[:, c % 2, :], ALU.mult).then_inc(squared, 1)
                    vec.wait_ge(squared, n + (c + 1))
                    vec.wait_ge(aux_hi_ready, AUX_AT["mlp"] + n + (c + 1))
                    hi, lo = aux(4 * par + c)
                    vec.tensor_tensor(lo, relu_sq[:, c % 2, :], hi.bitcast(F32), ALU.subtract).then_inc(aux_ready, 1)

            def mlp_add(full, i):
                for m in range(MT):
                    xm = x[:, m, i * NCOL:(i + 1) * NCOL]
                    vec.wait_ge(proj_full, full + (m + 1))
                    vec.tensor_tensor(xm, xm, proj[:, m, :], ALU.add).then_inc(proj_free, 1)

            mlp_rest(ups[0].bank0, 0, 0, 0)
            mlp_rest(ups[1].bank0, 4, 1, 4)
            for i in range(2):
                mlp_add(downs[i].bank0, i)
            with vec.Fori(0, LOOP_TURNS) as turn:
                for t in range(2):
                    up, d0, d1 = LOOP_SLABS[3 * t:3 * t + 3]
                    mlp_rest(turn * LOOP_BANKS + up.bank0, turn * 8 + 4 * (2 + t), t, 8)
                    mlp_add(turn * LOOP_BANKS + d0.bank0, 0)
                    mlp_add(turn * LOOP_BANKS + d1.bank0, 1)
            fill_lo("aux0", AUX_AT["p"], 2, turn=True)
            add_to_x(downs[-2], 0)
            add_to_x(downs[-1], 1, "ln3")

            fill_lo("act", ACT_AT["ln3"], KD, turn=True, gain=LN3)
            n = 0
            for i, s in enumerate(by_name["ple_gate"]):
                for m in range(MT):
                    vec.wait_ge(proj_free, s.bank0 + m + 1)
                    g_ = ple_sig[:, n % 2, :]
                    xm = x[:, m, i * NCOL:(i + 1) * NCOL]
                    step(vec.tensor_tensor(g_, g_, ple_pp[:, m, i * NCOL:(i + 1) * NCOL], ALU.mult))
                    vec.tensor_tensor(xm, xm, g_, ALU.add).then_inc(ple_done, 1)
                    vec.wait_ge(ple_done, n + 1)
                    vec.tensor_tensor(ple_pp[:, m, i * NCOL:(i + 1) * NCOL], xm, ln_f_row[:, i * NCOL:(i + 1) * NCOL], ALU.mult)\
                       .then_inc(x_gain_ready, 1)
                    n += 1
            at = SUMS_AT["ln_f"] + 1
            vec.wait_ge(sums_ready, at)
            vec.tensor_tensor(stat[:, ALL], stat[:, ALL], stat[:, MT:2 * MT], ALU.add).then_inc(sums_added, 1)
            step(vec.tensor_tensor(scale[:], stat[:, 2 * MT:3 * MT], stat[:, 3 * MT:4 * MT], ALU.add))
            vec.wait_ge(sums_added, at)
            vec.scalar_tensor_tensor(scale[:], stat[:, ALL], EPS, scale[:], ALU.mult, ALU.add).then_inc(scale_ready, 1)
            second_scale("pre0")
            for m in range(MT):
                diagonal(rstd[:, MT + m:MT + m + 1], m)
            for m in range(MT):
                scale_rest(scaled_x, ple_pp, rstd[:, MT + m:MT + m + 1], m)
            fill_lo("act", ACT_AT["pre0"], 3, turn=True, gain=PRE)
            vec.wait_ge(root_ready, at)
            step(vec.reciprocal(rstd[:, ALL], root[:, ALL]))
            for m in range(MT):
                fill_lo("act", ACT_AT["pre0"], 4 + m, turn=True, gain=PRE, k0=3 + m)
                vec.tensor_scalar(x[:, m, :], ple_pp[:, m, :], rstd[:, m:m + 1], None, ALU.mult).then_inc(x_final, 1)
            fill_lo("act", ACT_AT["pre0"], KD, turn=True, gain=PRE, k0=3 + MT)

            H = LSTM_HEADS
            vec.tensor_copy(if_rows, bank(by_name["lstm_if"][0], 0)[0:2 * H, :]).then_inc(lstm_if_copied, 1)
            vec.wait_ge(lstm_if_copied, 1)
            vec.tensor_scalar(row["i"], if_rows[0:H], lstm_b[:, 0:1], None, ALU.add).then_inc(proj_free, 1)
            vec.wait_ge(lstm_f_moved, 16)
            vec.tensor_scalar(row["f"], row["f"], lstm_b[:, 1:2], None, ALU.add).then_inc(lstm_f_ready, 1)
            vec.wait_ge(lstm_f_ready, 1)
            step(vec.tensor_scalar(row["min"], row["f"], 0.0, None, ALU.min))
            step(vec.memset(lstm_reset, 1.0))
            step(vec.memset(lstm_reset.rearrange("p (m t) -> p m t", m=MT)[:, :, 0:1], 0.0))
            step(vec.memset(lstm_m[:, 0:1], 0.0))
            vec.wait_ge(lstm_l1, 1)
            step(vec.tensor_tensor(row["min"], row["min"], row["l1"], ALU.subtract))
            step(vec.tensor_tensor_scan(row["b"], lstm_reset[0:H, :], row["min"], 0.0, ALU.mult, ALU.add))
            step(vec.tensor_tensor(row["a"], row["i"], row["b"], ALU.subtract))
            for c in range(MT):
                t0, t1 = c * P, (c + 1) * P
                step(vec.tensor_tensor_scan(row["e"][:, t0:t1], row["a"][:, t0:t1], row["a"][:, t0:t1],
                                            lstm_m[:, c:c + 1], ALU.max, ALU.max))
                step(vec.tensor_tensor(lstm_m[:, c + 1:c + 2], row["b"][:, t1 - 1:t1], row["e"][:, t1 - 1:t1], ALU.add))

            def chunks(r):
                return row[r].rearrange("p (m t) -> p m t", m=MT)

            e_last = chunks("e")[:, :, P - 1:P]
            vec.tensor_scalar(row["neg_e"], row["e"], -1.0, None, ALU.mult)
            vec.tensor_tensor(chunks("inter"), lstm_m[:, 0:MT].unsqueeze(2).to_broadcast([H, MT, P]), chunks("e"), ALU.subtract)
            vec.tensor_tensor(chunks("wa"), chunks("a"), e_last.to_broadcast([H, MT, P]), ALU.subtract)
            vec.tensor_tensor(row["emt"], row["b"], row["e"], ALU.add)
            vec.tensor_tensor(lstm_dec[:], lstm_m[:, 0:MT], e_last[:, :, 0], ALU.subtract).then_inc(lstm_rows, 1)
            for at, (dst, name) in enumerate(((lstm_q, "lstm_q"), (lstm_k, "lstm_k"))):
                if at:
                    vec.wait_ge(lstm_cols_full, 1)
                    vec.tensor_copy(lstm_cols[:], work[:, 0, 0:48]).then_inc(lstm_cols_ready, 1)
                    vec.wait_ge(lstm_cols_full, 2)
                    vec.tensor_copy(decay[:, 0:MT * H], work[:, 1, 0:MT * H]).then_inc(lstm_cols_ready, 1)
                    vec.wait_ge(lstm_cols_ready, 2)
                for i, s in enumerate(by_name[name]):
                    for c in range(4):
                        u, o_ = conv_raw[:, c, :], dst[:, 4 * i + c, :]
                        vec.wait_ge(proj_free, s.bank0 + c + 1)
                        tap = [cols[:, CONV_AT + k * 16 + 8 * at + 4 * i + c:CONV_AT + k * 16 + 8 * at + 4 * i + c + 1]
                               for k in range(CONV)]
                        step(vec.tensor_scalar(o_, u, tap[CONV - 1], None, ALU.mult))
                        for back in range(1, CONV):
                            ins = vec.scalar_tensor_tensor(o_[:, back:], u[:, 0:SEQ - back], tap[CONV - 1 - back], o_[:, back:],
                                                           ALU.mult, ALU.add)
                            if back < CONV - 1:
                                step(ins)
                        ins.then_inc(conv_done, 1)
            va = lstm_v.rearrange("p m (h c) -> p m h c", h=H)
            vec.wait_ge(conv_done, 16)
            step(vec.memset(va[:, :, :, LSTM_HD:LSTM_HD + 1], 1.0))
            for h in range(H):
                vec.wait_ge(neg_e_full, h + 1)
                vec.tensor_tensor(lstm_w[:, h % 2, :].rearrange("p (m t) -> p m t", m=MT),
                                  work[:, 1, :].rearrange("p (m t) -> p m t", m=MT),
                                  upto_neg[:].unsqueeze(1).to_broadcast([P, MT, P]), ALU.add).then_inc(w_masked, 1)
                vec.wait_ge(qk_full, h + 1)
                vec.wait_ge(inter_full, h + 1)
                for kk in range(2):
                    q_ = lstm_q[:, 2 * h + kk, :]
                    ins = vec.tensor_tensor(q_, q_, work[:, 2, :], ALU.mult)
                ins.then_inc(q_inter, 1)
                for pair in range(2):
                    vec.wait_ge(lstm_kt_full, 2 * h + pair + 1)
                    for mm in range(2):
                        m = 2 * pair + mm
                        ins = vec.tensor_scalar(k_wa[:, m, h * LSTM_HD:(h + 1) * LSTM_HD],
                                                work[:, 3, mm * LSTM_HD:(mm + 1) * LSTM_HD],
                                                lstm_cols[:, 16 + m * 4 + h:16 + m * 4 + h + 1], LSTM_HD ** -0.5,
                                                ALU.mult, ALU.mult)
                    ins.then_inc(lstm_kt_ready, 1)
                vec.wait_ge(w_ready, h + 1)
                vec.scalar_tensor_tensor(lstm_s[:, h, :], work[:, 0, :], LSTM_HD ** -0.5, lstm_w[:, h % 2, :],
                                         ALU.mult, ALU.mult).then_inc(s_ready, 1)
            core = by_name["lstm_core"][0]
            for m in range(MT):
                for h in range(H):
                    vec.wait_ge(proj_full, core.bank0 + 4 * m + h + 1)
                    den = lstm_den[:, m * 4 + h:m * 4 + h + 1]
                    raw = proj[:, h, LSTM_HD:LSTM_HD + 1]
                    step(vec.scalar_tensor_tensor(den, raw, -1.0, lstm_cols[:, 32 + m * 4 + h:32 + m * 4 + h + 1],
                                                  ALU.mult, ALU.max))
                    step(vec.tensor_tensor(den, raw, den, ALU.max))
                    step(vec.reciprocal(den, den))
                    vec.tensor_scalar(lstm_h[:, m, h * LSTM_HD:(h + 1) * LSTM_HD], proj[:, h, 0:LSTM_HD], den, None, ALU.mult)\
                       .then_inc(proj_free, 1)
                    for hk in (2 * h, 2 * h + 1) if m < MT - 1 else ():
                        vec.wait_ge(lstm_upd_full, 8 * m + hk + 1)
                        c_ = lstm_c[:, hk, :]
                        upd = work[:, hk % 4, 0:LSTM_HD + 1]
                        if m == 0:
                            vec.tensor_copy(c_, upd).then_inc(lstm_c_ready, 1)
                        else:
                            vec.wait_ge(lstm_c_ready, 8 * (m - 1) + hk + 1)
                            d = (hk // 2) * MT + m
                            vec.scalar_tensor_tensor(c_, c_, decay[:, d:d + 1], upd, ALU.mult, ALU.add).then_inc(lstm_c_ready, 1)
            n = 0
            for i, s in enumerate(by_name["lstm_o"]):
                for m in range(MT):
                    vec.wait_ge(proj_free, s.bank0 + m + 1)
                    h_ = lstm_h[:, m, i * NCOL:(i + 1) * NCOL]
                    vec.tensor_tensor(h_, h_, gate_tmp[:, n % 2, :], ALU.mult).then_inc(lstm_gated, 1)
                    n += 1
            head_scales(2)
            n = 0
            for i, s in enumerate(by_name["lstm_z"]):
                for m in range(MT):
                    vec.wait_ge(proj_free, s.bank0 + m + 1)
                    for hh in range(2):
                        h = 2 * i + hh
                        h_ = lstm_h[:, m, h * LSTM_HD:(h + 1) * LSTM_HD]
                        ins = vec.scalar_tensor_tensor(h_, h_, rstd[:, m * 4 + h:m * 4 + h + 1],
                                                       gate_tmp[:, n % 2, hh * LSTM_HD:(hh + 1) * LSTM_HD], ALU.mult, ALU.mult)
                    ins.then_inc(ya_ready, 1)
                    n += 1

            def queries(half):
                s = by_name["sb_q"][half]
                for h in range(4):
                    vec.tensor_scalar(sb_q[half][:, h, :], bank(s, h), HD ** -0.5, None, ALU.mult).then_inc(proj_free, 1)

            def keys(half):
                s = by_name["sb_k"][half]
                for h in range(4):
                    vec.tensor_copy(sb_k[half][:, h, :], bank(s, h)).then_inc(proj_free, 1)

            def terms(u):
                nk = (u % MT + 1) * P
                z, l_ = work[:, u % 2, 0:nk], sb_l[:, u % 2, 0:nk]
                own = slice(nk - P, nk)
                vec.wait_ge(sb_l1, u + 1)
                step(vec.scalar_tensor_tensor(l_, z, 0.0, l_, ALU.max, ALU.add))
                step(vec.tensor_tensor(l_[:, own], l_[:, own], before_ok[:], ALU.mult))
                ones = one_col[:, 0:1].to_broadcast([P, nk])
                step(vec.tensor_tensor_scan(l_[:, ::-1], ones, l_[:, ::-1], 0.0, ALU.mult, ALU.add))
                step(vec.tensor_tensor(l_, z, l_, ALU.subtract))
                vec.tensor_tensor(l_[:, own], l_[:, own], before_neg[:], ALU.add).then_inc(sb_t, 1)

            def output(u):
                h, blk = u // MT, u % MT
                vec.wait_ge(sb_o_full, u + 1)
                vec.tensor_copy(sb_o[:, blk, h * HD:(h + 1) * HD], work[:, 3, 0:HD]).then_inc(sb_o_copied, 1)

            def gated(i):
                vec.wait_ge(sb_o_copied, SB_UNITS // 2 * (i + 1))
                for m in range(MT):
                    vec.wait_ge(proj_free, by_name["sb_z"][i].bank0 + m + 1)
                    o_ = sb_o[:, m, i * NCOL:(i + 1) * NCOL]
                    vec.tensor_tensor(o_, o_, sb_gate[:, m, :], ALU.mult).then_inc(yb_ready, 1)

            def first_half_out(name, i):
                s = by_name[name][i]
                for m in range(MT):
                    vec.tensor_copy(y[:, m, i * NCOL:(i + 1) * NCOL], bank(s, m)).then_inc(proj_free, 1)

            queries(0)
            fill_lo("aux", AUX_AT["ya"], KD, turn=True, gain=HN)
            keys(0)
            for i in range(SB_STEPS + 1):
                if i >= 3:
                    output(i - 3)
                if i < SB_UNITS:
                    terms(i)
                for s, j in beside[i]:
                    if j < s.n - 1:
                        continue
                    if s is by_name["sb_q"][1]:
                        queries(1)
                    elif s is by_name["sb_k"][1]:
                        keys(1)
                    elif s is by_name["sb_z"][0]:
                        gated(0)
                    elif s is by_name["even_out0"][0]:
                        first_half_out("even_out0", 0)
            gated(1)
            first_half_out("even_out0", 1)

            def layer_out(name, first, second):
                if name == "post0":
                    fill_lo("act", ACT_AT["yb"], KD, turn=True)
                else:
                    first_half_out("odd_out0", 0)
                    pool_mixed(3)
                    fill_lo("aux", AUX_AT["mixb"], KD, src=odd_z[:, KD:2 * KD, :])
                    first_half_out("odd_out0", 1)
                vec.wait_ge(proj_free, end(first))
                vec.wait_ge(post_loaded, 32)
                for i, s in enumerate(by_name[second]):
                    part = slice(i * NCOL, (i + 1) * NCOL)
                    for m in range(MT):
                        vec.tensor_tensor(y[:, m, part], y[:, m, part], bank(s, m), ALU.add).then_inc(proj_free, 1)
                        vec.wait_ge(proj_free, s.bank0 + m + 1)
                        ins = vec.tensor_tensor(y_gain[:, m, part], y[:, m, part],
                                                post_row[0 if name == "post0" else 1][:, part], ALU.mult)
                        if i == 0:
                            continue
                        step(ins)
                        token_scale(name, tile(m))
                        for half, done in ((0, x_half), (1, x_final)):
                            h_ = slice(half * NCOL, (half + 1) * NCOL)
                            vec.scalar_tensor_tensor(x[:, m, h_], y_gain[:, m, h_], rstd[:, m:m + 1], x[:, m, h_], ALU.mult, ALU.add)\
                               .then_inc(done, 1)
                        if name == "post0":
                            vec.wait_ge(sums2_ready, m + 1)
                            c = 2 * MT + m
                            vec.tensor_tensor(stat[:, c:c + 1], stat[:, c:c + 1], stat[:, c + MT:c + MT + 1], ALU.add)\
                               .then_inc(sums2_added, 1)
                            second_scale("pre1", tile(m))
                            diagonal(rstd[:, MT + m:MT + m + 1], m)

            layer_out("post0", "even_out0", "even_out1")
            for m in range(MT):
                scale_rest(scaled_x1, x, rstd[:, MT + m:MT + m + 1], m)
            fill_lo("act", ACT_AT["pre1"], KD, turn=True, gain=PRE + 8)

            step(vec.memset(pool_raw[:, :, 0:POOL_PAD], 0.0))
            step(vec.memset(pool_sum[:, :, 0:POOL_PAD], 0.0))
            n = 0

            def pool_lo_of(n):
                vec.wait_ge(aux_hi_ready, AUX_AT["pool"] + n + 1)
                hi, lo = aux(n % 8)
                vec.tensor_tensor(lo, pooled[:, n % 4, :], hi.bitcast(F32), ALU.subtract).then_inc(aux_ready, 1)

            def pool_mixed(g):
                s = by_name["pool_mix"][g]
                for c in range(4):
                    t = odd_z[:, 4 * g + c, :]
                    vec.scalar_tensor_tensor(t, bank(s, c), cols[:, PS + 4 * g + c:PS + 4 * g + c + 1], t,
                                             ALU.mult, ALU.mult).then_inc(proj_free, 1)

            for g, s in enumerate(by_name["pool_in"]):
                w = POOL_WINDOWS[g]
                if g == 3:
                    fill_lo("act", ACT_AT["mixa"], KD, src=odd_z)
                for c in range(4):
                    if g and c == (1 if g == 3 else 2):
                        pool_mixed(g - 1)
                    vec.wait_ge(proj_free, s.bank0 + c + 1)
                    raw = src = pool_raw[:, n % 4, :]
                    back, level = 1, 0
                    while back < w:
                        dst = pool_sum[:, level % 2, :]
                        step(vec.tensor_tensor(dst[:, POOL_PAD:], src[:, POOL_PAD:], src[:, POOL_PAD - back:PADDED - back], ALU.add))
                        src, back, level = dst, 2 * back, level + 1
                    first = src[:, POOL_PAD:2 * POOL_PAD]
                    step(vec.tensor_tensor(first, first, edges[:, g, :], ALU.mult))
                    vec.scalar_tensor_tensor(pooled[:, n % 4, :], src[:, POOL_PAD:], 1.0 / w, raw[:, POOL_PAD:],
                                             ALU.mult, ALU.subtract).then_inc(pool_done, 1)
                    vec.wait_ge(pool_done, n + 1)
                    if c:
                        pool_lo_of(n - 1)
                    n += 1
                pool_lo_of(n - 1)
            layer_out("post1", "odd_out0", "odd_out1")

        @block.tensor
        def _(pe):
            def three(out_, a_hi, a_lo, b_hi, b_lo, first, last):
                pe.matmul(out_, a_hi, b_hi, start=first, stop=False)
                pe.matmul(out_, a_hi, b_lo, start=False, stop=False)
                return pe.matmul(out_, a_lo, b_hi, start=False, stop=last)

            def natural(m):
                return slice(m * P, (m + 1) * P)

            def by_stride(z):
                return slice(z, SEQ, 4)

            def slab_block(s, j, kind, pair, k, tokens, wait_bank):
                slot = (s.first + j) % RING
                hi, lo = tile_of(pair)(k)
                wh, wl = w_hi[:, slot, :], w_lo[:, slot, :]
                for c in range(4):
                    if j == 0:
                        wait_bank(c)
                    f = slice(c * P, (c + 1) * P)
                    t = tokens(c)
                    a, b = ((hi[:, t], lo[:, t]), (wh, wl)) if kind == "tokens" else ((wh[:, f], wl[:, f]), (hi, lo))
                    ins = three(proj[:, c, :], *a, *b, j == 0, j == s.n - 1)
                    if j == s.n - 1:
                        ins.then_inc(proj_full, 1)
                ins if j == s.n - 1 else ins.then_inc(block_used, 1)

            def slab(s, kind, pair="act", ready=None, tokens=natural, k0=0, before=None):
                for j in range(s.n):
                    if before:
                        before(j)
                    pe.wait_ge(lo_ready, s.first + j + 1)
                    if ready:
                        pe.wait_ge(ready[0], ready[1] + k0 + j + 1)

                    def wait_bank(c):
                        if s.need[c]:
                            pe.wait_ge(proj_free, s.need[c])

                    slab_block(s, j, kind, pair, k0 + j, tokens, wait_bank)

            def slab_by_bank(s, pair, ready=None):
                for c in range(s.banks):
                    if s.need[c]:
                        pe.wait_ge(proj_free, s.need[c])
                    for j in range(s.n):
                        if c == 0:
                            pe.wait_ge(lo_ready, s.first + j + 1)
                            if ready:
                                pe.wait_ge(ready[0], ready[1] + j + 1)
                        slot = (s.first + j) % RING
                        hi, lo = tile_of(pair)(j)
                        t = natural(c)
                        ins = three(proj[:, c, :], hi[:, t], lo[:, t], w_hi[:, slot, :], w_lo[:, slot, :], j == 0, j == s.n - 1)
                        if j == s.n - 1:
                            ins.then_inc(proj_full, 1)
                        elif c == s.banks - 1:
                            ins.then_inc(block_used, 1)

            def slabs_of(name, kind, pair="act", ready=None, skip=0):
                ss = by_name[name][skip:]
                s0 = ss[0]
                assert s0.n == RING
                if slabs[s0.at - 1].banks % 4:
                    pe.wait_ge(proj_free, s0.bank0)
                if ready:
                    pe.wait_ge(ready[0], ready[1] + KD)
                with pe.Fori(0, len(ss)) as i:
                    for j in range(s0.n):
                        pe.wait_ge(lo_ready, i * s0.n + (s0.first + j + 1))
                        slab_block(s0, j, kind, pair, j, natural,
                                   lambda c: pe.wait_ge(proj_free, i * 4 + (s0.bank0 + c - 3)))

            def narrow_slab(s, phys, ready=None, before=None):
                for j in range(s.n):
                    pe.wait_ge(lo_ready, s.first + j + 1)
                    if j == 0 and s.need[0]:
                        pe.wait_ge(proj_free, s.need[0])
                    slot = (s.first + j) % RING
                    for kk in range(4):
                        k = 4 * j + kk
                        if before:
                            before(k)
                        if ready:
                            pe.wait_ge(ready[0], ready[1] + k + 1)
                        f = slice(kk * P, (kk + 1) * P)
                        ins = three(proj[:, phys, :], w_hi[:, slot, f], w_lo[:, slot, f], act_hi[:, k, :], act_lo[:, k, :],
                                    k == 0, k == KD - 1)
                    ins.then_inc(proj_full if j == s.n - 1 else block_used, 1)

            def turn_tile(src, k, ready_sem, base, k_src=None, by_root=False, tiles=range(MT)):
                if k >= 4:
                    pe.wait_ge(ready_sem, base + k - 3)
                at_ = (k if k_src is None else k_src) * P
                for m in tiles:
                    o_, i_ = work[:, k % 4, m * P:(m + 1) * P], src[:, m, at_:at_ + P]
                    ins = pe.matmul(o_, i_, root_diag[:, m, :], start=True, stop=True) if by_root else \
                        pe.transpose(o_, i_, ident[:])
                if MT - 1 in tiles:
                    ins.then_inc(turned, 1)

            def ahead_of(tile):
                def before(k):
                    for t in range(0 if k == 0 else k + 2, min(k + 3, KD)):
                        tile(t)
                return before

            def turn(src, ready_sem, base):
                return ahead_of(lambda k: turn_tile(src, k, ready_sem, base))

            def turn_norm(name, src=x, rest=scaled_x, by_tile=False, after_first=None):
                early = range(MT - 1) if by_tile else range(0)
                if early:
                    pe.wait_ge(scaled, MT * NORM[name] + MT - 1)
                    for k in range(DIAG_TILES):
                        turn_tile(src, k, act_ready, ACT_AT[name], by_root=True, tiles=early)
                pe.wait_ge(scaled, MT * (NORM[name] + 1))

                def tile(k):
                    if k == DIAG_TILES:
                        pe.wait_ge(x_scaled, MT * (NORM[name] + 1))
                    if k < DIAG_TILES:
                        turn_tile(src, k, act_ready, ACT_AT[name], by_root=True, tiles=range(len(early), MT))
                        if k == 0 and after_first:
                            after_first()
                    else:
                        turn_tile(rest, k, act_ready, ACT_AT[name], k_src=k - DIAG_TILES)

                return ahead_of(tile)

            def ready_act(name):
                return act_ready, ACT_AT[name]

            pe.wait_ge(consts_ready, 1)
            def params_turned():
                pe.wait_ge(params_loaded, 16 * 15)
                pe.transpose(work[:, 3, 0:CONV_AT], rows1[0:CONV_AT, :], ident[0:CONV_AT, 0:CONV_AT])
                pe.transpose(work[:, 3, P:P + 64], rows2[0:64, :], ident[0:64, 0:64]).then_inc(cols_full, 1)

            turn_ln1 = turn_norm("ln1", after_first=params_turned)
            turn_ln1(0)

            def before_a(k):
                if k == 0:
                    return
                if k == 1:
                    pe.wait_ge(cols_ready, 1)
                turn_ln1(k)

            narrow_slab(by_name["gla_a"][0], 0, ready=ready_act("ln1"), before=before_a)
            pe.wait_ge(proj_free, 1)
            for h in range(GLA_HEADS):
                pe.matmul(work[:, h, :], w_a2[0:GLA_RANK, h * P:(h + 1) * P], gla_a[0:GLA_RANK, :], start=True, stop=True)\
                  .then_inc(gate_full, 1)
            slab(by_name["gla_q"][0], "features")
            pe.wait_ge(gate_done, 1)
            pe.wait_ge(rel_ready, 1)
            for g in range(3):
                pe.matmul(work[0:ATT_HEADS, 1 + g, 0:DIAG[g]], rel_rows[0:REL_BUCKETS + 1, 4 * g:4 * g + 4],
                          one_hot[0:REL_BUCKETS + 1, DIAG_AT[g]:DIAG_AT[g] + DIAG[g]], start=True, stop=True)\
                  .then_inc(diag_full, 1)
            slab(by_name["gla_k"][0], "features")
            slabs_of("gla_v", "tokens")
            pe.wait_ge(diag_copied, 3)
            for h in range(GLA_HEADS):
                pe.wait_ge(proj_free, by_name["gla_k"][0].bank0 + h + 1)
                for m in range(MT):
                    ins = pe.transpose(work[:, h, m * P:(m + 1) * P], k_out[:, h, m * P:(m + 1) * P], ident[:])
                ins.then_inc(ktok_full, 1)
            for h in range(GLA_HEADS):
                pe.wait_ge(ktok_ready, h + 1)
                for m in range(MT):
                    t = natural(m)
                    ins = pe.matmul(work[:, h, t], k_in[:, h, t], q_dec[:, h, t], start=True, stop=True)
                ins.then_inc(gla_att_full, 1)
            pe.wait_ge(proj_free, end("gla_v"))
            pe.wait_ge(gla_att_ready, GLA_HEADS)
            for m in range(MT):
                for half in range(2):
                    n = 2 * m + half
                    rows = slice(half * CHUNK, (half + 1) * CHUNK)
                    if n < NCH - 1:
                        for h in range(GLA_HEADS):
                            if n and h % 2 == 0:
                                pe.wait_ge(gla_state_ready, 4 * (n - 1) + h + 2)
                            ins = pe.matmul(work[:, 2 + h // 2, (h % 2) * GLA_DV:(h % 2 + 1) * GLA_DV],
                                            k_tok[rows, h, natural(m)], gla_v[rows, m, h * GLA_DV:(h + 1) * GLA_DV],
                                            start=True, stop=True)
                            if h % 2:
                                ins.then_inc(gla_upd_full, 1)
                    if half == 0:
                        for h in range(GLA_HEADS):
                            if m and h % 2 == 0:
                                pe.wait_ge(gla_o_copied, 2 * (m - 1) + h // 2 + 1)
                            pe.matmul(work[:, h // 2, (h % 2) * GLA_DV:(h % 2 + 1) * GLA_DV], gla_att[:, h, natural(m)],
                                      gla_v[:, m, h * GLA_DV:(h + 1) * GLA_DV], start=(h % 2 == 0), stop=False, skip_group_check=True)
                    for s, j in gla_beside[n]:
                        pe.wait_ge(lo_ready, s.first + j + 1)
                        slab_block(s, j, "tokens", "act", j, natural, lambda c: pe.wait_ge(proj_free, s.need[c]))
                    for h in range(GLA_HEADS):
                        if n:
                            pe.wait_ge(gla_state_ready, 4 * (n - 1) + h + 1)
                            ins = pe.matmul(work[rows, h // 2, (h % 2) * GLA_DV:(h % 2 + 1) * GLA_DV],
                                            q_dec[:, h, n * CHUNK:(n + 1) * CHUNK], gla_state[:, n % 2, h, :],
                                            start=False, stop=(half == 1), skip_group_check=True)
                            if half and h % 2:
                                ins.then_inc(gla_o_full, 1)
            for g in range(3):
                slab(by_name[f"att_q{g}"][0], "features")
                sk = by_name[f"att_k{g}"][0]
                slab(sk, "features")
                if g:
                    pe.wait_ge(biased, 4 * g)
                else:
                    pe.wait_ge(gla_o_copied, 2 * MT)
                    pe.wait_ge(gla_state_ready, 4 * (NCH - 1))
                for h in range(ATT_HEADS):
                    pe.wait_ge(proj_free, sk.bank0 + h + 1)
                    if g == 0 and h >= 2:
                        pe.wait_ge(biased, h - 1)
                    for z in range(4):
                        q_ = att_q[:, h, natural(z)]
                        if g == 0:
                            k0 = max(z - 1, 0) * P
                            n_ = P if z == 0 else 2 * P
                            o_ = work[:, 2 * (h % 2) + z // 2, (z % 2) * 2 * P:(z % 2) * 2 * P + n_]
                            ins = pe.matmul(o_, q_, att_k[:, h, k0:k0 + n_], start=True, stop=True)
                        else:
                            ins = pe.matmul(work[:, h, natural(z)], q_, att_k[:, h, natural(z)], start=True, stop=True)
                    ins.then_inc(logits_full, 1)
            slab(by_name["att_v0"][0], "tokens")
            pe.wait_ge(lse_ready, 1)
            pe.wait_ge(biased, 12)
            for g in range(3):
                for z in range(4):
                    c = (g * 4 + z) * 4
                    ins = pe.transpose(work[0:4, g, natural(z)], att_tmp[:, c:c + 4], ident[:])
                ins.then_inc(lse_full, 1)
            slab(by_name["att_v1"][0], "tokens", tokens=by_stride)
            pe.wait_ge(share_ready, 1)
            for g in range(3):
                for z in range(4):
                    c = (g * 4 + z) * 4
                    t = natural(z) if g == 0 else by_stride(z)
                    ins = pe.transpose(work[:, 3, c:c + 4], lse_rows[0:4, g, t], ident[0:4, 0:4])
            ins.then_inc(share_full, 1)
            slab(by_name["att_v2"][0], "tokens", tokens=by_stride)
            pairs = [(z, kb) for z in range(4) for kb in ((z - 1, z) if z else (0,))]

            def probs_turned(u):
                h, g = u // 3, u % 3
                pe.wait_ge(p_scaled, u + 1)
                if g == 0:
                    if h:
                        pe.wait_ge(pt_copied[2], h)
                    for at, (z, kb) in enumerate(pairs):
                        k0 = z * KEYS[0] + (0 if kb < z else P)
                        ins = pe.transpose(work[:, at // 4, (at % 4) * P:(at % 4 + 1) * P], att_p[0][:, h, k0:k0 + P], ident[:])
                else:
                    if g == 2:
                        pe.wait_ge(pt_copied[0], 2 * h + 2)
                    elif h:
                        pe.wait_ge(pt_copied[1], h)
                    for z in range(4):
                        ins = pe.transpose(work[:, 2 if g == 1 else 0, natural(z)], att_p[g][:, h, natural(z)], ident[:])
                ins.then_inc(pt_full, 1)

            def values_weighted(u):
                h, g = u // 3, u % 3
                if g == 0 and h:
                    pe.wait_ge(att_o_copied, h)
                pe.wait_ge(pt_copied[g], 2 * h + 2 if g == 0 else h + 1)
                todo = [(at, kb, natural(z)) for at, (z, kb) in enumerate(pairs)] if g == 0 else \
                       [(z, z, by_stride(z)) for z in range(4)]
                for n, (at, kb, t) in enumerate(todo):
                    ins = pe.matmul(work[:, 3, t], att_v[g][:, kb, h * HD:(h + 1) * HD], att_pt[g][:, at * P:(at + 1) * P],
                                    start=(g == 0 and n == 0), stop=(g == 2 and n == 3), skip_group_check=True)
                ins.then_inc(pv_done, 1)

            pe.wait_ge(proj_free, end("att_v2"))
            probs_turned(0)
            for u in range(12):
                if u + 1 < 12:
                    probs_turned(u + 1)
                for s, j in probs_beside[u]:
                    pe.wait_ge(lo_ready, s.first + j + 1)
                    slab_block(s, j, "features", "act", j, natural, lambda c: pe.wait_ge(proj_free, s.need[c]))
                values_weighted(u)
            slabs_of("mix_gate", "features", skip=1)
            pe.wait_ge(gla_gated, 2 * MT)
            pe.wait_ge(att_o_copied, ATT_HEADS)
            def two_tiles(k):
                for t in (2 * k, 2 * k + 1):
                    turn_tile(gla_o, t, act_ready, ACT_AT["gla"])

            slab(by_name["att_out"][0], "features", pair="aux0", ready=(aux_ready, AUX_AT["att"]), before=two_tiles)
            slabs_of("gla_out", "features", ready=ready_act("gla"))
            slab(by_name["att_out"][1], "features", pair="aux0")
            s = by_name["mix_out"][0]
            slab(s, "tokens", ready=ready_act("mix"))
            slab(by_name["mix_out"][1], "tokens")

            ups, downs = by_name["mlp_up"], by_name["mlp_down"]

            def down_pair(g):
                for i in range(2):
                    slab(downs[2 * g + i], "tokens", pair=f"aux{g % 2}", ready=(aux_ready, AUX_AT["mlp"] + 4 * g))

            slab(ups[0], "features", ready=ready_act("ln2"), before=turn_norm("ln2"))
            slab(ups[1], "features")
            down_pair(0)
            with pe.Fori(0, LOOP_TURNS) as i:
                for at, s in enumerate(LOOP_SLABS):
                    t = at // 3
                    for j in range(s.n):
                        pe.wait_ge(lo_ready, i * LOOP_BLOCKS + (s.first + j + 1))
                        if at % 3:
                            pe.wait_ge(aux_ready, i * 8 + (AUX_AT["mlp"] + 4 * (1 + t) + j + 1))
                        slab_block(s, j, "tokens" if at % 3 else "features", f"aux{(1 + t) % 2}" if at % 3 else "act", j,
                                   natural, lambda c: pe.wait_ge(proj_free, i * LOOP_BANKS + s.need[c]))
            pe.wait_ge(ple_loaded, 32)
            for k in range(PLE // P):
                turn_tile(ple_in, k, aux_ready, AUX_AT["p"])
            down_pair(D_FF // NCOL - 1)

            for s in by_name["ple_p"]:
                slab(s, "tokens", pair="aux0", ready=(aux_ready, AUX_AT["p"]))
            pe.wait_ge(aux_ready, AUX_AT["p"] + 2)
            slab(by_name["ple_gate"][0], "tokens", ready=ready_act("ln3"), before=turn_norm("ln3"))
            slab_by_bank(by_name["ple_gate"][1], "act")

            narrow_slab(by_name["lstm_if"][0], 0, ready=ready_act("pre0"), before=turn_norm("pre0", ple_pp))
            H = LSTM_HEADS
            for s in by_name["lstm_q"]:
                slab(s, "features")
            pe.wait_ge(lstm_exps, 4)
            pe.wait_ge(act_ready, ACT_AT["pre0"] + KD)
            for at, r in enumerate(("a", "wa", "emt")):
                for m in range(MT):
                    ins = pe.transpose(work[:, 0, 16 * at + 4 * m:16 * at + 4 * m + 4], row[r][:, natural(m)], ident[0:H, 0:H])
            ins.then_inc(lstm_cols_full, 1)
            for h in range(H):
                ins = pe.matmul(work[:, 1, h * MT:(h + 1) * MT], sel[:, h, :], lstm_dec[:], start=True, stop=True)
            ins.then_inc(lstm_cols_full, 1)
            slabs_of("lstm_k", "features")
            def blocks_beside(todo, kind):
                for s, j in todo:
                    pe.wait_ge(lo_ready, s.first + j + 1)
                    slab_block(s, j, kind, "act", j, natural, lambda c: pe.wait_ge(proj_free, s.need[c]))

            blocks_beside(heads_beside[0], "tokens")
            pe.wait_ge(lstm_cols_ready, 2)
            for h in range(H):
                pe.wait_ge(conv_silu, 8 + 2 * h + 2)
                if h:
                    pe.wait_ge(s_ready, h)
                for m in range(MT):
                    for kk in range(2):
                        ins = pe.matmul(work[:, 0, natural(m)], lstm_k[:, 2 * h + kk, natural(m)], lstm_q[:, 2 * h + kk, natural(m)],
                                        start=(kk == 0), stop=(kk == 1))
                ins.then_inc(qk_full, 1)
                if h:
                    pe.wait_ge(w_masked, h)
                pe.matmul(work[:, 1, :], sel[:, h, :], row["neg_e"], start=True, stop=True).then_inc(neg_e_full, 1)
                if h:
                    pe.wait_ge(q_inter, h)
                pe.matmul(work[:, 2, :], sel[:, h, :], row["inter"], start=True, stop=True).then_inc(inter_full, 1)
                for pair in range(2):
                    if h or pair:
                        pe.wait_ge(lstm_kt_ready, 2 * h + pair)
                    for mm in range(2):
                        for kk in range(2):
                            at = mm * LSTM_HD + kk * P
                            ins = pe.transpose(work[:, 3, at:at + P], lstm_k[:, 2 * h + kk, natural(2 * pair + mm)], ident[:])
                    ins.then_inc(lstm_kt_full, 1)
                    todo = heads_beside[h + 1]
                    blocks_beside(todo[:2] if pair == 0 else todo[2:], "tokens")
            core = by_name["lstm_core"][0]
            va = lstm_v.rearrange("p m (h c) -> p m h c", h=H)
            pe.wait_ge(proj_free, end("lstm_v"))
            pe.wait_ge(s_ready, H)
            pe.wait_ge(lstm_kt_ready, 2 * H)
            for m in range(MT):
                for h in range(H):
                    if m:
                        pe.wait_ge(proj_free, core.need[4 * m + h])
                    ins = pe.matmul(proj[:, h, 0:LSTM_HD + 1], lstm_s[:, h, natural(m)], va[:, m, h, :], start=True, stop=(m == 0),
                                    skip_group_check=True)
                    if m == 0:
                        ins.then_inc(proj_full, 1)
                for h in range(H):
                    if m:
                        pe.wait_ge(lstm_c_ready, 8 * (m - 1) + 2 * h + 2)
                        for kk in range(2):
                            ins = pe.matmul(proj[:, h, 0:LSTM_HD + 1], lstm_q[:, 2 * h + kk, natural(m)], lstm_c[:, 2 * h + kk, :],
                                            start=False, stop=(kk == 1), skip_group_check=True)
                        ins.then_inc(proj_full, 1)
                    if m < MT - 1:
                        for kk in range(2):
                            hk = 2 * h + kk
                            if 8 * m + hk >= 4:
                                pe.wait_ge(lstm_c_ready, 8 * m + hk - 3)
                            pe.matmul(work[:, hk % 4, 0:LSTM_HD + 1], k_wa[:, m, h * LSTM_HD + kk * P:h * LSTM_HD + (kk + 1) * P],
                                      va[:, m, h, :], start=True, stop=True).then_inc(lstm_upd_full, 1)
            slabs_of("lstm_o", "tokens")
            slabs_of("lstm_z", "tokens")
            slab(by_name["sb_q"][0], "features")
            pe.wait_ge(ya_ready, 2 * MT)
            pe.wait_ge(lstm_c_ready, 8 * (MT - 1))
            slab(by_name["sb_k"][0], "features", before=turn(lstm_h, aux_ready, AUX_AT["ya"]))
            slab(by_name["sb_v"][0], "tokens")
            pe.wait_ge(aux_ready, AUX_AT["ya"] + KD)

            def scores(u):
                half, h, nk = u // 16, u % 16 // MT, (u % MT + 1) * P
                if u % 16 == 0:
                    pe.wait_ge(proj_free, by_name["sb_k"][half].end)
                if u >= 2:
                    pe.wait_ge(sb_t, u - 1)
                pe.matmul(work[:, u % 2, 0:nk], sb_q[half][:, h, natural(u % MT)], sb_k[half][:, h, 0:nk],
                          start=True, stop=True).then_inc(sb_z_full, 1)

            def weights_turned(u):
                pe.wait_ge(sb_a, u + 1)
                if u:
                    pe.wait_ge(sb_at_ready, u)
                for kb in range(u % MT + 1):
                    ins = pe.transpose(work[:, 2, natural(kb)], sb_l[:, u % 2, natural(kb)], ident[:])
                ins.then_inc(sb_at_full, 1)

            def values(u):
                half, h, n_ = u // 16, u % 16 // MT, u % MT + 1
                if u % 16 == 0:
                    pe.wait_ge(proj_free, by_name["sb_v"][half].end)
                pe.wait_ge(sb_at_ready, u + 1)
                if u:
                    pe.wait_ge(sb_o_copied, u)
                for kb in range(n_):
                    ins = pe.matmul(work[:, 3, 0:HD], sb_at[:, u % 2, natural(kb)], sb_v[half][:, kb, h * HD:(h + 1) * HD],
                                    start=(kb == 0), stop=(kb == n_ - 1))
                ins.then_inc(sb_o_full, 1)

            for i in range(SB_STEPS + 1):
                if i < SB_UNITS:
                    scores(i)
                for s, j in beside[i]:
                    pe.wait_ge(lo_ready, s.first + j + 1)
                    slab_block(s, j, "features" if s.name in ("sb_q", "sb_k") else "tokens",
                               "aux" if s.name == "even_out0" else "act", j, natural,
                               lambda c: pe.wait_ge(proj_free, s.need[c]))
                if 1 <= i <= SB_UNITS:
                    weights_turned(i - 1)
                if 2 <= i < SB_STEPS:
                    values(i - 2)
            pe.wait_ge(yb_ready, 2 * MT)
            slab(by_name["even_out1"][0], "tokens", ready=ready_act("yb"), before=turn(sb_o, act_ready, ACT_AT["yb"]))
            slab_by_bank(by_name["even_out1"][1], "act")

            slab(by_name["odd_z"][0], "features", ready=ready_act("pre1"), before=turn_norm("pre1", rest=scaled_x1, by_tile=True))
            slabs_of("odd_z", "features", skip=1)
            ins_, mixes = by_name["pool_in"], by_name["pool_mix"]
            def mix_group(g):
                slab(mixes[g], "features", pair=f"aux{g % 2}", ready=(aux_ready, AUX_AT["pool"] + 4 * g))

            slab(ins_[0], "features")
            for g in range(1, len(POOL_WINDOWS)):
                slab(ins_[g], "features")
                mix_group(g - 1)
            slab(by_name["odd_out0"][0], "tokens", ready=ready_act("mixa"))
            mix_group(len(POOL_WINDOWS) - 1)
            slab(by_name["odd_out0"][1], "tokens")
            slab(by_name["odd_out1"][0], "tokens", pair="aux", ready=(aux_ready, AUX_AT["mixb"]))
            slab_by_bank(by_name["odd_out1"][1], "aux")


_INS = ["x", "p", "ln1", "w_in", "w_a2", "b_a", "gla_gn", "w_o_gla", "w_o_attn", "w_out", "ln2", "w_mlp1", "w_mlp2",
        "ln3", "w_pp", "w_pg", "rel_bias", "ln_f", "pre_norm_g_2", "post_norm_g_2", "w_in_ab_2", "conv_qk_2",
        "bias_i_2", "bias_f_2", "head_norm_g_2", "w_out_ab_2", "w_in_c_2", "pool_w_2", "pool_scale_2", "w_out_c_2"]
_FLAT = {"w_in": (D, -1), "w_a2": (GLA_RANK, -1), "w_o_gla": (D, D), "w_o_attn": (-1, D), "w_out": (D, D),
         "w_mlp1": (D, D_FF), "w_mlp2": (D_FF, D), "w_pp": (PLE, D), "w_pg": (D, D), "w_in_ab_2": (D, -1),
         "w_out_ab_2": (2 * D, D), "w_in_c_2": (D, 2 * C_WIDTH), "pool_w_2": (C_WIDTH, -1), "w_out_c_2": (C_WIDTH, D),
         "conv_qk_2": (CONV, 2 * D)}


def kernel(**inputs):
    import concourse.bacc as bacc
    from concourse.bass_utils import run_bass_kernel_spmd

    nc = bacc.Bacc("TRN2", target_bir_lowering=False, num_devices=1)
    arrays, aps = {}, {}

    def give(name, a):
        arrays[f"in_{name}"] = a
        aps[name] = nc.dram_tensor(f"in_{name}", a.shape, mybir.dt.from_np(a.dtype), kind="ExternalInput").ap()

    for name in _INS:
        a = np.ascontiguousarray(inputs[name])
        give(name, a.reshape(_FLAT[name]) if name in _FLAT else a)
    give("bucket_one_hot", bucket_one_hot())
    give("pool_edges", pool_edges())
    out = nc.dram_tensor("out", (1, SEQ, D), F32, kind="ExternalOutput").ap()
    two_blocks(nc, aps, out)
    r = run_bass_kernel_spmd(nc, [arrays], core_ids=[0])
    return r.results[0]["out"]
```
